# Optimizing a Trainium2 kernel written in Bass

```python
import math
import jax, jax.numpy as jnp
from jax import lax
import numpy as np

D_MODEL = 1024
BATCH = 1
SEQ = 512
DEPTH = 2

N_MIXERS = 2
N_GDN_LAYERS = (DEPTH + N_MIXERS - 1) // N_MIXERS
N_MLA_LAYERS = DEPTH // N_MIXERS

GDN_HEADS = 8
GDN_HEAD_DIM = 128
GDN_KEY_DIM = GDN_HEADS * GDN_HEAD_DIM
GDN_VALUE_DIM = GDN_HEADS * GDN_HEAD_DIM
GDN_CONV = 4
GDN_CHUNK = 64
GDN_IN = 2 * GDN_KEY_DIM + 2 * GDN_VALUE_DIM + 2 * GDN_HEADS

MLA_HEADS = 8
MLA_NOPE = 128
MLA_ROPE = 64
MLA_V = 128
MLA_Q_RANK = 384
MLA_KV_RANK = 256
MLA_IN = MLA_Q_RANK + MLA_KV_RANK + MLA_ROPE
ROPE_THETA = 10000.0
Q_BLOCK = 128

D_FF = ((8 * D_MODEL + 3 * 256 - 1) // (3 * 256)) * 256
N_MOD = 6
EPS = 1e-6


def rmsnorm(x, g):
    xf = x.astype(jnp.float32)
    y = xf * lax.rsqrt(jnp.mean(xf * xf, axis=-1, keepdims=True) + EPS)
    return (y * g.astype(jnp.float32)).astype(x.dtype)

def l2norm(x):
    return x * lax.rsqrt(jnp.sum(x * x, axis=-1, keepdims=True) + EPS)

def causal_depthwise_conv(x, w):
    K = w.shape[-1]
    kern = jnp.transpose(w)[:, None, :].astype(x.dtype)
    return lax.conv_general_dilated(
        x, kern, window_strides=(1,), padding=[(K - 1, 0)],
        dimension_numbers=("NWC", "WIO", "NWC"), feature_group_count=x.shape[-1])

def chunk_gated_delta_rule(q, k, v, g, beta):
    B, H, T, Dk = q.shape
    Dv = v.shape[-1]
    C = GDN_CHUNK
    N = T // C
    q = q.reshape(B, H, N, C, Dk)
    k = k.reshape(B, H, N, C, Dk)
    v = v.reshape(B, H, N, C, Dv)
    g_cum = jnp.cumsum(g.reshape(B, H, N, C), axis=-1)
    beta = beta.reshape(B, H, N, C)

    tril = jnp.tril(jnp.ones((C, C), dtype=bool))
    strict = jnp.tril(jnp.ones((C, C), dtype=bool), k=-1)
    diff = g_cum[..., :, None] - g_cum[..., None, :]
    decay = jnp.exp(jnp.where(tril, diff, -jnp.inf))

    kb = k * beta[..., None]
    L = jnp.where(strict, jnp.einsum("bhnid,bhnjd->bhnij", kb, k) * decay, 0.0)
    A = L + jnp.eye(C, dtype=L.dtype)
    u = lax.linalg.triangular_solve(A, v * beta[..., None], left_side=True, lower=True,
                                    unit_diagonal=True)
    w = lax.linalg.triangular_solve(A, kb * jnp.exp(g_cum)[..., None], left_side=True,
                                    lower=True, unit_diagonal=True)
    attn = jnp.einsum("bhnid,bhnjd->bhnij", q, k) * decay
    q_dec = q * jnp.exp(g_cum)[..., None]
    k_dec = k * jnp.exp(g_cum[..., -1:] - g_cum)[..., None]
    g_last = jnp.exp(g_cum[..., -1])

    def step(S, xs):
        q_i, k_i, w_i, u_i, a_i, gl_i = xs
        v_new = u_i - jnp.einsum("bhck,bhkv->bhcv", w_i, S)
        o_i = jnp.einsum("bhck,bhkv->bhcv", q_i, S) + jnp.einsum("bhij,bhjv->bhiv", a_i, v_new)
        S = S * gl_i[..., None, None] + jnp.einsum("bhck,bhcv->bhkv", k_i, v_new)
        return S, o_i

    xs = tuple(jnp.moveaxis(t, 2, 0) for t in (q_dec, k_dec, w, u, attn, g_last))
    S0 = jnp.zeros((B, H, Dk, Dv), dtype=jnp.float32)
    _, o = lax.scan(step, S0, xs)
    return jnp.moveaxis(o, 0, 2).reshape(B, H, T, Dv)

def gdn_mixer(h, w_in, conv_w, a_log, dt_bias, norm_g, w_out):
    B, T, _ = h.shape
    proj = h @ w_in
    qkv = proj[..., :2 * GDN_KEY_DIM + GDN_VALUE_DIM]
    o0 = 2 * GDN_KEY_DIM + GDN_VALUE_DIM
    gate = proj[..., o0:o0 + GDN_VALUE_DIM]
    a_in = proj[..., o0 + GDN_VALUE_DIM:o0 + GDN_VALUE_DIM + GDN_HEADS]
    b_in = proj[..., o0 + GDN_VALUE_DIM + GDN_HEADS:]

    qkv = jax.nn.silu(causal_depthwise_conv(qkv, conv_w)).astype(jnp.float32)
    q = qkv[..., :GDN_KEY_DIM].reshape(B, T, GDN_HEADS, GDN_HEAD_DIM)
    k = qkv[..., GDN_KEY_DIM:2 * GDN_KEY_DIM].reshape(B, T, GDN_HEADS, GDN_HEAD_DIM)
    v = qkv[..., 2 * GDN_KEY_DIM:].reshape(B, T, GDN_HEADS, GDN_HEAD_DIM)
    q = l2norm(q) * (GDN_HEAD_DIM ** -0.5)
    k = l2norm(k)
    beta = jax.nn.sigmoid(b_in.astype(jnp.float32))
    g = -jnp.exp(a_log.astype(jnp.float32)) * jax.nn.softplus(
        a_in.astype(jnp.float32) + dt_bias.astype(jnp.float32))

    to_bhtd = lambda t: jnp.transpose(t, (0, 2, 1, 3))
    o = chunk_gated_delta_rule(to_bhtd(q), to_bhtd(k), to_bhtd(v),
                               jnp.transpose(g, (0, 2, 1)), jnp.transpose(beta, (0, 2, 1)))
    o = jnp.transpose(o, (0, 2, 1, 3)).astype(h.dtype)
    o = rmsnorm(o, norm_g) * jax.nn.silu(gate.reshape(B, T, GDN_HEADS, GDN_HEAD_DIM))
    return o.reshape(B, T, GDN_VALUE_DIM) @ w_out

def apply_rope(x, cos, sin):
    half = x.shape[-1] // 2
    x1, x2 = x[..., :half], x[..., half:]
    return jnp.concatenate([x1 * cos - x2 * sin, x2 * cos + x1 * sin], axis=-1)

def causal_mla_attention(q_nope, q_rope, k_nope, k_rope, v):
    B, T, H, _ = q_nope.shape
    nb = T // Q_BLOCK
    scale = (MLA_NOPE + MLA_ROPE) ** -0.5
    qn = jnp.moveaxis(q_nope.reshape(B, nb, Q_BLOCK, H, MLA_NOPE), 1, 0)
    qr = jnp.moveaxis(q_rope.reshape(B, nb, Q_BLOCK, H, MLA_ROPE), 1, 0)
    kpos = jnp.arange(T)

    def block(args):
        qn_b, qr_b, start = args
        s = (jnp.einsum("bqhd,bkhd->bhqk", qn_b, k_nope)
             + jnp.einsum("bqhd,bkd->bhqk", qr_b, k_rope)).astype(jnp.float32) * scale
        qpos = start + jnp.arange(Q_BLOCK)
        s = jnp.where(kpos[None, :] <= qpos[:, None], s, -jnp.inf)
        p = jax.nn.softmax(s, axis=-1).astype(v.dtype)
        return jnp.einsum("bhqk,bkhd->bqhd", p, v)

    o = lax.map(block, (qn, qr, jnp.arange(nb) * Q_BLOCK))
    return jnp.moveaxis(o, 0, 1).reshape(B, T, H, MLA_V)

def mla_mixer(h, cos, sin, w_in, q_norm_g, kv_norm_g, w_uq, w_ukv, w_out):
    B, T, _ = h.shape
    proj = h @ w_in
    c_q = proj[..., :MLA_Q_RANK]
    c_kv = proj[..., MLA_Q_RANK:MLA_Q_RANK + MLA_KV_RANK]
    k_rope = proj[..., MLA_Q_RANK + MLA_KV_RANK:]
    q = (rmsnorm(c_q, q_norm_g) @ w_uq).reshape(B, T, MLA_HEADS, MLA_NOPE + MLA_ROPE)
    kv = (rmsnorm(c_kv, kv_norm_g) @ w_ukv).reshape(B, T, MLA_HEADS, MLA_NOPE + MLA_V)
    q_nope, q_rope = q[..., :MLA_NOPE], q[..., MLA_NOPE:]
    k_nope, v = kv[..., :MLA_NOPE], kv[..., MLA_NOPE:]
    q_rope = apply_rope(q_rope, cos[:, :, None, :], sin[:, :, None, :])
    k_rope = apply_rope(k_rope, cos, sin)
    o = causal_mla_attention(q_nope, q_rope, k_nope, k_rope, v)
    return o.reshape(B, T, MLA_HEADS * MLA_V) @ w_out

def swiglu(h, w_gate, w_up, w_down):
    return (jax.nn.silu(h @ w_gate) * (h @ w_up)) @ w_down

def first_inputs(seed: int = 0) -> dict:
    key = jax.random.key(seed)
    ks = jax.random.split(key, 24)
    f32 = jnp.float32
    nrm = lambda k, shape, s: jax.random.normal(k, shape, f32) * s
    x = jax.random.normal(ks[0], (BATCH, SEQ, D_MODEL), f32)
    c = jax.random.normal(ks[1], (BATCH, D_MODEL), f32)
    positions = (jnp.arange(SEQ, dtype=jnp.int32)[None, :]
                 + jax.random.randint(ks[2], (BATCH, 1), 0, 1024, dtype=jnp.int32))
    ada_w = nrm(ks[3], (DEPTH, D_MODEL, N_MOD * D_MODEL), 0.5 * D_MODEL ** -0.5)
    ada_b = nrm(ks[4], (DEPTH, N_MOD * D_MODEL), 0.02)
    norm_mix_g = 1.0 + nrm(ks[5], (DEPTH, D_MODEL), 0.05)
    norm_ffn_g = 1.0 + nrm(ks[6], (DEPTH, D_MODEL), 0.05)

    gdn_w_in = nrm(ks[7], (N_GDN_LAYERS, D_MODEL, GDN_IN), D_MODEL ** -0.5)
    gdn_conv_w = nrm(ks[8], (N_GDN_LAYERS, 2 * GDN_KEY_DIM + GDN_VALUE_DIM, GDN_CONV),
                     GDN_CONV ** -0.5)
    gdn_a_log = jnp.log(jax.random.uniform(ks[9], (N_GDN_LAYERS, GDN_HEADS), f32, 1.0, 16.0))
    dt = jnp.exp(jax.random.uniform(ks[10], (N_GDN_LAYERS, GDN_HEADS), f32,
                                    math.log(1e-3), math.log(1e-1)))
    gdn_dt_bias = dt + jnp.log(-jnp.expm1(-dt))
    gdn_norm_g = 1.0 + nrm(ks[11], (N_GDN_LAYERS, GDN_HEAD_DIM), 0.05)
    gdn_w_out = nrm(ks[12], (N_GDN_LAYERS, GDN_VALUE_DIM, D_MODEL), GDN_VALUE_DIM ** -0.5)

    mla_w_in = nrm(ks[13], (N_MLA_LAYERS, D_MODEL, MLA_IN), D_MODEL ** -0.5)
    mla_q_norm_g = 1.0 + nrm(ks[14], (N_MLA_LAYERS, MLA_Q_RANK), 0.05)
    mla_kv_norm_g = 1.0 + nrm(ks[15], (N_MLA_LAYERS, MLA_KV_RANK), 0.05)
    mla_w_uq = nrm(ks[16], (N_MLA_LAYERS, MLA_Q_RANK, MLA_HEADS * (MLA_NOPE + MLA_ROPE)),
                   MLA_Q_RANK ** -0.5)
    mla_w_ukv = nrm(ks[17], (N_MLA_LAYERS, MLA_KV_RANK, MLA_HEADS * (MLA_NOPE + MLA_V)),
                    MLA_KV_RANK ** -0.5)
    mla_w_out = nrm(ks[18], (N_MLA_LAYERS, MLA_HEADS * MLA_V, D_MODEL),
                    (MLA_HEADS * MLA_V) ** -0.5)

    ffn_w_gate = nrm(ks[19], (DEPTH, D_MODEL, D_FF), D_MODEL ** -0.5)
    ffn_w_up = nrm(ks[20], (DEPTH, D_MODEL, D_FF), D_MODEL ** -0.5)
    ffn_w_down = nrm(ks[21], (DEPTH, D_FF, D_MODEL), D_FF ** -0.5)
    final_norm_g = 1.0 + nrm(ks[22], (D_MODEL,), 0.05)
    return {
        "x": x, "c": c, "positions": positions,
        "ada_w": ada_w, "ada_b": ada_b, "norm_mix_g": norm_mix_g, "norm_ffn_g": norm_ffn_g,
        "gdn_w_in": gdn_w_in, "gdn_conv_w": gdn_conv_w, "gdn_a_log": gdn_a_log,
        "gdn_dt_bias": gdn_dt_bias, "gdn_norm_g": gdn_norm_g, "gdn_w_out": gdn_w_out,
        "mla_w_in": mla_w_in, "mla_q_norm_g": mla_q_norm_g, "mla_kv_norm_g": mla_kv_norm_g,
        "mla_w_uq": mla_w_uq, "mla_w_ukv": mla_w_ukv, "mla_w_out": mla_w_out,
        "ffn_w_gate": ffn_w_gate, "ffn_w_up": ffn_w_up, "ffn_w_down": ffn_w_down,
        "final_norm_g": final_norm_g,
    }

def first_block(x, c, positions, ada_w, ada_b, norm_mix_g, norm_ffn_g,
              gdn_w_in, gdn_conv_w, gdn_a_log, gdn_dt_bias, gdn_norm_g, gdn_w_out,
              mla_w_in, mla_q_norm_g, mla_kv_norm_g, mla_w_uq, mla_w_ukv, mla_w_out,
              ffn_w_gate, ffn_w_up, ffn_w_down, final_norm_g):
    inv_freq = ROPE_THETA ** (-jnp.arange(0, MLA_ROPE, 2, dtype=jnp.float32) / MLA_ROPE)
    ang = positions.astype(jnp.float32)[..., None] * inv_freq
    cos = jnp.cos(ang).astype(x.dtype)
    sin = jnp.sin(ang).astype(x.dtype)
    c_act = jax.nn.silu(c)

    for layer in range(DEPTH):
        mod = c_act @ ada_w[layer] + ada_b[layer]
        shift_m, scale_m, gate_m, shift_f, scale_f, gate_f = [
            m[:, None, :] for m in jnp.split(mod, N_MOD, axis=-1)]

        h = rmsnorm(x, norm_mix_g[layer]) * (1.0 + scale_m) + shift_m
        j = layer // N_MIXERS
        if layer % N_MIXERS == 0:
            y = gdn_mixer(h, gdn_w_in[j], gdn_conv_w[j], gdn_a_log[j], gdn_dt_bias[j],
                          gdn_norm_g[j], gdn_w_out[j])
        else:
            y = mla_mixer(h, cos, sin, mla_w_in[j], mla_q_norm_g[j], mla_kv_norm_g[j],
                          mla_w_uq[j], mla_w_ukv[j], mla_w_out[j])
        x = x + gate_m * y

        h = rmsnorm(x, norm_ffn_g[layer]) * (1.0 + scale_f) + shift_f
        x = x + gate_f * swiglu(h, ffn_w_gate[layer], ffn_w_up[layer], ffn_w_down[layer])

    return rmsnorm(x, final_norm_g)


DEPTH_2 = 1

RET_HEADS = 4
RET_QK_DIM = 128
RET_V_DIM = 256
RET_CHUNK = 128
ATTN_Q_HEADS = 16
ATTN_KV_HEADS = 2
ATTN_HEAD_DIM = 64
WINDOW = 128
ATTN_BLOCK = 128
D_FF_2 = -(-8 * D_MODEL // (3 * 256)) * 256

RET_QK = RET_HEADS * RET_QK_DIM
RET_V = RET_HEADS * RET_V_DIM
ATTN_Q = ATTN_Q_HEADS * ATTN_HEAD_DIM
ATTN_KV = ATTN_KV_HEADS * ATTN_HEAD_DIM
SPLITS = [RET_QK, RET_QK, RET_V, RET_V, ATTN_Q, ATTN_KV, ATTN_KV, D_MODEL, D_MODEL]
D_IN = sum(SPLITS)
SPLIT_IDX = [int(v) for v in np.cumsum(SPLITS)[:-1]]


def rms_norm(x, g):
    xf = x.astype(jnp.float32)
    y = xf * lax.rsqrt(jnp.mean(xf * xf, axis=-1, keepdims=True) + EPS)
    return (y * g.astype(jnp.float32)).astype(x.dtype)

def rotary(x, pos):
    d = x.shape[-1]
    half = d // 2
    inv_freq = ROPE_THETA ** (-jnp.arange(half, dtype=jnp.float32) / half)
    ang = pos.astype(jnp.float32)[:, None] * inv_freq[None, :]
    cos = jnp.cos(ang)[None, :, None, :]
    sin = jnp.sin(ang)[None, :, None, :]
    xf = x.astype(jnp.float32)
    x1, x2 = xf[..., :half], xf[..., half:]
    out = jnp.concatenate([x1 * cos - x2 * sin, x2 * cos + x1 * sin], axis=-1)
    return out.astype(x.dtype)

def retention_chunkwise(q, k, v):
    B, S, H, dk = q.shape
    dv = v.shape[-1]
    C = RET_CHUNK
    N = S // C
    log_gamma = jnp.log1p(-jnp.exp2(-5.0 - jnp.arange(H, dtype=jnp.float32)))
    idx = jnp.arange(C, dtype=jnp.float32)
    rel = idx[:, None] - idx[None, :]
    intra_decay = jnp.where(rel[None] >= 0,
                            jnp.exp(log_gamma[:, None, None] * jnp.maximum(rel, 0.0)[None]), 0.0)
    q_decay = jnp.exp(log_gamma[:, None] * (idx + 1.0))[None, :, :, None]
    k_decay = jnp.exp(log_gamma[:, None] * (C - 1.0 - idx))[None, :, :, None]
    chunk_decay = jnp.exp(log_gamma * C)[None, :, None, None]

    qf = q.astype(jnp.float32) * (dk ** -0.5)
    kf = k.astype(jnp.float32)
    vf = v.astype(jnp.float32)
    to_chunks = lambda t: t.reshape(B, N, C, H, t.shape[-1]).transpose(1, 0, 3, 2, 4)
    qc, kc, vc = to_chunks(qf), to_chunks(kf), to_chunks(vf)

    def step(state, inp):
        qn, kn, vn = inp
        scores = jnp.einsum('bhcd,bhsd->bhcs', qn, kn) * intra_decay
        inner = jnp.einsum('bhcs,bhse->bhce', scores, vn)
        cross = jnp.einsum('bhcd,bhde->bhce', qn, state) * q_decay
        new_state = state * chunk_decay + jnp.einsum('bhsd,bhse->bhde', kn * k_decay, vn)
        return new_state, inner + cross

    state0 = jnp.zeros((B, H, dk, dv), jnp.float32)
    _, out = lax.scan(step, state0, (qc, kc, vc))
    return out.transpose(1, 0, 3, 2, 4).reshape(B, S, H, dv)

def head_group_norm(y, g):
    B, S, H, dv = y.shape
    mu = jnp.mean(y, axis=-1, keepdims=True)
    yc = y - mu
    var = jnp.mean(yc * yc, axis=-1, keepdims=True)
    yn = (yc * lax.rsqrt(var + EPS)).reshape(B, S, H * dv)
    return yn * g.astype(jnp.float32)

def sliding_window_sink_attention(q, k, v, sinks):
    B, S, Hq, d = q.shape
    Hkv = k.shape[2]
    G = Hq // Hkv
    C = ATTN_BLOCK
    N = S // C
    qb = q.reshape(B, N, C, Hkv, G, d)
    pad = ((0, 0), (C, 0), (0, 0), (0, 0))
    kp = jnp.pad(k, pad).reshape(B, N + 1, C, Hkv, d)
    vp = jnp.pad(v, pad).reshape(B, N + 1, C, Hkv, d)
    kb = jnp.concatenate([kp[:, :-1], kp[:, 1:]], axis=2)
    vb = jnp.concatenate([vp[:, :-1], vp[:, 1:]], axis=2)
    scores = jnp.einsum('bnqhgd,bnkhd->bnhgqk', qb, kb).astype(jnp.float32) * (d ** -0.5)
    qi = jnp.arange(C)[:, None]
    kj = jnp.arange(2 * C)[None, :]
    rel = C + qi - kj
    key_pos = jnp.arange(N)[:, None, None] * C + kj[None] - C
    mask = (rel[None] >= 0) & (rel[None] < WINDOW) & (key_pos >= 0)
    scores = jnp.where(mask[None, :, None, None], scores, -1e30)
    sink = sinks.astype(jnp.float32).reshape(1, 1, Hkv, G, 1, 1)
    m = jnp.maximum(jnp.max(scores, axis=-1, keepdims=True), sink)
    e = jnp.exp(scores - m)
    probs = e / (jnp.sum(e, axis=-1, keepdims=True) + jnp.exp(sink - m))
    out = jnp.einsum('bnhgqk,bnkhd->bnqhgd', probs.astype(v.dtype), vb)
    return out.reshape(B, S, Hq, d)

def second_inputs(seed: int = 0) -> dict:
    key = jax.random.key(seed)
    ks = jax.random.split(key, 16)
    nrm = lambda k, shape, fan_in: jax.random.normal(k, shape, jnp.float32) * (fan_in ** -0.5)
    gain = lambda k, shape: 1.0 + 0.02 * jax.random.normal(k, shape, jnp.float32)
    return {
        "x": jax.random.normal(ks[0], (BATCH, SEQ, D_MODEL), jnp.float32),
        "ln1_g": gain(ks[1], (DEPTH_2, D_MODEL)),
        "w_in": nrm(ks[2], (DEPTH_2, D_MODEL, D_IN), D_MODEL),
        "b_in": 0.02 * jax.random.normal(ks[3], (DEPTH_2, D_IN), jnp.float32),
        "ret_norm_g": gain(ks[4], (DEPTH_2, RET_V)),
        "w_ret_out": nrm(ks[5], (DEPTH_2, RET_V, D_MODEL), RET_V),
        "attn_sinks": 0.5 * jax.random.normal(ks[6], (DEPTH_2, ATTN_Q_HEADS), jnp.float32),
        "w_attn_out": nrm(ks[7], (DEPTH_2, ATTN_Q, D_MODEL), ATTN_Q),
        "w_out": nrm(ks[8], (DEPTH_2, D_MODEL, D_MODEL), D_MODEL),
        "ln2_g": gain(ks[9], (DEPTH_2, D_MODEL)),
        "w_ffn_gate": nrm(ks[10], (DEPTH_2, D_MODEL, D_FF_2), D_MODEL),
        "w_ffn_up": nrm(ks[11], (DEPTH_2, D_MODEL, D_FF_2), D_MODEL),
        "w_ffn_down": nrm(ks[12], (DEPTH_2, D_FF_2, D_MODEL), D_FF_2),
        "lnf_g": gain(ks[13], (D_MODEL,)),
    }

def second_block(x, ln1_g, w_in, b_in, ret_norm_g, w_ret_out, attn_sinks, w_attn_out, w_out,
              ln2_g, w_ffn_gate, w_ffn_up, w_ffn_down, lnf_g):
    B, S, _ = x.shape
    pos = jnp.arange(S, dtype=jnp.int32)
    for l in range(DEPTH_2):
        h = rms_norm(x, ln1_g[l])
        proj = h @ w_in[l] + b_in[l]
        rq, rk, rv, rg, aq, ak, av, gate_a, gate_b = jnp.split(proj, SPLIT_IDX, axis=-1)

        rq = rotary(rq.reshape(B, S, RET_HEADS, RET_QK_DIM), pos)
        rk = rotary(rk.reshape(B, S, RET_HEADS, RET_QK_DIM), pos)
        ry = retention_chunkwise(rq, rk, rv.reshape(B, S, RET_HEADS, RET_V_DIM))
        ry = head_group_norm(ry, ret_norm_g[l]).astype(x.dtype)
        branch_a = (jax.nn.silu(rg) * ry) @ w_ret_out[l]

        aq = rotary(aq.reshape(B, S, ATTN_Q_HEADS, ATTN_HEAD_DIM), pos)
        ak = rotary(ak.reshape(B, S, ATTN_KV_HEADS, ATTN_HEAD_DIM), pos)
        ay = sliding_window_sink_attention(aq, ak, av.reshape(B, S, ATTN_KV_HEADS, ATTN_HEAD_DIM),
                                           attn_sinks[l])
        branch_b = ay.reshape(B, S, ATTN_Q) @ w_attn_out[l]

        merged = jax.nn.sigmoid(gate_a) * branch_a + jax.nn.sigmoid(gate_b) * branch_b
        x = x + merged @ w_out[l]

        h2 = rms_norm(x, ln2_g[l])
        x = x + (jax.nn.silu(h2 @ w_ffn_gate[l]) * (h2 @ w_ffn_up[l])) @ w_ffn_down[l]
    return rms_norm(x, lnf_g)


def setup_inputs(seed=0):
    out = dict(first_inputs(seed))
    for name, value in second_inputs(seed + 1).items():
        if name != "x":
            out[name + "_2"] = value
    return out


def reference(
    x, c, positions, ada_w, ada_b, norm_mix_g, norm_ffn_g, gdn_w_in, gdn_conv_w, gdn_a_log,
    gdn_dt_bias, gdn_norm_g, gdn_w_out, mla_w_in, mla_q_norm_g, mla_kv_norm_g, mla_w_uq,
    mla_w_ukv, mla_w_out, ffn_w_gate, ffn_w_up, ffn_w_down, final_norm_g, ln1_g_2, w_in_2,
    b_in_2, ret_norm_g_2, w_ret_out_2, attn_sinks_2, w_attn_out_2, w_out_2, ln2_g_2,
    w_ffn_gate_2, w_ffn_up_2, w_ffn_down_2, lnf_g_2,
):
    x = first_block(
        x, c, positions, ada_w, ada_b, norm_mix_g, norm_ffn_g, gdn_w_in, gdn_conv_w, gdn_a_log,
        gdn_dt_bias, gdn_norm_g, gdn_w_out, mla_w_in, mla_q_norm_g, mla_kv_norm_g, mla_w_uq,
        mla_w_ukv, mla_w_out, ffn_w_gate, ffn_w_up, ffn_w_down, final_norm_g,
    )
    return second_block(
        x, ln1_g_2, w_in_2, b_in_2, ret_norm_g_2, w_ret_out_2, attn_sinks_2, w_attn_out_2,
        w_out_2, ln2_g_2, w_ffn_gate_2, w_ffn_up_2, w_ffn_down_2, lnf_g_2,
    )


_drawn_inputs = setup_inputs


def setup_inputs(seed=0):
    import zlib

    import numpy as np

    out = dict(_drawn_inputs(seed))
    spreads = {}
    factors = {'gdn_norm_g': 3.941,
     'mla_q_norm_g': 8.0,
     'mla_kv_norm_g': 7.739,
     'ln1_g_2': 3.765,
     'b_in_2': 2.796,
     'ret_norm_g_2': 8.0,
     'attn_sinks_2': 64.0,
     'ln2_g_2': 12.15,
     'lnf_g_2': 7.718}
    for name, (base, spread) in spreads.items():
        noise = np.random.default_rng([zlib.crc32(name.encode()), seed]).standard_normal(out[name].shape)
        drawn = base * np.exp(spread * noise) if base else spread * noise
        out[name] = __import__('jax').numpy.asarray(drawn.astype(out[name].dtype))
    for name, factor in factors.items():
        out[name] = (out[name] * factor).astype(out[name].dtype)
    return out
```

```python
import numpy as np
import concourse.bass as bass
from concourse import mybir
from contextlib import ExitStack

P = 128
DM, T, NT = 1024, 512, 4
KC = DM // P
SLAB = 2048
EPS = 1e-6
DFF = 2816
FA, FB = 16, 6
GH = 8
N_AB, N_GDN, N_OUT = 1, 16, 4
N_GUA, N_DNA, N_GUB, N_DNB = FA, KC, FB, KC // 2
N_FFN = N_GUA + N_DNA + N_GUB + N_DNB
N_MIN, N_MLA = 3, 16
N_RET, N_GR, N_KV, N_AQ, N_GA = 12, 8, 2, 4, 8
G_AB = 0
G_GDN = G_AB + N_AB
G_GOUT = G_GDN + N_GDN
G_FFN0 = G_GOUT + N_OUT
G_MIN = G_FFN0 + N_FFN
G_MLA = G_MIN + N_MIN
G_MOUT = G_MLA + N_MLA
G_FFN1 = G_MOUT + N_OUT
G_RET = G_FFN1 + N_FFN
G_GR = G_RET + N_RET
G_KV = G_GR + N_GR
G_AQ = G_KV + N_KV
G_GA = G_AQ + N_AQ
G_ROUT = G_GA + N_GA
G_FFN2 = G_ROUT + N_OUT
N_SLABS = G_FFN2 + N_FFN
ADA_L = 24
ADA0 = 8
ADA_P = 8
V = {}
def _vec(name, n, at=[0]):
    V[name] = at[0]
    at[0] += n
for _n, _k in (("c", 8), ("ada_b", 96), ("mix_g", 16), ("ffn_g", 16), ("conv", 96), ("gdn_g", 1), ("a_log", 1),
               ("dt_b", 1), ("q_g", 3), ("kv_g", 2), ("fin_g", 8), ("ln1", 8), ("b_in", 42), ("ret_g", 8),
               ("ln2", 8), ("lnf", 8), ("sink", 16), ("zero", 1), ("kdec", 4), ("freq", 2), ("eps", 1), ("cdec", 4)):
    _vec(_n, _k)
NV = sum((8, 96, 16, 16, 96, 1, 1, 1, 3, 2, 8, 8, 42, 8, 8, 8, 16, 1, 4, 2, 1, 4))
C_ID, C_ONE, C_NEG, C_CAUS = 0, 128, 256, 384
NC_ = 512


class Chain:
    def __init__(self, eng, sem):
        self.eng, self.sem, self.base, self.at, self.i, self.per = eng, sem, 0, 0, None, 0

    def enter(self, i, per):
        self.i, self.per, self.at = i, per, 0

    def leave(self, n):
        assert self.at == self.per, (self.at, self.per)
        self.base, self.at, self.i = self.base + n * self.per, 0, None

    def link(self, ins):
        ins.then_inc(self.sem, 1)
        if self.i is None:
            self.base += 1
            self.eng.wait_ge(self.sem, self.base)
        else:
            self.at += 1
            self.eng.wait_ge(self.sem, self.i * self.per + (self.base + self.at))


class Slab:
    def __init__(self, b, i=None, step=0):
        self.b, self.i, self.step, self.slot = b, i, step, b % 2

    def plus(self, k):
        return self.b + k if self.i is None else self.i * self.step + (self.b + k)

    def prior(self, k=0, times=1):
        n = ((self.b - self.slot) // 2 + k) * times
        return n if self.i is None else self.i * (self.step // 2 * times) + n

    def next(self, k=1):
        return Slab(self.b + k, self.i, self.step)


def at(base, i=None, step=0):
    return base if i is None else i * step + base


def loop(eng, n, body, chain=None, per=0):
    with eng.Fori(0, n) as i:
        if chain:
            chain.enter(i, per)
        body(i)
    if chain:
        chain.leave(n)


def build(nc, slabs, ada, vecs, consts, masks, rope, vbias, pos, xin, out):
    fp32, f32r, i32 = mybir.dt.float32, mybir.dt.float32r, mybir.dt.int32
    ALU, ACT, AX = mybir.AluOpType, mybir.ActivationFunctionType, mybir.AxisListType
    V_, S_, T_ = nc.vector, nc.scalar, nc.tensor
    ctx = ExitStack()
    with ctx:
        def sb(name, shape, dt=fp32, scope=ctx):
            return scope.enter_context(nc.sbuf_tensor(name, shape, dt))

        def sem(name):
            return ctx.enter_context(nc.semaphore(name))

        x = sb("x", [P, KC, T])
        raw = [sb(f"raw{s}", [P, SLAB]) for s in range(2)]
        hi = [sb(f"hi{s}", [P, SLAB], f32r) for s in range(2)]
        lo = [sb(f"lo{s}", [P, SLAB], f32r) for s in range(2)]
        vec = sb("vec", [P, NV])
        cst = sb("cst", [P, NC_])
        ident, ones, neg, caus = (cst[:, c:c + P] for c in (C_ID, C_ONE, C_NEG, C_CAUS))
        mod = sb("mod", [P, 96])
        eps = vec[:, V["eps"]:V["eps"] + 1]
        gsc = sb("gsc", [P, 4 * KC])
        hH = sb("hH", [P, KC, T], f32r)
        hL = sb("hL", [P, KC, T], f32r)
        small = sb("small", [P, 64])
        posi = sb("posi", [P, T], i32)
        swp = sb("swp", [P, 2 * P])
        D = [ctx.enter_context(nc.psum_tensor(f"D{i}", [P, 2, T], fp32)) for i in range(4)]

        first = ExitStack()
        ctx.enter_context(first)
        adar = [sb(f"adar{s}", [P, SLAB], scope=first) for s in range(2)]
        cact = sb("cact", [P, KC], scope=first)

        gdn = ExitStack()
        lvl = sb("lvl", [P, 7 * P], i32, gdn)
        rows = sb("rows", [GH, 4, T], scope=gdn)
        tsc = sb("tsc", [P, 4, NT, GH], scope=gdn)
        qs = sb("qs", [P, 2, T], scope=gdn)
        ks = sb("ks", [P, 2, T], scope=gdn)
        vs = sb("vs", [P, 2, T], scope=gdn)
        gs = sb("gs", [P, 2, T], scope=gdn)
        sq = sb("sq", [P, 4, T], scope=gdn)
        rtmp = sq[0:GH, 0:3]
        eg = sb("eg", [P, 2, T], scope=gdn)
        dt = sb("dt", [P, 2, T], scope=gdn)
        kb = sb("kb", [P, 2, T], scope=gdn)
        qd = sb("qd", [P, 2, T], scope=gdn)
        up = sb("up", [P, 2, T], scope=gdn)
        att = sb("att", [P, 2, T], scope=gdn)
        xi = sb("xi", [P, 2, T], scope=gdn)
        zi = sb("zi", [P, 2, T], scope=gdn)
        st = sb("st", [P, 4, P], scope=gdn)
        vn = sb("vn", [P, 2, P], scope=gdn)
        go = sb("go", [P, KC, T], scope=gdn)
        gdn.close()
        ffn = ExitStack()
        aH = sb("aH", [P, FA, T], f32r, ffn)
        aL = sb("aL", [P, FA, T], f32r, ffn)
        sg = sb("sg", [P, 2, T], scope=ffn)
        af = sb("af", [P, 2, T], scope=ffn)
        nrs = sb("nrs", [P, T], scope=ffn)
        ffn.close()
        mla = ExitStack()
        craw = sb("craw", [P, 6, T], scope=mla)
        cH = sb("cH", [P, 5, T], f32r, mla)
        cL = sb("cL", [P, 5, T], f32r, mla)
        mcos = sb("mcos", [P, T], scope=mla)
        msin = sb("msin", [P, T], scope=mla)
        qn = sb("qn", [P, 2, T], scope=mla)
        qr0 = sb("qr0", [P, T], scope=mla)
        qr = sb("qr", [P, T], scope=mla)
        kn = sb("kn", [P, 2, T], scope=mla)
        vt = sb("vt", [P, NT, 2 * P], scope=mla)
        pr = sb("pr", [P, 2, T], scope=mla)
        pT = sb("pT", [P, 2, T], scope=mla)
        krp = sb("krp", [P, T], scope=mla)
        nsq = sb("nsq", [P, 2, T], scope=mla)
        ntm = sb("ntm", [P, 2, T], scope=mla)
        mrs = sb("mrs", [P, T], scope=mla)
        mla.close()
        first.close()
        blk2 = ExitStack()
        TAB = 7 * T
        tab = sb("tab", [P, TAB], scope=blk2)
        rcos, rsin, acos, asin, intra, qdec, win = (tab[:, k * T:k * T + T] for k in range(7))
        vb = sb("vb", [P, 9 * P], scope=blk2)
        rH = sb("rH", [P, KC, T], f32r, blk2)
        rL = sb("rL", [P, KC, T], f32r, blk2)
        qk = sb("qk", [P, 2, T], scope=blk2)
        kq = sb("kq", [P, 2, T], scope=blk2)
        tm2 = sb("tm2", [P, 2, T], scope=blk2)
        rvt = sb("rvt", [P, NT, 2 * P], scope=blk2)
        rg = sb("rg", [P, 2, T], scope=blk2)
        ka = sb("ka", [P, 2, T], scope=blk2)
        qde = sb("qde", [P, T], scope=blk2)
        rst = sb("rst", [P, 2, 2 * P], scope=blk2)
        ry = sb("ry", [P, 2, T], scope=blk2)
        rsq = sb("rsq", [P, 2, T], scope=blk2)
        mg = sb("mg", [P, KC, T], scope=blk2)
        blk2.close()

        x_in, slab_in, ada_in = sem("x_in"), [sem("slab_in0"), sem("slab_in1")], [sem("ada_in0"), sem("ada_in1")]
        hi_ready, lo_ready, slab_done = sem("hi_ready"), sem("lo_ready"), sem("slab_done")
        bank_free = [sem("bank_free0"), sem("bank_free1")]
        ada_done, mod_ready, cact_ready = sem("ada_done"), sem("mod_ready"), sem("cact_ready")
        ada_sum, pool_chain = sem("ada_sum"), sem("pool_chain")
        act_chain, dve_chain = sem("act_chain"), sem("dve_chain")
        sq_ready, sq_used, ssq_ready, xg_ready = sem("sq_ready"), sem("sq_used"), sem("ssq_ready"), sem("xg_ready")
        hh_ready, h_ready = sem("hh_ready"), sem("h_ready")
        aH_ready, aL_ready = sem("aH_ready"), sem("aL_ready")
        out_done = sem("out_done")
        tab_in = sem("tab_in")
        rms_ready = sem("rms_ready")

        def product(pe, s, kc, nt, H, L, between={}):
            pe.wait_ge(lo_ready, s.plus(1))
            if s.b >= 2:
                pe.wait_ge(bank_free[s.slot], s.prior())
            for m in range(nt):
                for k in range(kc):
                    if m * kc + k in between:
                        between[m * kc + k]()
                    w = slice((k * nt + m) * P, (k * nt + m + 1) * P)
                    o = D[s.slot][:, m, :]
                    T_.matmul(o, lo[s.slot][:, w], H[:, k, :], start=(k == 0), stop=False)
                    T_.matmul(o, hi[s.slot][:, w], L[:, k, :], start=False, stop=False)
                    last = T_.matmul(o, hi[s.slot][:, w], H[:, k, :], start=False, stop=(k == kc - 1))
            last.then_inc(slab_done, 1)

        def product_t(pe, s, kc, H, L, width=2 * P):
            pe.wait_ge(lo_ready, s.plus(1))
            pe.wait_ge(bank_free[s.slot], s.prior())
            for t in range(NT):
                o = D[s.slot].rearrange("p a (b n) -> p (a b) n", b=2)[:, t, 0:width]
                tok = slice(t * P, (t + 1) * P)
                for k in range(kc):
                    w = slice(k * 2 * P, k * 2 * P + width)
                    T_.matmul(o, L[:, k, tok], hi[s.slot][:, w], start=(k == 0), stop=False)
                    T_.matmul(o, H[:, k, tok], lo[s.slot][:, w], start=False, stop=False)
                    last = T_.matmul(o, H[:, k, tok], hi[s.slot][:, w], start=False, stop=(k == kc - 1))
            last.then_inc(slab_done, 1)

        def split_hi(act, s):
            act.wait_ge(slab_in[s.slot], s.prior(1, 16))
            if s.b >= 2:
                act.wait_ge(slab_done, s.plus(-1))
            S_.activation(hi[s.slot][:], raw[s.slot][:], ACT.Copy).then_inc(hi_ready, 1)

        def split_lo(dve, s):
            dve.wait_ge(hi_ready, s.plus(1))
            V_.tensor_tensor(lo[s.slot][:], raw[s.slot][:], hi[s.slot][:], ALU.subtract).then_inc(lo_ready, 1)

        def ada_mm(pe, a):
            pe.wait_ge(ada_in[a.slot], a.prior(1, 16))
            for m in range(2):
                for k in range(KC):
                    last = T_.matmul(D[3][:, 1, bass.ds(at(2 * a.b + m, a.i, 2 * a.step), 1)],
                                     adar[a.slot][:, (2 * k + m) * P:(2 * k + m + 1) * P], cact[:, k:k + 1],
                                     start=(k == 0), stop=(k == KC - 1))
            last.then_inc(ada_done, 1)

        def ada_chunks(pool, chain):
            def body(i):
                for j in range(2):
                    a = Slab(ADA0 + j, i, 2)
                    r = adar[a.slot]
                    pool.wait_ge(ada_in[a.slot], a.prior(1, 16))
                    r3 = r[:].rearrange("p (k n) -> p k n", k=KC)
                    chain.link(nc.gpsimd.tensor_tensor(r3, r3, cact[:].unsqueeze(2).to_broadcast([P, KC, 2 * P]),
                                                       ALU.mult))
                    for n in (4 * 2 * P, 2 * 2 * P, 2 * P):
                        last = nc.gpsimd.tensor_tensor(r[:, 0:n], r[:, 0:n], r[:, n:2 * n], ALU.add)
                        if n > 2 * P:
                            chain.link(last)
                    last.then_inc(ada_sum, 1)
            loop(pool, (2 * ADA_L - ADA0) // 2, body, chain, 6)

        def ada_pe(pe, a, wait_mod):
            pe.wait_ge(mod_ready, wait_mod)
            pe.wait_ge(ada_sum, a.plus(1 - ADA0))
            for m in range(2):
                last = T_.matmul(D[3][:, 1, bass.ds(at(2 * a.b + m, a.i, 2 * a.step), 1)],
                                 adar[a.slot][:, m * P:(m + 1) * P], ones[:, 0:1], start=True, stop=True)
            last.then_inc(ada_done, 1)

        def load_slab(sp, s):
            if s.b >= 2:
                sp.wait_ge(lo_ready, s.plus(-1))
            sp.dma_start(raw[s.slot][:], slabs[bass.ds(s.plus(0), 1), :, :].rearrange("a p n -> p (a n)")
                         if s.i is not None else slabs[s.b, :, :]).then_inc(slab_in[s.slot], 16)

        def load_ada(sp, a):
            if a.b >= 2:
                sp.wait_ge(ada_done, a.plus(-1))
            sp.dma_start(adar[a.slot][:], ada[bass.ds(a.plus(0), 1), :, :].rearrange("a p n -> p (a n)")
                         if a.i is not None else ada[a.b, :, :]).then_inc(ada_in[a.slot], 16)

        def norm_pe(pe, n, nsq):
            for c in range(KC):
                pe.wait_ge(sq_ready, KC * n + c + 1)
                last = T_.matmul(D[2][:, 0, :], ones, nsq[:, c % 2, :], start=(c == 0), stop=(c == KC - 1))
                last.then_inc(sq_used, 1)

        def x_normed(n):
            return lambda eng: eng.wait_ge(xg_ready, KC * n)

        def x_written(eng, g):
            for s in (Slab(g - 1), Slab(g - 2)):
                eng.wait_ge(bank_free[s.slot], s.prior(1))

        def norm_act(act, n, nsq, nrs, ntm, shift, g, to_h=True):
            if callable(g):
                g(act)
            elif g:
                x_written(act, g)
            else:
                act.wait_ge(x_in, 16)
            for c in range(KC):
                if c >= 2 or n:
                    act.wait_ge(sq_used, KC * n + c - 1)
                S_.activation(nsq[:, c % 2, :], x[:, c, :], ACT.Square, scale=DM ** -0.5).then_inc(sq_ready, 1)
            act.wait_ge(sq_used, KC * n + KC)
            S_.activation(nrs, D[2][:, 0, :], ACT.Ln, bias=eps).then_inc(rms_ready, 1)
            act.wait_ge(rms_ready, 2 * n + 1)
            S_.activation(nrs, nrs, ACT.Exp, scale=-0.5).then_inc(rms_ready, 1)
            for c in range(KC if to_h else 0):
                act.wait_ge(xg_ready, KC * n + c + 1)
                S_.activation(hH[:, c, :], ntm[:, c % 2, :], ACT.Identity, bias=shift(c)).then_inc(hh_ready, 1)

        def norm_dve(dve, n, hb, nrs, ntm, gain, shift, chain):
            dve.wait_ge(rms_ready, 2 * n + 2)
            for c in range(KC + 1):
                if c < KC:
                    if c >= 2:
                        dve.wait_ge(h_ready, KC * hb + c - 1)
                    V_.scalar_tensor_tensor(out=ntm[:, c % 2, :], in0=x[:, c, :], scalar=gain(c), in1=nrs,
                                            op0=ALU.mult, op1=ALU.mult).then_inc(xg_ready, 1)
                if c >= 1:
                    dve.wait_ge(hh_ready, KC * hb + c)
                    dve.wait_ge(xg_ready, KC * n + c)
                    V_.scalar_tensor_tensor(out=hL[:, c - 1, :], in0=ntm[:, (c - 1) % 2, :], scalar=shift(c - 1),
                                            in1=hH[:, c - 1, :], op0=ALU.add, op1=ALU.subtract).then_inc(h_ready, 1)

        def norm_x_dve(dve, n, nrs, gain, chain):
            dve.wait_ge(rms_ready, 2 * n + 2)
            for c in range(KC):
                V_.scalar_tensor_tensor(out=x[:, c, :], in0=x[:, c, :], scalar=gain(c), in1=nrs,
                                        op0=ALU.mult, op1=ALU.mult).then_inc(xg_ready, 1)

        def to_h_act(act, src):
            for c in range(KC):
                S_.activation(hH[:, c, :], src[:, c, :], ACT.Copy).then_inc(hh_ready, 1)

        def to_h_dve(dve, hb, src):
            for c in range(KC):
                dve.wait_ge(hh_ready, KC * hb + c + 1)
                V_.tensor_tensor(hL[:, c, :], src[:, c, :], hH[:, c, :], ALU.subtract).then_inc(h_ready, 1)

        def add_act(act, base, n):
            def body(i):
                for j in range(2):
                    split_hi(act, Slab(base + j, i, 2).next())
            loop(act, n // 2, body)

        def add_dve(dve, base, n, nt, gate):
            def body(i):
                for j in range(2):
                    s = Slab(base + j, i, 2)
                    split_lo(dve, s.next())
                    dve.wait_ge(slab_done, s.plus(1))
                    for m in range(nt):
                        c = at(nt * j + m, i, 2 * nt)
                        xc = x[:, bass.ds(c, 1), :].rearrange("p a n -> p (a n)")
                        last = V_.scalar_tensor_tensor(out=xc, in0=D[s.slot][:, m, :],
                                                       scalar=gate(c) if gate else 1.0, in1=xc,
                                                       op0=ALU.mult, op1=ALU.add)
                    last.then_inc(bank_free[s.slot], 1)
            loop(dve, n // 2, body)

        MD = lambda layer, part: 48 * layer + KC * part

        def gain_cols(chain, norm, src, layer, part):
            chain.link(V_.scalar_tensor_tensor(
                out=gsc[:, KC * norm:KC * norm + KC], in0=mod[:, MD(layer, part):MD(layer, part) + KC], scalar=1.0,
                in1=vec[:, V[src] + KC * layer:V[src] + KC * layer + KC], op0=ALU.add, op1=ALU.mult))

        def mod_dve(dve, chain, lo_, hi_, ada_n):
            dve.wait_ge(ada_done, ada_n)
            V_.tensor_tensor(mod[:, lo_:hi_], D[3][:, 1, lo_:hi_], vec[:, V["ada_b"] + lo_:V["ada_b"] + hi_],
                             ALU.add).then_inc(mod_ready, 1)

        gg = {n: sem("g_" + n) for n in (
            "row", "rowd", "rowp", "qkv", "sq", "ssq", "qkn", "sel", "br", "dif", "expd", "egr", "kbq", "gram", "up",
            "kt", "ktv", "bb", "pp", "pb", "qq1", "qq2", "qq3", "qq4",
            "qq5", "qq6", "xx", "xt", "zz", "wtp", "wt", "vp", "vn", "op", "stp", "st", "osq", "oss",
            "of", "rt", "ort")}

        def tiles(t_, m=None):
            v = t_[:].rearrange("p m (t n) -> p m t n", t=NT)
            return v if m is None else v[:, m]

        def over(ap, n=NT):
            return ap.unsqueeze(1).to_broadcast([P, n, P])

        def rows_dve(dve, chain):
            L = chain.link
            a_, u_, w_ = (rtmp[:, k, :] for k in range(3))
            gc, beta, dl, nbe = (rows[:, k, :] for k in range(4))
            dve.wait_ge(slab_done, 1)
            L(V_.tensor_scalar(a_, D[0][0:GH, 0, :], vec[0:GH, V["dt_b"]:V["dt_b"] + 1], None, ALU.add))
            L(V_.tensor_copy(beta, D[0][0:GH, 1, :]))
            V_.scalar_tensor_tensor(out=u_, in0=a_, scalar=-1.0, in1=a_, op0=ALU.mult, op1=ALU.max).then_inc(bank_free[0], 1)
            dve.wait_ge(gg["row"], 2)
            L(V_.tensor_scalar(w_, u_, 1.0, None, ALU.add))
            L(V_.tensor_copy(gc, w_))
            L(V_.tensor_scalar(dl, w_, 1.0, None, ALU.subtract))
            V_.tensor_scalar(w_, dl, 0.0, None, ALU.is_equal).then_inc(gg["rowd"], 1)
            dve.wait_ge(gg["row"], 3)
            dve.wait_ge(gg["rowd"], 1)
            L(V_.tensor_tensor(gc, gc, w_, ALU.add))
            L(V_.tensor_tensor(dl, dl, w_, ALU.add))
            L(V_.tensor_tensor(gc, gc, u_, ALU.mult))
            L(V_.reciprocal(dl, dl))
            L(V_.tensor_tensor(gc, gc, dl, ALU.mult))
            L(V_.scalar_tensor_tensor(out=gc, in0=a_, scalar=0.0, in1=gc, op0=ALU.max, op1=ALU.add))
            L(V_.tensor_scalar(a_, gc, small[0:GH, 0:1], -1.0, ALU.mult, ALU.mult))
            L(V_.memset(w_, 0.0))
            for t in range(NT):
                c = slice(t * P, t * P + P)
                L(V_.tensor_tensor_scan(gc[:, c], a_[:, c], w_[:, c], 0.0, ALU.add, ALU.add))
            g3 = gc.rearrange("p (t n) -> p t n", t=NT)
            V_.tensor_tensor(u_.rearrange("p (t n) -> p t n", t=NT), g3[:, :, P - 1:P].to_broadcast([GH, NT, P]), g3,
                             ALU.subtract).then_inc(gg["rowd"], 1)
            dve.wait_ge(gg["row"], 5)
            V_.scalar_tensor_tensor(out=nbe, in0=beta, scalar=-1.0, in1=w_, op0=ALU.mult,
                                    op1=ALU.mult).then_inc(gg["rowd"], 1)
            dve.wait_ge(gg["rowp"], 1)
            V_.tensor_copy(tsc[:].rearrange("p a t h -> p (a t h)"), D[3][:, 0, 0:4 * NT * GH]).then_inc(gg["of"], 1)
            dve.wait_ge(gg["of"], 1)

        def rows_act(act):
            u_, w_ = rtmp[:, 1, :], rtmp[:, 2, :]
            gc, beta, dl = (rows[:, k, :] for k in range(3))
            S_.activation(small[0:GH, 0:1], vec[0:GH, V["a_log"]:V["a_log"] + 1], ACT.Exp)
            act.wait_ge(bank_free[0], 1)
            S_.activation(beta, beta, ACT.Sigmoid).then_inc(gg["row"], 1)
            S_.activation(u_, u_, ACT.Exp, scale=-1.0).then_inc(gg["row"], 1)
            act.wait_ge(gg["rowd"], 1)
            S_.activation(gc, gc, ACT.Ln).then_inc(gg["row"], 1)
            act.wait_ge(gg["rowd"], 2)
            S_.activation(w_, gc, ACT.Exp).then_inc(gg["row"], 1)
            S_.activation(dl, u_, ACT.Exp).then_inc(gg["row"], 1)

        def rows_pe(pe):
            pe.wait_ge(gg["rowd"], 3)
            for a in range(4):
                for t in range(NT):
                    o = (a * NT + t) * GH
                    last = T_.transpose(D[3][:, 0, o:o + GH], rows[:, a, t * P:t * P + P], ident[0:GH, 0:GH])
            last.then_inc(gg["rowp"], 1)

        PAIR = 4
        qkv = (qs, ks, vs)
        half_t = lambda t_, m: t_[:, m, :].rearrange("p (t n) -> p t n", t=NT)

        def gdn_act(act):
            def body(p):
                w = lambda n, k, per: act.wait_ge(gg[n], at(k, p, per))

                def conv_done(j):
                    s = Slab(G_GDN + j, p, PAIR)
                    act.wait_ge(bank_free[s.slot], s.prior(1))
                    S_.activation(qkv[j][:], qkv[j][:], ACT.Silu).then_inc(gg["qkv"], 1)

                def log(a):
                    w("ssq", a + 1, 2)
                    S_.activation(sq[:, 2 * a:2 * a + 2], D[2][:], ACT.Ln, bias=eps).then_inc(gg["rt"], 1)
                split_hi(act, Slab(G_GDN + 1, p, PAIR))
                w("br", 1, 2)
                S_.activation(kb[:], D[2][:], ACT.Copy).then_inc(gg["bb"], 1)
                split_hi(act, Slab(G_GDN + 2, p, PAIR))
                w("br", 2, 2)
                S_.activation(eg[:], D[2][:], ACT.Exp).then_inc(gg["egr"], 1)
                conv_done(0)
                w("qkv", 1, 3)
                S_.activation(sq[:, 0:2], qs[:], ACT.Square).then_inc(gg["sq"], 1)
                split_hi(act, Slab(G_GDN + 3, p, PAIR))
                w("dif", 1, 1)
                S_.activation(dt[:], dt[:], ACT.Exp).then_inc(gg["expd"], 1)
                log(0)
                conv_done(1)
                w("qkv", 2, 3)
                S_.activation(sq[:, 2:4], ks[:], ACT.Square).then_inc(gg["sq"], 1)
                split_hi(act, Slab(G_GDN + 4, p, PAIR))
                log(1)
                w("rt", 2, 3)
                S_.activation(sq[:], sq[:], ACT.Exp, scale=-0.5).then_inc(gg["rt"], 1)
                conv_done(2)
                s = Slab(G_GDN + 3, p, PAIR)
                act.wait_ge(slab_done, s.plus(1))
                S_.activation(gs[:], D[s.slot][:], ACT.Silu).then_inc(bank_free[s.slot], 1)
                for lv in range(7):
                    for m in range(2 if lv else 0):
                        w("pp", 2 * lv - 1 + m, 12)
                        S_.activation(sq[:, m], D[0][:, m, :], ACT.Copy).then_inc(gg["pb"], 1)
                    for m in range(2):
                        w("xt", 2 * lv + m + 1, 14)
                        S_.activation((zi if lv else xi)[:, m], D[2][:, m, :], ACT.Copy).then_inc(gg["zz"], 1)
                w("wtp", 1, 1)
                S_.activation(sq[:, 2:4], D[0][:], ACT.Copy).then_inc(gg["wt"], 1)
                for t in range(NT):
                    w("vp", t + 1, NT)
                    S_.activation(vn[:], D[1][:, :, 0:P], ACT.Copy).then_inc(gg["vn"], 1)
                w("op", 1, 1)
                S_.activation(sq[:, 0:2], D[2][:], ACT.Square, scale=P ** -0.5).then_inc(gg["osq"], 1)
                w("oss", 1, 1)
                S_.activation(sq[:, 2:4], D[0][:], ACT.Ln, bias=eps).then_inc(gg["ort"], 1)
                w("ort", 1, 2)
                S_.activation(sq[:, 2:4], sq[:, 2:4], ACT.Exp, scale=-0.5).then_inc(gg["ort"], 1)
            split_hi(act, Slab(G_GDN))
            loop(act, GH // 2, body)

        def gdn_dve(dve, chain):
            def body(p):
                L = chain.link
                w = lambda n, k, per: dve.wait_ge(gg[n], at(k, p, per))

                def conv(j):
                    s = Slab(G_GDN + j, p, PAIR)
                    dve.wait_ge(slab_done, s.plus(1))
                    for tap in range(4):
                        for m in range(2):
                            cw = vec[:, bass.ds(at(V["conv"] + (j * GH + m) * 4 + 3 - tap, p, 8), 1)]
                            o = qkv[j][:, m, tap:]
                            if tap == 0:
                                last = V_.tensor_scalar(o, D[s.slot][:, m, :], cw, None, ALU.mult)
                            else:
                                last = V_.scalar_tensor_tensor(out=o, in0=D[s.slot][:, m, 0:T - tap], scalar=cw, in1=o,
                                                               op0=ALU.mult, op1=ALU.add)
                        if tap < 3:
                            L(last)
                    last.then_inc(bank_free[s.slot], 1)
                for m in range(2):
                    one = cst[0:GH, bass.ds(at(C_ID + m, p, 2), 1)]
                    V_.tensor_scalar(up[0:GH, m, :], rows[:, 0, :], one, None, ALU.mult)
                    last = V_.tensor_scalar(att[0:GH, m, :], rows[:, 1, :], one, None, ALU.mult)
                last.then_inc(gg["sel"], 1)
                split_lo(dve, Slab(G_GDN + 1, p, PAIR))
                conv(0)
                split_lo(dve, Slab(G_GDN + 2, p, PAIR))
                w("br", 2, 2)
                w("egr", 1, 1)
                for m in range(2):
                    gcj = tsc[:, 0, :, bass.ds(at(m, p, 2), 1)].to_broadcast([P, NT, P])
                    last = V_.tensor_tensor(tiles(dt, m), tiles(D[2], m), gcj, ALU.subtract)
                L(last)
                V_.tensor_tensor(dt[:].rearrange("p m (t n) -> p (m t) n", t=NT),
                                 dt[:].rearrange("p m (t n) -> p (m t) n", t=NT), over(neg, 2 * NT),
                                 ALU.min).then_inc(gg["dif"], 1)
                conv(1)
                split_lo(dve, Slab(G_GDN + 3, p, PAIR))
                conv(2)
                split_lo(dve, Slab(G_GDN + 4, p, PAIR))
                w("rt", 3, 3)
                w("qkv", 2, 3)
                V_.scalar_tensor_tensor(out=qs[:], in0=qs[:], scalar=P ** -0.5, in1=sq[:, 0:2], op0=ALU.mult,
                                        op1=ALU.mult)
                L(V_.tensor_tensor(ks[:], ks[:], sq[:, 2:4], ALU.mult))
                w("bb", 1, 1)
                V_.tensor_tensor(kb[:], ks[:], kb[:], ALU.mult).then_inc(gg["kbq"], 1)
                V_.tensor_tensor(qd[:], qs[:], eg[:], ALU.mult).then_inc(gg["kbq"], 1)
                w("expd", 1, 1)
                for m in range(2):
                    w("gram", m + 1, 3)
                    V_.scalar_tensor_tensor(out=up[:, m], in0=D[1][:, m, :], scalar=-1.0, in1=dt[:, m], op0=ALU.mult,
                                            op1=ALU.mult).then_inc(gg["up"], 1)
                    if m == 0:
                        L(V_.tensor_copy(zi[:].rearrange("p m (t n) -> p (m t) n", t=NT), over(ident, 2 * NT)))
                for m in range(2):
                    dve.wait_ge(x_in, 64)
                    w("up", m + 1, 3)
                    V_.copy_predicated(half_t(zi, m), over(lvl[:, 0:P]), half_t(up, m)).then_inc(gg["xx"], 1)
                w("gram", 3, 3)
                V_.tensor_tensor(att[:], D[2][:], dt[:], ALU.mult).then_inc(gg["up"], 1)
                w("kt", 1, 2)
                for m in range(2):
                    h1 = bass.ds(at(m, p, 2), 1)
                    V_.tensor_tensor(tiles(kb, m), tiles(D[0], m), tsc[:, 3, :, h1].to_broadcast([P, NT, P]), ALU.mult)
                    last = V_.tensor_tensor(tiles(ks, m), tiles(D[0], m),
                                            tsc[:, 2, :, h1].to_broadcast([P, NT, P]), ALU.mult)
                last.then_inc(gg["ktv"], 1)
                w("kt", 2, 2)
                for m in range(2):
                    h1 = bass.ds(at(m, p, 2), 1)
                    last = V_.tensor_tensor(tiles(vs, m), tiles(D[1], m),
                                            tsc[:, 1, :, h1].to_broadcast([P, NT, P]), ALU.mult)
                last.then_inc(gg["ktv"], 1)
                for lv in range(1, 7):
                    for m in range(2):
                        dve.wait_ge(x_in, 64)
                        w(f"qq{lv}", m + 1, 2)
                        V_.copy_predicated(half_t(xi, m), over(lvl[:, lv * P:lv * P + P]),
                                           half_t(D[1], m)).then_inc(gg["xx"], 1)
                for t in range(NT - 1):
                    w("stp", t + 1, NT - 1)
                    for m in range(2):
                        if t == 0:
                            last = V_.tensor_copy(st[:, m], D[0][:, m, 0:P])
                        else:
                            last = V_.scalar_tensor_tensor(out=st[:, 2 * (t % 2) + m], in0=st[:, 2 * ((t - 1) % 2) + m],
                                                           scalar=eg[:, m, t * P + P - 1:t * P + P],
                                                           in1=D[0][:, m, 0:P], op0=ALU.mult, op1=ALU.add)
                    last.then_inc(gg["st"], 1)
                    w("st", t + 1, NT - 1)
                w("ort", 2, 2)
                L(V_.scalar_tensor_tensor(out=sq[:, 2:4], in0=D[2][:], scalar=vec[:, V["gdn_g"]:V["gdn_g"] + 1],
                                          in1=sq[:, 2:4], op0=ALU.mult, op1=ALU.mult))
                V_.tensor_tensor(go[:, bass.ds(at(0, p, 2), 2), :], sq[:, 2:4], gs[:], ALU.mult).then_inc(gg["of"], 1)
            split_lo(dve, Slab(G_GDN))
            loop(dve, GH // 2, body, chain, 3 * 3 + 4)

        def gdn_pe(pe):
            def body(p):
                w = lambda n, k, per: pe.wait_ge(gg[n], at(k, p, per))
                blk = lambda t_, b: t_[:, b // NT, (b % NT) * P:(b % NT) * P + P]
                heads = [range(m * NT, m * NT + NT) for m in range(2)]

                def along(src):
                    for m in range(2):
                        last = T_.matmul(D[2][:, m, :], ones[0:GH], src[0:GH, m, :], start=True, stop=True)
                    last.then_inc(gg["br"], 1)

                def gc_rows():
                    w("bb", 1, 1)
                    along(up)

                def squares(a):
                    w("sq", a + 1, 2)
                    if a:
                        w("rt", 1, 3)
                    else:
                        w("dif", 1, 1)
                    for m in range(2):
                        last = T_.matmul(D[2][:, m, :], ones, sq[:, 2 * a + m, :], start=True, stop=True)
                    last.then_inc(gg["ssq"], 1)
                slab = lambda j: Slab(G_GDN + j, p, PAIR)
                ada_at = lambda j: ada_pe(pe, Slab(ADA0 + j, p, ADA_P), 1)
                product(pe, slab(0), KC, 2, hH, hL)
                w("of", 1, 1)
                w("sel", 1, 1)
                along(att)
                product(pe, slab(1), KC, 2, hH, hL, {8: gc_rows})
                ada_at(0)
                product(pe, slab(2), KC, 2, hH, hL, {8: lambda: squares(0)})
                ada_at(1)
                product(pe, slab(3), KC, 2, hH, hL, {4: lambda: squares(1)})
                ada_at(2)
                pe.wait_ge(bank_free[slab(2).slot], slab(2).prior(1))
                w("kbq", 1, 2)
                for m in range(2):
                    for b in heads[m]:
                        last = T_.matmul(blk(D[1], b), blk(ks, b), blk(kb, b), start=True, stop=True)
                    last.then_inc(gg["gram"], 1)
                w("rt", 2, 3)
                for b in range(2 * NT):
                    last = T_.matmul(blk(D[2], b), blk(ks, b), blk(qs, b), start=True, stop=True)
                last.then_inc(gg["gram"], 1)
                pe.wait_ge(bank_free[slab(3).slot], slab(3).prior(1))
                for b in range(2 * NT):
                    last = T_.transpose(blk(D[0], b), blk(ks, b), ident)
                last.then_inc(gg["kt"], 1)
                w("up", 2, 3)
                w("qkv", 3, 3)
                for b in range(2 * NT):
                    last = T_.transpose(blk(D[1], b), blk(vs, b), ident)
                last.then_inc(gg["kt"], 1)
                w("up", 3, 3)
                for m in range(2):
                    w("xx", m + 1, 14)
                    for b in heads[m]:
                        last = T_.transpose(blk(D[2], b), blk(zi, b), ident)
                    last.then_inc(gg["xt"], 1)
                for lv in range(1, 7):
                    if lv == 1:
                        w("ktv", 1, 2)
                    for m in range(2):
                        w("zz", 2 * lv - 1 + m, 14)
                        for b in heads[m]:
                            last = T_.matmul(blk(D[0], b), blk(up, b), blk(xi, b), start=True, stop=True)
                        last.then_inc(gg["pp"], 1)
                    if lv >= 2:
                        ada_at(lv + 1)
                    if lv == 1:
                        w("ktv", 2, 2)
                    for m in range(2):
                        w("pb", 2 * lv - 1 + m, 12)
                        for b in heads[m]:
                            last = T_.matmul(blk(D[1], b), blk(zi, b), blk(sq, b), start=True, stop=True)
                        last.then_inc(gg[f"qq{lv}"], 1)
                    for m in range(2):
                        w("xx", 2 * lv + m + 1, 14)
                        for b in heads[m]:
                            last = T_.transpose(blk(D[2], b), blk(xi, b), ident)
                        last.then_inc(gg["xt"], 1)
                w("zz", 14, 14)
                for b in range(2 * NT):
                    last = T_.matmul(blk(D[0], b), blk(kb, b), blk(zi, b), start=True, stop=True)
                last.then_inc(gg["wtp"], 1)
                w("kbq", 2, 2)
                for t in range(NT):
                    if t == 1:
                        w("wt", 1, 1)
                    if t:
                        w("st", t, NT - 1)
                    for m in range(2):
                        b = m * NT + t
                        last = T_.matmul(D[1][:, m, 0:P], blk(zi, b), blk(vs, b), start=True, stop=(t == 0))
                        if t:
                            last = T_.matmul(D[1][:, m, 0:P], sq[:, 2 + m, t * P:t * P + P],
                                             st[:, 2 * ((t - 1) % 2) + m], start=False, stop=True)
                    last.then_inc(gg["vp"], 1)
                    if t == 0:
                        w("wt", 1, 1)
                    w("vn", t + 1, NT)
                    if t < NT - 1:
                        for m in range(2):
                            last = T_.matmul(D[0][:, m, 0:P], blk(ks, m * NT + t), vn[:, m], start=True, stop=True)
                        last.then_inc(gg["stp"], 1)
                    for m in range(2):
                        b = m * NT + t
                        if t:
                            T_.matmul(blk(D[2], b), st[:, 2 * ((t - 1) % 2) + m], blk(qd, b), start=True, stop=False)
                        last = T_.matmul(blk(D[2], b), vn[:, m], blk(att, b), start=(t == 0), stop=True)
                last.then_inc(gg["op"], 1)
                w("osq", 1, 1)
                for m in range(2):
                    last = T_.matmul(D[0][:, m, :], ones, sq[:, m, :], start=True, stop=True)
                last.then_inc(gg["oss"], 1)
            loop(pe, GH // 2, body)

        def linear_pe(pe, base, n, kc, nt, H, L, ada_base=None):
            per = 2 if ada_base is None else 4
            def body(i):
                for j in range(per):
                    product(pe, Slab(base + j, i, per), kc, nt, H, L)
                    if per == 4 and j % 2:
                        ada_pe(pe, Slab(ada_base + j // 2, i, 2), 2)
            loop(pe, n // per, body)

        def ffn_pe(pe, base, f, ada_base=None):
            for part, (ng, nd, kc, nt, off) in enumerate(((N_GUA, N_DNA, FA, 1, 0), (N_GUB, N_DNB, FB, 2, FA // 2))):
                a0 = ada_base if part == 0 else None
                linear_pe(pe, base, ng, KC, 2, hH, hL, a0)
                pe.wait_ge(aL_ready, 11 * f + off + ng // 2)
                linear_pe(pe, base + ng, nd, kc, nt, aH, aL)
                base += ng + nd

        def ffn_act(act, base, f):
            for ng, nd in ((N_GUA, N_DNA), (N_GUB, N_DNB)):
                def body(i):
                    s = Slab(base, i, 2)
                    split_hi(act, s.next())
                    act.wait_ge(slab_done, s.plus(1))
                    S_.activation(sg[:], D[s.slot][:], ACT.Silu).then_inc(bank_free[s.slot], 1)
                    u = s.next()
                    split_hi(act, u.next())
                    act.wait_ge(bank_free[u.slot], u.prior(1))
                    S_.activation(aH[:, bass.ds(at(0, i, 2), 2), :], af[:], ACT.Copy).then_inc(aH_ready, 1)
                loop(act, ng // 2, body)
                add_act(act, base + ng, nd)
                base += ng + nd

        def ffn_dve(dve, base, f, gate):
            for part, (ng, nd, nt) in enumerate(((N_GUA, N_DNA, 1), (N_GUB, N_DNB, 2))):
                def body(i):
                    s = Slab(base, i, 2)
                    u = s.next()
                    split_lo(dve, u)
                    split_lo(dve, u.next())
                    dve.wait_ge(slab_done, u.plus(1))
                    dve.wait_ge(bank_free[s.slot], s.prior(1))
                    V_.tensor_tensor(af[:], sg[:], D[u.slot][:], ALU.mult).then_inc(bank_free[u.slot], 1)
                    dve.wait_ge(aH_ready, at(11 * f + part * FA // 2 + 1, i, 1))
                    two = bass.ds(at(0, i, 2), 2)
                    V_.tensor_tensor(aL[:, two, :], af[:], aH[:, two, :], ALU.subtract).then_inc(aL_ready, 1)
                loop(dve, ng // 2, body)
                add_dve(dve, base + ng, nd, nt, gate)
                base += ng + nd

        ms = {n: sem("m_" + n) for n in ("ang", "trig", "sq", "ss", "rs", "cn", "cH", "cL", "ksw", "kr", "sw", "qr", "sc",
                                         "mx", "ex", "pn", "tr", "pt", "pv")}
        MS = (128 + 64) ** -0.5
        MAGIC = 12582912.0
        PI = float(np.float32(np.pi)) - 2.4e-7
        C1, C2 = 6.28125, 0.0019350051879882812
        C3 = 2 * np.pi - C1 - C2
        csq = (qn[:, 0], qn[:, 1], kn[:, 0], kn[:, 1], pT[:, 0])

        def angles_dve(dve, chain):
            L = chain.link
            dve.wait_ge(tab_in, 32)
            L(V_.tensor_copy(qr0[:], posi[:]))
            L(V_.tensor_scalar(qr0[:], qr0[:], vec[:, V["freq"]:V["freq"] + 1], None, ALU.mult))
            for dst, turn in ((msin, 0.0), (mcos, 0.25)):
                L(V_.tensor_scalar(qr[:], qr0[:], float(0.5 / np.pi), turn, ALU.mult, ALU.add))
                L(V_.tensor_scalar(qr[:], qr[:], MAGIC, None, ALU.add))
                L(V_.tensor_scalar(qr[:], qr[:], -MAGIC, None, ALU.add))
                L(V_.scalar_tensor_tensor(out=dst[:], in0=qr[:], scalar=-C1, in1=qr0[:], op0=ALU.mult, op1=ALU.add))
                L(V_.scalar_tensor_tensor(out=dst[:], in0=qr[:], scalar=-C2, in1=dst[:], op0=ALU.mult, op1=ALU.add))
                L(V_.scalar_tensor_tensor(out=dst[:], in0=qr[:], scalar=-C3, in1=dst[:], op0=ALU.mult, op1=ALU.add))
                L(V_.tensor_scalar(dst[:], dst[:], 2 * np.pi * turn, PI, ALU.add, ALU.min))
                V_.tensor_scalar(dst[:], dst[:], -PI, None, ALU.max).then_inc(ms["ang"], 1)

        def mla_in_pe(pe):
            for j in range(N_MIN):
                product(pe, Slab(G_MIN + j), KC, 2, hH, hL)
            for c in range(5):
                pe.wait_ge(ms["sq"], c + 1)
                last = T_.matmul(D[2][:, c // 3, :], ones, csq[c], start=(c in (0, 3)), stop=(c in (2, 4)))
            last.then_inc(ms["ss"], 1)
            pe.wait_ge(tab_in, 32)
            T_.matmul(D[3][:, 0, :], swp[:, 0:P], craw[:, 5, :], start=True, stop=True).then_inc(ms["ksw"], 1)
            pe.wait_ge(ms["cL"], 5)

        def mla_in_act(act):
            for j in range(N_MIN):
                s = Slab(G_MIN + j)
                split_hi(act, s.next())
                act.wait_ge(slab_done, s.plus(1))
                S_.activation(craw[:, 2 * j:2 * j + 2], D[s.slot][:], ACT.Copy).then_inc(bank_free[s.slot], 1)
            for j in range(N_MIN):
                s = Slab(G_MIN + j)
                act.wait_ge(bank_free[s.slot], s.prior(1))
            for c in range(5):
                S_.activation(csq[c], craw[:, c, :], ACT.Square,
                              scale=(3 if c < 3 else 2) ** -0.5 * P ** -0.5).then_inc(ms["sq"], 1)
            act.wait_ge(ms["ss"], 1)
            S_.activation(pr[:], D[2][:], ACT.Ln, bias=eps).then_inc(ms["rs"], 1)
            act.wait_ge(ms["rs"], 1)
            S_.activation(pr[:], pr[:], ACT.Exp, scale=-0.5).then_inc(ms["rs"], 1)
            for c in range(5):
                act.wait_ge(ms["cn"], c + 1)
                S_.activation(cH[:, c, :], craw[:, c, :], ACT.Copy).then_inc(ms["cH"], 1)
            act.wait_ge(ms["ang"], 2)
            S_.activation(mcos[:], mcos[:], ACT.Sin).then_inc(ms["trig"], 1)
            S_.activation(msin[:], msin[:], ACT.Sin, scale=vec[:, V["freq"] + 1:V["freq"] + 2]).then_inc(ms["trig"], 1)

        def mla_in_dve(dve, chain):
            for j in range(N_MIN):
                split_lo(dve, Slab(G_MIN + j).next())
            angles_dve(dve, chain)
            dve.wait_ge(ms["rs"], 2)
            gain = [vec[:, V["q_g"] + c:V["q_g"] + c + 1] for c in range(3)]
            gain += [vec[:, V["kv_g"] + c:V["kv_g"] + c + 1] for c in range(2)]
            for c in range(5):
                V_.scalar_tensor_tensor(out=craw[:, c, :], in0=craw[:, c, :], scalar=gain[c], in1=pr[:, c // 3, :],
                                        op0=ALU.mult, op1=ALU.mult).then_inc(ms["cn"], 1)
            for c in range(5):
                dve.wait_ge(ms["cH"], c + 1)
                V_.tensor_tensor(cL[:, c, :], craw[:, c, :], cH[:, c, :], ALU.subtract).then_inc(ms["cL"], 1)
            dve.wait_ge(ms["trig"], 2)
            dve.wait_ge(ms["ksw"], 1)
            chain.link(V_.tensor_tensor(krp[:], craw[:, 5, :], mcos[:], ALU.mult))
            chain.link(V_.tensor_tensor(qr0[:], D[3][:, 0, :], msin[:], ALU.mult))
            V_.tensor_tensor(krp[:], krp[:], qr0[:], ALU.add).then_inc(ms["kr"], 1)

        U = 2 * NT
        mxs, sums = small[:, 8:8 + U], small[:, 16:16 + U]

        def mla_pe(pe, hb):
            def body(p):
                w = lambda n, k, per: pe.wait_ge(ms[n], at(k, p, per))
                s = Slab(G_MLA, p, PAIR)
                product(pe, s, 3, 2, cH[:, 0:3], cL[:, 0:3])
                product(pe, s.next(1), 3, 1, cH[:, 0:3], cL[:, 0:3])
                product(pe, s.next(2), 2, 2, cH[:, 3:5], cL[:, 3:5])
                pe.wait_ge(bank_free[s.next(1).slot], s.next(1).prior(1))
                T_.matmul(D[2][:, 0, :], swp[:, 0:P], qr0[:], start=True, stop=True).then_inc(ms["sw"], 1)
                product_t(pe, s.next(3), 2, cH[:, 3:5], cL[:, 3:5])
                for k in (2, 3):
                    pe.wait_ge(bank_free[s.next(k).slot], s.next(k).prior(1))
                pe.wait_ge(ms["kr"], 1)
                w("qr", 1, 1)
                for u in range(U + 2):
                    if u < U:
                        m, b = divmod(u, NT)
                        n = (b + 1) * P
                        if u >= 2:
                            w("ex", u - 1, U)
                        o = D[2][:, u % 2, 0:n]
                        T_.matmul(o, qn[:, m, b * P:b * P + P], kn[:, m, 0:n], start=True, stop=False)
                        T_.matmul(o, qr[64 * m:64 * m + 64, b * P:b * P + P], krp[64 * m:64 * m + 64, 0:n],
                                  start=False, stop=True).then_inc(ms["sc"], 1)
                    if 1 <= u <= U:
                        v = u - 1
                        w("pn", v + 1, U)
                        if v >= 2:
                            w("pt", v - 1, U)
                        for j in range(v % NT + 1):
                            last = T_.transpose(D[3][:, v % 2, j * P:j * P + P], pr[:, v % 2, j * P:j * P + P], ident)
                        last.then_inc(ms["tr"], 1)
                    if u >= 2:
                        v = u - 2
                        m, b = divmod(v, NT)
                        w("pt", v + 1, U)
                        for j in range(b + 1):
                            last = T_.matmul(D[0][:, m, b * P:b * P + P], vt[:, j, m * P:m * P + P],
                                             pT[:, v % 2, j * P:j * P + P], start=(j == 0), stop=(j == b))
                        last.then_inc(ms["pv"], 1)
                pe.wait_ge(h_ready, at(KC * hb + 2, p, 2))
            loop(pe, GH // 2, body)

        def mla_act(act):
            def body(p):
                w = lambda n, k, per: act.wait_ge(ms[n], at(k, p, per))
                for k in range(PAIR):
                    s = Slab(G_MLA + k, p, PAIR)
                    split_hi(act, s.next())
                    if k == 2:
                        continue
                    act.wait_ge(slab_done, s.plus(1))
                    if k == 0:
                        last = S_.activation(qn[:], D[s.slot][:], ACT.Copy)
                    elif k == 1:
                        last = S_.activation(qr0[:], D[s.slot][:, 0, :], ACT.Copy)
                    else:
                        last = S_.activation(vt[:].rearrange("p t n -> p (t n)"),
                                             D[s.slot].rearrange("p a n -> p (a n)"), ACT.Copy)
                    last.then_inc(bank_free[s.slot], 1)
                for u in range(U + 1):
                    if u < U:
                        n = (u % NT + 1) * P
                        w("mx", u + 1, U)
                        if u >= 2:
                            w("tr", u - 1, U)
                        S_.activation(pr[:, u % 2, 0:n], D[2][:, u % 2, 0:n], ACT.Exp, bias=mxs[:, u:u + 1], scale=MS,
                                      accum_out=sums[:, u:u + 1]).then_inc(ms["ex"], 1)
                    if u >= 1:
                        v = u - 1
                        n = (v % NT + 1) * P
                        w("tr", v + 1, U)
                        if v >= 2:
                            w("pv", v - 1, U)
                        S_.activation(pT[:, v % 2, 0:n], D[3][:, v % 2, 0:n], ACT.Copy).then_inc(ms["pt"], 1)
                w("pv", U, U)
                S_.activation(hH[:, bass.ds(at(0, p, 2), 2), :], D[0][:], ACT.Copy).then_inc(hh_ready, 2)
            loop(act, GH // 2, body)

        def mla_dve(dve, chain, hb):
            def body(p):
                L = chain.link
                w = lambda n, k, per: dve.wait_ge(ms[n], at(k, p, per))
                for k in range(PAIR):
                    s = Slab(G_MLA + k, p, PAIR)
                    split_lo(dve, s.next())
                    if k == 2:
                        dve.wait_ge(slab_done, s.plus(1))
                        V_.tensor_copy(kn[:], D[s.slot][:]).then_inc(bank_free[s.slot], 1)
                w("sw", 1, 1)
                V_.tensor_tensor(qr[:], qr0[:], mcos[:], ALU.mult)
                L(V_.tensor_tensor(craw[:, 5, :], D[2][:, 0, :], msin[:], ALU.mult))
                V_.tensor_tensor(qr[:], qr[:], craw[:, 5, :], ALU.add).then_inc(ms["qr"], 1)
                for u in range(U + 1):
                    if u < U:
                        b = u % NT
                        w("sc", u + 1, U)
                        dg = D[2][:, u % 2, b * P:b * P + P]
                        L(V_.tensor_tensor(dg, dg, caus, ALU.add))
                        L(V_.reduce_max(mxs[:, u:u + 1], D[2][:, u % 2, 0:(b + 1) * P], AX.X))
                        V_.tensor_scalar(mxs[:, u:u + 1], mxs[:, u:u + 1], -MS, None, ALU.mult).then_inc(ms["mx"], 1)
                    if u >= 1:
                        v = u - 1
                        n = (v % NT + 1) * P
                        w("ex", v + 1, U)
                        L(V_.reciprocal(sums[:, v:v + 1], sums[:, v:v + 1]))
                        V_.tensor_scalar(pr[:, v % 2, 0:n], pr[:, v % 2, 0:n], sums[:, v:v + 1], None,
                                         ALU.mult).then_inc(ms["pn"], 1)
                dve.wait_ge(hh_ready, at(KC * hb + 2, p, 2))
                two = bass.ds(at(0, p, 2), 2)
                V_.tensor_tensor(hL[:, two, :], D[0][:], hH[:, two, :], ALU.subtract).then_inc(h_ready, 2)
            loop(dve, GH // 2, body, chain, 1 + 3 * U)

        rs_ = {n: sem("r_" + n) for n in ("sw", "rot", "kt", "sc", "a", "ds", "st", "y", "yc", "mu", "c", "sq", "var",
                                          "rs", "o", "H", "L")}
        HS = 3
        b_col = lambda o, i=None, step=0: vec[:, bass.ds(at(V["b_in"] + o, i, step), 1)]
        pairs = lambda ap: ap.unsqueeze(1).to_broadcast([P, 2, T])

        def rope_dve(chain, dst, raw_, cos_, sin_):
            V_.tensor_tensor(dst[:], raw_[:], pairs(cos_), ALU.mult)
            chain.link(V_.tensor_tensor(tm2[:], D[2][:], pairs(sin_), ALU.mult))
            return V_.tensor_tensor(dst[:], dst[:], tm2[:], ALU.add)

        def ret_pe(pe):
            def body(i):
                for m in range(2):
                    w = lambda n, k=1, per=1: pe.wait_ge(rs_[n], at(m * per + k, i, 2 * per))
                    s = Slab(G_RET + HS * m, i, 2 * HS)
                    product(pe, s, KC, 2, hH, hL)
                    pe.wait_ge(bank_free[s.slot], s.prior(1))
                    for e in range(2):
                        last = T_.matmul(D[2][:, e, :], swp[:, P:2 * P], qk[:, e, :], start=True, stop=True)
                    last.then_inc(rs_["sw"], 1)
                    product_t(pe, s.next(1), KC, hH, hL)
                    w("rot")
                    for t in range(NT):
                        c = slice(t * P, t * P + P)
                        last = T_.transpose(D[3][:, 0, c], kq[:, 1, c], ident)
                    last.then_inc(rs_["kt"], 1)
                    for t in range(NT):
                        c = slice(t * P, t * P + P)
                        last = T_.matmul(D[3][:, 1, c], kq[:, 1, c], kq[:, 0, c], start=True, stop=True)
                    last.then_inc(rs_["sc"], 1)
                    product(pe, s.next(2), KC, 2, hH, hL)
                    pe.wait_ge(bank_free[s.next(1).slot], s.next(1).prior(1))
                    w("a")
                    for t in range(NT):
                        c = slice(t * P, t * P + P)
                        if t < NT - 1:
                            if t:
                                w("st", t, NT - 1)
                            T_.matmul(D[3][:, 0, 0:2 * P], ka[:, 0, c], rvt[:, t, :], start=True,
                                      stop=True).then_inc(rs_["ds"], 1)
                        elif t:
                            w("st", t, NT - 1)
                        for e in range(2):
                            o = D[2][:, e, c]
                            if t:
                                T_.matmul(o, rst[:, (t - 1) % 2, e * P:e * P + P], qde[:, c], start=True, stop=False)
                            last = T_.matmul(o, rvt[:, t, e * P:e * P + P], ka[:, 1, c], start=(t == 0), stop=True)
                    last.then_inc(rs_["y"], 1)
                    for a, b in (("yc", "mu"), ("sq", "var")):
                        w(a)
                        src = ry if a == "yc" else rsq
                        for e in range(2):
                            last = T_.matmul(D[3][:, 1, :], ones, src[:, e, :], start=(e == 0), stop=(e == 1))
                        last.then_inc(rs_[b], 1)
                    w("L")
            loop(pe, 2, body)

        def ret_act(act):
            def body(i):
                for m in range(2):
                    w = lambda n, k=1, per=1: act.wait_ge(rs_[n], at(m * per + k, i, 2 * per))
                    s = Slab(G_RET + HS * m, i, 2 * HS)
                    split_hi(act, s.next())
                    act.wait_ge(slab_done, s.plus(1))
                    for e in range(2):
                        last = S_.activation(qk[:, e, :], D[s.slot][:, e, :], ACT.Identity, bias=b_col(4 * m + e, i, 8))
                    last.then_inc(bank_free[s.slot], 1)
                    split_hi(act, s.next(2))
                    split_hi(act, s.next(3))
                    g = s.next(2)
                    act.wait_ge(slab_done, g.plus(1))
                    for e in range(2):
                        last = S_.activation(rg[:, e, :], D[g.slot][:, e, :], ACT.Silu, bias=b_col(4 * m + 2 + e, i, 8))
                    last.then_inc(bank_free[g.slot], 1)
                    w("y")
                    S_.activation(ry[:], D[2][:], ACT.Copy).then_inc(rs_["yc"], 1)
                    w("c")
                    S_.activation(rsq[:], ry[:], ACT.Square, scale=1 / 16).then_inc(rs_["sq"], 1)
                    w("var")
                    S_.activation(tm2[:, 0, :], D[3][:, 1, :], ACT.Ln, bias=eps).then_inc(rs_["rs"], 1)
                    w("rs", 1, 2)
                    S_.activation(tm2[:, 0, :], tm2[:, 0, :], ACT.Exp, scale=-0.5).then_inc(rs_["rs"], 1)
                    w("o")
                    S_.activation(rH[:, bass.ds(at(2 * m, i, 4), 2), :], ry[:], ACT.Copy).then_inc(rs_["H"], 1)
            loop(act, 2, body)

        def ret_dve(dve, chain):
            def body(i):
                L = chain.link
                for m in range(2):
                    w = lambda n, k=1, per=1: dve.wait_ge(rs_[n], at(m * per + k, i, 2 * per))
                    s = Slab(G_RET + HS * m, i, 2 * HS)
                    head = lambda ap: ap.rearrange("p (h n) -> p h n", n=P)[:, bass.ds(at(m, i, 2), 1), :]
                    split_lo(dve, s.next())
                    w("sw")
                    dve.wait_ge(bank_free[s.slot], s.prior(1))
                    rope_dve(chain, kq, qk, rcos, rsin).then_inc(rs_["rot"], 1)
                    w("rot")
                    V_.tensor_tensor(qde[:].rearrange("p (t n) -> p t n", t=NT),
                                     kq[:, 0, :].rearrange("p (t n) -> p t n", t=NT),
                                     head(qdec).to_broadcast([P, NT, P]), ALU.mult)
                    split_lo(dve, s.next(2))
                    v = s.next(1)
                    dve.wait_ge(slab_done, v.plus(1))
                    vbh = vb[:, bass.ds(at(2 * P * m, i, 4 * P), 2 * P)].unsqueeze(1).to_broadcast([P, NT, 2 * P])
                    V_.tensor_tensor(rvt[:], D[v.slot].rearrange("p a (b n) -> p (a b) n", b=2), vbh,
                                     ALU.add).then_inc(bank_free[v.slot], 1)
                    split_lo(dve, s.next(3))
                    w("kt")
                    w("sc")
                    V_.tensor_scalar(ka[:, 0, :], D[3][:, 0, :], vec[:, bass.ds(at(V["kdec"] + m, i, 2), 1)], None,
                                     ALU.mult)
                    V_.tensor_tensor(ka[:, 1, :].rearrange("p (t n) -> p t n", t=NT),
                                     D[3][:, 1, :].rearrange("p (t n) -> p t n", t=NT),
                                     head(intra).to_broadcast([P, NT, P]), ALU.mult).then_inc(rs_["a"], 1)
                    for t in range(NT - 1):
                        w("ds", t + 1, NT - 1)
                        if t == 0:
                            V_.tensor_copy(rst[:, 0, :], D[3][:, 0, 0:2 * P]).then_inc(rs_["st"], 1)
                        else:
                            V_.scalar_tensor_tensor(out=rst[:, t % 2, :], in0=rst[:, (t - 1) % 2, :],
                                                    scalar=vec[:, bass.ds(at(V["cdec"] + m, i, 2), 1)],
                                                    in1=D[3][:, 0, 0:2 * P], op0=ALU.mult,
                                                    op1=ALU.add).then_inc(rs_["st"], 1)
                        w("st", t + 1, NT - 1)
                    w("mu")
                    V_.scalar_tensor_tensor(out=ry[:], in0=D[3][:, 1:2, :].to_broadcast([P, 2, T]), scalar=-1 / 256,
                                            in1=ry[:], op0=ALU.mult, op1=ALU.add).then_inc(rs_["c"], 1)
                    w("rs", 2, 2)
                    for e in range(2):
                        last = V_.scalar_tensor_tensor(out=rsq[:, e, :], in0=ry[:, e, :],
                                                       scalar=vec[:, bass.ds(at(V["ret_g"] + 2 * m + e, i, 4), 1)],
                                                       in1=tm2[:, 0, :], op0=ALU.mult, op1=ALU.mult)
                    L(last)
                    V_.tensor_tensor(ry[:], rsq[:], rg[:], ALU.mult).then_inc(rs_["o"], 1)
                    w("H")
                    two = bass.ds(at(2 * m, i, 4), 2)
                    V_.tensor_tensor(rL[:, two, :], ry[:], rH[:, two, :], ALU.subtract).then_inc(rs_["L"], 1)
            loop(dve, 2, body, chain, 4)

        def merge_pe(pe, base, H, L):
            def body(i):
                product(pe, Slab(base, i, 2), KC, 2, hH, hL)
                product(pe, Slab(base + 1, i, 2), KC, 2, H, L)
            loop(pe, N_OUT, body)

        def merge_act(act, base, bias0):
            def body(i):
                s = Slab(base, i, 2)
                u = s.next()
                split_hi(act, u)
                act.wait_ge(slab_done, s.plus(1))
                for m in range(2):
                    last = S_.activation(qk[:, m, :], D[s.slot][:, m, :], ACT.Sigmoid, bias=b_col(bias0 + m, i, 2))
                last.then_inc(bank_free[s.slot], 1)
                split_hi(act, u.next())
                act.wait_ge(bank_free[u.slot], u.prior(1))
            loop(act, N_OUT, body)

        def merge_dve(dve, chain, base, add):
            def body(i):
                s = Slab(base, i, 2)
                u = s.next()
                split_lo(dve, u)
                split_lo(dve, u.next())
                dve.wait_ge(slab_done, u.plus(1))
                dve.wait_ge(bank_free[s.slot], s.prior(1))
                two = mg[:, bass.ds(at(0, i, 2), 2), :]
                if add:
                    chain.link(V_.tensor_tensor(tm2[:], qk[:], D[u.slot][:], ALU.mult))
                    V_.tensor_tensor(two, two, tm2[:], ALU.add).then_inc(bank_free[u.slot], 1)
                else:
                    V_.tensor_tensor(two, qk[:], D[u.slot][:], ALU.mult).then_inc(bank_free[u.slot], 1)
            loop(dve, N_OUT, body, chain, int(add))

        as_ = {n: sem("a_" + n) for n in ("sw", "kk", "stage", "qr", "sc", "mx", "ex", "pn", "tr", "pt", "pv", "H", "L")}
        kks, kst, av, vst, sco, prb, ptb = rg, qde, rvt, rst[:, 0, :].rearrange("p (t n) -> p t n", t=NT), ry, rsq, ka
        four = lambda t_: t_[:].rearrange("p a (b n) -> p (a b) n", b=2)
        AS = 64 ** -0.5
        AU = 4
        amx, asum, aes = small[:, 24:28], small[:, 28:32], small[:, 32:36]

        def kv_pe(pe):
            s = Slab(G_KV)
            product(pe, s, KC, 2, hH, hL)
            pe.wait_ge(bank_free[s.slot], s.prior(1))
            for e in range(2):
                last = T_.matmul(D[2][:, e, :], swp[:, 0:P], qk[:, e, :], start=True, stop=True)
            last.then_inc(as_["sw"], 1)
            product_t(pe, s.next(), KC, hH, hL, P)

        def kv_act(act):
            s = Slab(G_KV)
            split_hi(act, s.next())
            act.wait_ge(slab_done, s.plus(1))
            for e in range(2):
                last = S_.activation(qk[:, e, :], D[s.slot][:, e, :], ACT.Identity, bias=b_col(24 + e))
            last.then_inc(bank_free[s.slot], 1)
            split_hi(act, s.next(2))

        def kv_dve(dve, chain):
            s = Slab(G_KV)
            split_lo(dve, s.next())
            dve.wait_ge(as_["sw"], 1)
            rope_dve(chain, kks, qk, acos, asin).then_inc(as_["kk"], 1)
            split_lo(dve, s.next(2))
            dve.wait_ge(slab_done, s.plus(2))
            V_.tensor_tensor(av[:, :, 0:P], D[s.next().slot].rearrange("p a (b n) -> p (a b) n", b=2)[:, :, 0:P],
                             vb[:, 8 * P:9 * P].unsqueeze(1).to_broadcast([P, NT, P]),
                             ALU.add).then_inc(bank_free[s.next().slot], 1)
            dve.wait_ge(as_["kk"], 1)
            dve.wait_ge(bank_free[s.next().slot], s.next().prior(1))

        def swa_pe(pe):
            def body(i):
                pe.wait_ge(as_["stage"], at(1, i, 1))
                for j in range(2):
                    w = lambda n, k=1, per=1: pe.wait_ge(as_[n], at(j * per + k, i, 2 * per))
                    s = Slab(G_AQ + j, i, 2)
                    product(pe, s, KC, 2, hH, hL)
                    pe.wait_ge(bank_free[s.slot], s.prior(1))
                    for e in range(2):
                        last = T_.matmul(D[2][:, e, :], swp[:, 0:P], qk[:, e, :], start=True, stop=True)
                    last.then_inc(as_["sw"], 1)
                    w("qr")
                    for v in range(AU + 1):
                        if v < AU:
                            m, hh = divmod(v, 2)
                            half = slice(64 * hh, 64 * hh + 64)
                            if v:
                                w("mx", v, AU)
                            for b in range(NT):
                                k0 = max(b - 1, 0) * P
                                last = T_.matmul(four(D[3])[:, b, :], kq[half, m, b * P:b * P + P],
                                                 kst[half, k0:k0 + 2 * P], start=True, stop=True)
                            last.then_inc(as_["sc"], 1)
                        if v:
                            u = v - 1
                            m, hh = divmod(u, 2)
                            w("pn", u + 1, AU)
                            for b in range(NT):
                                for k in range(2):
                                    last = T_.transpose(four(D[2])[:, b, k * P:k * P + P],
                                                        four(prb)[:, b, k * P:k * P + P], ident)
                            last.then_inc(as_["tr"], 1)
                            w("pt", u + 1, AU)
                            for b in range(NT):
                                k0 = max(b - 1, 0)
                                for k in range(2 if b else 1):
                                    last = T_.matmul(D[s.slot][64 * hh:64 * hh + 64, m, b * P:b * P + P],
                                                     vst[:, k0 + k, 0:64], four(ptb)[:, b, k * P:k * P + P],
                                                     start=(k == 0), stop=(k == (1 if b else 0)))
                            last.then_inc(as_["pv"], 1)
                    w("L")
            loop(pe, 2, body)

        def swa_act(act):
            def body(i):
                for j in range(2):
                    w = lambda n, k=1, per=1: act.wait_ge(as_[n], at(j * per + k, i, 2 * per))
                    s = Slab(G_AQ + j, i, 2)
                    split_hi(act, s.next())
                    act.wait_ge(slab_done, s.plus(1))
                    for e in range(2):
                        last = S_.activation(qk[:, e, :], D[s.slot][:, e, :], ACT.Identity,
                                             bias=b_col(26 + 2 * j + e, i, 4))
                    last.then_inc(bank_free[s.slot], 1)
                    for v in range(AU):
                        sink = vec[:, bass.ds(at(V["sink"] + 4 * j + v, i, 8), 1)]
                        w("mx", v + 1, AU)
                        if v:
                            w("tr", v, AU)
                        for b in range(NT):
                            S_.activation(four(prb)[:, b, :], four(sco)[:, b, :], ACT.Exp, bias=amx[:, b:b + 1],
                                          accum_out=asum[:, b:b + 1])
                        S_.activation(aes, amx, ACT.Exp, bias=sink).then_inc(as_["ex"], 1)
                        w("tr", v + 1, AU)
                        if v:
                            w("pv", v, AU)
                        S_.activation(ptb[:], D[2][:], ACT.Copy).then_inc(as_["pt"], 1)
                    w("pv", AU, AU)
                    S_.activation(rH[:, bass.ds(at(2 * j, i, 4), 2), :], D[s.slot][:], ACT.Copy).then_inc(as_["H"], 1)
            loop(act, 2, body)

        def swa_dve(dve, chain):
            def body(i):
                L = chain.link
                V_.tensor_copy(kst[:], kks[:, bass.ds(i, 1), :].rearrange("p a n -> p (a n)"))
                V_.tensor_scalar(vst, av[:, :, bass.ds(at(0, i, 64), 64)], 1.0, None,
                                 ALU.mult).then_inc(as_["stage"], 1)
                for j in range(2):
                    w = lambda n, k=1, per=1: dve.wait_ge(as_[n], at(j * per + k, i, 2 * per))
                    s = Slab(G_AQ + j, i, 2)
                    split_lo(dve, s.next())
                    dve.wait_ge(bank_free[s.slot], s.prior(1))
                    dve.wait_ge(as_["sw"], at(j + 2, i, 2))
                    rope_dve(chain, kq, qk, acos, asin).then_inc(as_["qr"], 1)
                    w1 = win[:, 2 * P:4 * P]
                    for v in range(AU):
                        sink = vec[:, bass.ds(at(V["sink"] + 4 * j + v, i, 8), 1)]
                        w("sc", v + 1, AU)
                        sc4 = four(sco)
                        V_.scalar_tensor_tensor(out=sc4[:, 0, :], in0=four(D[3])[:, 0, :], scalar=AS,
                                                in1=win[:, 0:2 * P], op0=ALU.mult, op1=ALU.add)
                        L(V_.scalar_tensor_tensor(out=sc4[:, 1:4, :], in0=four(D[3])[:, 1:4, :], scalar=AS,
                                                  in1=w1.unsqueeze(1).to_broadcast([P, 3, 2 * P]), op0=ALU.mult,
                                                  op1=ALU.add))
                        L(V_.reduce_max(amx, sc4, AX.X))
                        V_.tensor_scalar(amx, amx, sink, -1.0, ALU.max, ALU.mult).then_inc(as_["mx"], 1)
                        w("ex", v + 1, AU)
                        L(V_.tensor_tensor(asum, asum, aes, ALU.add))
                        L(V_.reciprocal(asum, asum))
                        V_.tensor_tensor(four(prb), four(prb), asum.unsqueeze(2).to_broadcast([P, NT, 2 * P]),
                                         ALU.mult).then_inc(as_["pn"], 1)
                    w("H")
                    two = bass.ds(at(2 * j, i, 4), 2)
                    V_.tensor_tensor(rL[:, two, :], D[s.slot][:], rH[:, two, :], ALU.subtract).then_inc(as_["L"], 1)
            loop(dve, 2, body, chain, 2 * (1 + 4 * AU))

        block = ctx.enter_context(nc.Block())
        gate_col = lambda layer, part: lambda c: mod[:, bass.ds(c + MD(layer, part), 1)]
        col = lambda t_, o: lambda c: t_[:, o + c:o + c + 1]
        zero = lambda c: vec[:, V["zero"]:V["zero"] + 1]

        @block.sync
        def _(sp):
            sp.dma_start(vec[:], vecs[:, :]).then_inc(x_in, 16)
            load_ada(sp, Slab(0))
            sp.dma_start(x[:], xin[:, :, :]).then_inc(x_in, 16)
            load_ada(sp, Slab(1))
            sp.dma_start(cst[:], consts[:, :]).then_inc(x_in, 16)
            sp.dma_start(lvl[:], masks[:, :]).then_inc(x_in, 16)
            load_slab(sp, Slab(0))
            sp.dma_start(posi[:], pos[0:1, :].to_broadcast([P, T])).then_inc(tab_in, 16)
            sp.dma_start(swp[:], rope[:, 0:2 * P]).then_inc(tab_in, 16)
            for a in range(2, ADA0):
                load_ada(sp, Slab(a))
            load_slab(sp, Slab(1))

            def both(g, a, n, per, ada_per):
                def body(i):
                    k = 0
                    for j in range(per):
                        load_slab(sp, Slab(g + j, i, per))
                        for _ in range(ada_per[j]):
                            load_ada(sp, Slab(a + k, i, sum(ada_per)))
                            k += 1
                loop(sp, n, body)

            def alone(g, n):
                def body(i):
                    for j in range(2):
                        load_slab(sp, Slab(g + j, i, 2))
                loop(sp, n // 2, body)
                if n % 2:
                    load_slab(sp, Slab(g + n - 1))
            both(2, ADA0, GH // 2, PAIR, (0, 1, 2, 5))
            alone(2 + N_GDN, N_OUT)
            ada1 = ADA0 + GH // 2 * ADA_P
            both(G_FFN0 + 1, ada1, (2 * ADA_L - ada1) // 2, 4, (0, 1, 0, 1))
            g = G_FFN0 + 1 + 2 * (2 * ADA_L - ada1)
            alone(g, G_RET + 1 - g)
            x_written(sp, G_RET)
            sp.dma_start(tab[:], rope[:, 2 * P:2 * P + TAB]).then_inc(tab_in, 16)
            sp.dma_start(vb[:], vbias[0:1, :].to_broadcast([P, 9 * P])).then_inc(tab_in, 16)
            alone(G_RET + 1, N_SLABS + 1 - (G_RET + 1))
            sp.wait_ge(xg_ready, 8 * KC)
            sp.dma_start(out[:, :, :], x[:]).then_inc(out_done, 16)
            sp.wait_ge(out_done, 16)

        @block.tensor
        def _(pe):
            pe.wait_ge(cact_ready, 1)
            for a in range(ADA0):
                ada_mm(pe, Slab(a))
            norm_pe(pe, 0, sq)
            pe.wait_ge(h_ready, KC)
            product(pe, Slab(G_AB), KC, 2, hH, hL)
            rows_pe(pe)
            gdn_pe(pe)
            pe.wait_ge(h_ready, 2 * KC)
            linear_pe(pe, G_GOUT, N_OUT, KC, 2, hH, hL)
            norm_pe(pe, 1, sg)
            pe.wait_ge(h_ready, 3 * KC)
            ffn_pe(pe, G_FFN0, 0, ADA0 + GH // 2 * ADA_P)
            norm_pe(pe, 2, nsq)
            pe.wait_ge(h_ready, 4 * KC)
            mla_in_pe(pe)
            mla_pe(pe, 4)
            linear_pe(pe, G_MOUT, N_OUT, KC, 2, hH, hL)
            norm_pe(pe, 3, sg)
            pe.wait_ge(h_ready, 6 * KC)
            ffn_pe(pe, G_FFN1, 1)
            norm_pe(pe, 4, sg)
            norm_pe(pe, 5, ry)
            pe.wait_ge(h_ready, 7 * KC)
            ret_pe(pe)
            merge_pe(pe, G_GR, rH, rL)
            kv_pe(pe)
            swa_pe(pe)
            merge_pe(pe, G_GA, rH, rL)
            pe.wait_ge(h_ready, 8 * KC)
            linear_pe(pe, G_ROUT, N_OUT, KC, 2, hH, hL)
            norm_pe(pe, 6, sg)
            pe.wait_ge(h_ready, 9 * KC)
            ffn_pe(pe, G_FFN2, 2)
            norm_pe(pe, 7, sg)

        @block.gpsimd
        def _(pool):
            chain = Chain(pool, pool_chain)
            pool.wait_ge(cact_ready, 1)
            ada_chunks(pool, chain)

        @block.scalar
        def _(act):
            act.wait_ge(x_in, 64)
            S_.activation(cact[:], vec[:, V["c"]:V["c"] + KC], ACT.Silu).then_inc(cact_ready, 1)
            split_hi(act, Slab(0))
            norm_act(act, 0, sq, kb[:, 0, :], sq[:, 2:4], col(mod, MD(0, 0)), 0)
            rows_act(act)
            gdn_act(act)
            act.wait_ge(gg["of"], GH // 2 + 1)
            to_h_act(act, go)
            add_act(act, G_GOUT, N_OUT)
            norm_act(act, 1, sg, nrs[:], af, col(mod, MD(0, 3)), G_FFN0)
            ffn_act(act, G_FFN0, 0)
            norm_act(act, 2, nsq, mrs[:], ntm, col(mod, MD(1, 0)), G_MIN)
            mla_in_act(act)
            mla_act(act)
            add_act(act, G_MOUT, N_OUT)
            norm_act(act, 3, sg, nrs[:], af, col(mod, MD(1, 3)), G_FFN1)
            ffn_act(act, G_FFN1, 1)
            norm_act(act, 4, sg, nrs[:], None, None, G_RET, to_h=False)
            norm_act(act, 5, ry, rst[:].rearrange("p a n -> p (a n)"), rsq, zero, x_normed(5))
            act.wait_ge(tab_in, 64)
            ret_act(act)
            merge_act(act, G_GR, 16)
            kv_act(act)
            swa_act(act)
            merge_act(act, G_GA, 34)
            to_h_act(act, mg)
            add_act(act, G_ROUT, N_OUT)
            norm_act(act, 6, sg, nrs[:], af, zero, G_FFN2)
            ffn_act(act, G_FFN2, 2)
            norm_act(act, 7, sg, nrs[:], None, None, N_SLABS, to_h=False)

        @block.vector
        def _(dve):
            chain = Chain(dve, dve_chain)
            dve.wait_ge(x_in, 64)
            split_lo(dve, Slab(0))
            mod_dve(dve, chain, 0, 2 * KC, ADA0)
            dve.wait_ge(mod_ready, 1)
            gain_cols(chain, 0, "mix_g", 0, 1)
            norm_dve(dve, 0, 0, kb[:, 0, :], sq[:, 2:4], col(gsc, 0), col(mod, MD(0, 0)), chain)
            rows_dve(dve, chain)
            gdn_dve(dve, chain)
            mod_dve(dve, chain, 2 * KC, 6 * KC, ADA0 + GH // 2 * ADA_P)
            dve.wait_ge(mod_ready, 2)
            gain_cols(chain, 1, "ffn_g", 0, 4)
            to_h_dve(dve, 1, go)
            add_dve(dve, G_GOUT, N_OUT, 2, gate_col(0, 2))
            norm_dve(dve, 1, 2, nrs[:], af, col(gsc, KC), col(mod, MD(0, 3)), chain)
            ffn_dve(dve, G_FFN0, 0, gate_col(0, 5))
            mod_dve(dve, chain, 6 * KC, 12 * KC, 2 * ADA_L)
            dve.wait_ge(mod_ready, 3)
            gain_cols(chain, 2, "mix_g", 1, 1)
            gain_cols(chain, 3, "ffn_g", 1, 4)
            norm_dve(dve, 2, 3, mrs[:], ntm, col(gsc, 2 * KC), col(mod, MD(1, 0)), chain)
            mla_in_dve(dve, chain)
            mla_dve(dve, chain, 4)
            add_dve(dve, G_MOUT, N_OUT, 2, gate_col(1, 2))
            norm_dve(dve, 3, 5, nrs[:], af, col(gsc, 3 * KC), col(mod, MD(1, 3)), chain)
            ffn_dve(dve, G_FFN1, 1, gate_col(1, 5))
            norm_x_dve(dve, 4, nrs[:], col(vec, V["fin_g"]), chain)
            norm_dve(dve, 5, 6, rst[:].rearrange("p a n -> p (a n)"), rsq, col(vec, V["ln1"]), zero, chain)
            dve.wait_ge(tab_in, 64)
            ret_dve(dve, chain)
            merge_dve(dve, chain, G_GR, False)
            kv_dve(dve, chain)
            swa_dve(dve, chain)
            merge_dve(dve, chain, G_GA, True)
            to_h_dve(dve, 7, mg)
            add_dve(dve, G_ROUT, N_OUT, 2, None)
            norm_dve(dve, 6, 8, nrs[:], af, col(vec, V["ln2"]), zero, chain)
            ffn_dve(dve, G_FFN2, 2, None)
            norm_x_dve(dve, 7, nrs[:], col(vec, V["lnf"]), chain)


def _slab(cols):
    k, n = cols.shape
    a = cols.reshape(k // P, P, n).transpose(1, 0, 2).reshape(P, -1)
    return np.pad(a, ((0, 0), (0, SLAB - a.shape[1])))


def _cols(w, n=2 * P):
    return [_slab(w[:, c:c + n]) for c in range(0, w.shape[1], n)]


def _ffn(wg, wu, wd):
    out = []
    for lo_, hi_ in ((0, FA), (FA, FA + FB)):
        g, u = (_cols(w[:, lo_ * P:hi_ * P]) for w in (wg, wu))
        for a, b in zip(g, u):
            out += [a, b]
        out += _cols(wd[lo_ * P:hi_ * P], P if lo_ == 0 else 2 * P)
    return out


def _slabs(i):
    w = i["gdn_w_in"][0]
    ab = np.zeros((DM, 2 * P), np.float32)
    ab[:, 0:GH] = w[:, 4096:4096 + GH]
    ab[:, P:P + GH] = w[:, 4096 + GH:4096 + 2 * GH]
    out = [_slab(ab)]
    for p in range(GH // 2):
        out += [_slab(w[:, j * DM + p * 256:j * DM + p * 256 + 256]) for j in range(4)]
    out += _cols(i["gdn_w_out"][0])
    out += _ffn(i["ffn_w_gate"][0], i["ffn_w_up"][0], i["ffn_w_down"][0])
    w = i["mla_w_in"][0]
    out += _cols(np.concatenate([w, w[:, 640:704]], 1))
    uq = i["mla_w_uq"][0].reshape(384, GH, 192)
    ukv = i["mla_w_ukv"][0].reshape(256, GH, 256)
    for p in range(0, GH, 2):
        out += [_slab(uq[:, p:p + 2, 0:128].reshape(384, 256)), _slab(uq[:, p:p + 2, 128:192].reshape(384, 128)),
                _slab(ukv[:, p:p + 2, 0:128].reshape(256, 256)), _slab(ukv[:, p:p + 2, 128:256].reshape(256, 256))]
    out += _cols(i["mla_w_out"][0])
    out += _ffn(i["ffn_w_gate"][1], i["ffn_w_up"][1], i["ffn_w_down"][1])
    w = i["w_in_2"][0]
    for h in range(4):
        qk = np.concatenate([w[:, h * P:h * P + P], w[:, 512 + h * P:512 + h * P + P]], 1)
        out += [_slab(qk), _slab(w[:, 1024 + 256 * h:1280 + 256 * h]), _slab(w[:, 2048 + 256 * h:2304 + 256 * h])]
    ga, ro = _cols(w[:, 4352:5376]), _cols(i["w_ret_out_2"][0])
    for a, b in zip(ga, ro):
        out += [a, b]
    k0, k1 = w[:, 4096:4160], w[:, 4160:4224]
    out += [_slab(np.concatenate([k0, k0, k1, k1], 1)), _slab(np.pad(w[:, 4224:4352], ((0, 0), (0, P))))]
    out += _cols(w[:, 3072:4096])
    gb, ao = _cols(w[:, 5376:6400]), _cols(i["w_attn_out_2"][0])
    for a, b in zip(gb, ao):
        out += [a, b]
    out += _cols(i["w_out_2"][0])
    out += _ffn(i["w_ffn_gate_2"][0], i["w_ffn_up_2"][0], i["w_ffn_down_2"][0])
    out += [np.zeros((P, SLAB), np.float32)]
    assert len(out) == N_SLABS + 1, (len(out), N_SLABS)
    return np.stack(out)


def _vectors(i):
    col = lambda a: np.ascontiguousarray(a).reshape(-1, P).T
    rep = lambda a: np.broadcast_to(a, (P, a.size))
    b = i["b_in_2"][0]
    bt = []
    for h in range(4):
        bt += [b[h * P:h * P + P], b[512 + h * P:512 + h * P + P], b[2048 + 256 * h:2304 + 256 * h]]
    bt += [b[4352:5376], b[4096:4160], b[4096:4160], b[4160:4224], b[4160:4224], b[3072:4096], b[5376:6400]]
    eight = lambda a: np.pad(a.reshape(-1, 1), ((0, P - GH), (0, 0)))
    j = np.arange(P)
    lg = np.log1p(-np.exp2(-5.0 - np.arange(4)))
    inv64 = 10000.0 ** (-np.arange(0, 64, 2, dtype=np.float32) / np.float32(64))
    parts = {
        "c": col(i["c"]), "ada_b": col(i["ada_b"]), "mix_g": col(i["norm_mix_g"]), "ffn_g": col(i["norm_ffn_g"]),
        "conv": i["gdn_conv_w"][0].reshape(24, P, 4).transpose(1, 0, 2).reshape(P, 96), "gdn_g": col(i["gdn_norm_g"]),
        "a_log": eight(i["gdn_a_log"][0]), "dt_b": eight(i["gdn_dt_bias"][0]), "q_g": col(i["mla_q_norm_g"]),
        "kv_g": col(i["mla_kv_norm_g"]), "fin_g": col(i["final_norm_g"]), "ln1": col(i["ln1_g_2"]),
        "b_in": col(np.concatenate(bt)), "ret_g": col(i["ret_norm_g_2"]), "ln2": col(i["ln2_g_2"]),
        "lnf": col(i["lnf_g_2"]), "sink": rep(i["attn_sinks_2"][0]), "zero": np.zeros((P, 1)),
        "kdec": np.exp(lg[None] * (P - 1.0 - j)[:, None]),
        "freq": np.stack([inv64[j % 32], np.where(j % 64 < 32, -1.0, 1.0)], 1), "eps": np.full((P, 1), EPS),
        "cdec": rep(np.exp(lg * P)),
    }
    out = []
    for n, c in V.items():
        a = parts[n]
        assert c == sum(o.shape[1] for o in out), n
        out.append(np.asarray(a, np.float32))
    return np.ascontiguousarray(np.concatenate(out, 1))


def _constants():
    j, i = np.arange(P)[:, None], np.arange(P)[None]
    return np.concatenate([np.eye(P), np.ones((P, P)), np.where(j <= i, 0, -1e30), np.where(i <= j, 0, -1e30)],
                          1).astype(np.float32)


def _levels():
    i, j = np.arange(P)[:, None], np.arange(P)[None]
    m = [(i // (2 * b) == j // (2 * b)) & (i % (2 * b) >= b) & (j % (2 * b) < b) for b in (1, 2, 4, 8, 16, 32, 64)]
    m[0] = m[0].T
    return np.concatenate(m, 1).astype(np.int32)


def _rope_tables():
    j = np.arange(P)
    perm = [np.eye(P)[(j // 64) * 64 + (j + 32) % 64], np.eye(P)[(j + 64) % P]]
    t = np.arange(T, dtype=np.float32)
    tabs = []
    for half in (64, 32):
        inv = (np.float32(10000.0) ** (-np.arange(half, dtype=np.float32) / np.float32(half))).astype(np.float32)
        ang = (t[None] * inv[j % half][:, None]).astype(np.float64)
        tabs += [np.cos(ang), np.sin(ang) * np.where(j % (2 * half) < half, -1.0, 1.0)[:, None]]
    lg = np.log1p(-np.exp2(-5.0 - np.arange(4)))
    rel = j[None] - j[:, None]
    intra = [np.where(rel >= 0, np.exp(g * np.maximum(rel, 0)), 0) * P ** -0.5 for g in lg]
    qdec = [np.broadcast_to(np.exp(g * (j + 1.0)) * P ** -0.5, (P, P)) for g in lg]
    cur = np.where(j[None] <= j[:, None], 0, -1e30)
    prev = np.where(j[None] > j[:, None], 0, -1e30)
    none = np.full((P, P), -1e30)
    win = [cur, none, prev, cur]
    return np.concatenate(perm + tabs + intra + qdec + win, 1).astype(np.float32)


def kernel(**inputs):
    import concourse.bacc as bacc
    from concourse.bass_utils import run_bass_kernel_spmd

    i = {k: np.asarray(v) for k, v in inputs.items()}
    b = i["b_in_2"][0]
    arrays = {
        "slabs": _slabs(i),
        "ada": np.stack([s for layer in range(2) for s in _cols(i["ada_w"][layer])]),
        "vecs": _vectors(i),
        "consts": _constants(),
        "masks": _levels(),
        "rope": _rope_tables(),
        "vbias": np.concatenate([b[1024:2048], b[4224:4352]]).reshape(1, -1),
        "pos": i["positions"].astype(np.int32).reshape(1, T),
        "xin": np.ascontiguousarray(i["x"][0].T.reshape(KC, P, T).transpose(1, 0, 2)),
    }
    nc = bacc.Bacc("TRN2", target_bir_lowering=False, num_devices=1)
    args = [nc.dram_tensor(f"in_{n}", a.shape, mybir.dt.from_np(a.dtype), kind="ExternalInput").ap()
            for n, a in arrays.items()]
    out = nc.dram_tensor("out", (P, KC, T), mybir.dt.float32, kind="ExternalOutput").ap()
    build(nc, *args, out)
    r = run_bass_kernel_spmd(nc, [{f"in_{n}": a for n, a in arrays.items()}], core_ids=[0])
    return r.results[0]["out"].transpose(1, 0, 2).reshape(DM, T).T.reshape(1, T, DM)
```

```python
import numpy as np
import concourse.bass as bass
from concourse import mybir
from contextlib import ExitStack

P = 128
DM, T, NT = 1024, 512, 4
KC = DM // P
SLAB = 2048
EPS = 1e-6
DFF = 2816
FA, FB = 16, 6
GH = 8
N_AB, N_GDN, N_OUT = 1, 16, 4
N_GUA, N_DNA, N_GUB, N_DNB = FA, KC, FB, KC // 2
N_FFN = N_GUA + N_DNA + N_GUB + N_DNB
N_MIN, N_MLA = 3, 16
N_RET, N_GR, N_KV, N_AQ, N_GA = 12, 8, 2, 4, 8
G_AB = 0
G_GDN = G_AB + N_AB
G_GOUT = G_GDN + N_GDN
G_FFN0 = G_GOUT + N_OUT
G_MIN = G_FFN0 + N_FFN
G_MLA = G_MIN + N_MIN
G_MOUT = G_MLA + N_MLA
G_FFN1 = G_MOUT + N_OUT
G_RET = G_FFN1 + N_FFN
G_GR = G_RET + N_RET
G_KV = G_GR + N_GR
G_AQ = G_KV + N_KV
G_GA = G_AQ + N_AQ
G_ROUT = G_GA + N_GA
G_FFN2 = G_ROUT + N_OUT
N_SLABS = G_FFN2 + N_FFN
ADA_L = 24
ADA0 = 8
ADA_V = 160
ADA_P = 8
V = {}
def _vec(name, n, at=[0]):
    V[name] = at[0]
    at[0] += n
for _n, _k in (("c", 8), ("ada_b", 96), ("mix_g", 16), ("ffn_g", 16), ("conv", 96), ("gdn_g", 1), ("a_log", 1),
               ("dt_b", 1), ("q_g", 3), ("kv_g", 2), ("fin_g", 8), ("ln1", 8), ("b_in", 42), ("ret_g", 8),
               ("ln2", 8), ("lnf", 8), ("sink", 16), ("zero", 1), ("kdec", 4), ("freq", 2), ("eps", 1), ("cdec", 4)):
    _vec(_n, _k)
NV = V["cdec"] + 4
C_ID, C_ONE, C_NEG, C_CAUS = 0, 128, 256, 384
NC_ = 512


class Chain:
    def __init__(self, eng, sem):
        self.eng, self.sem, self.base, self.at, self.i, self.per = eng, sem, 0, 0, None, 0

    def enter(self, i, per):
        self.i, self.per, self.at = i, per, 0

    def leave(self, n):
        assert self.at == self.per, (self.at, self.per)
        self.base, self.at, self.i = self.base + n * self.per, 0, None

    def link(self, ins):
        ins.then_inc(self.sem, 1)
        if self.i is None:
            self.base += 1
            self.eng.wait_ge(self.sem, self.base)
        else:
            self.at += 1
            self.eng.wait_ge(self.sem, self.i * self.per + (self.base + self.at))


class Slab:
    def __init__(self, b, i=None, step=0):
        self.b, self.i, self.step, self.slot = b, i, step, b % 2

    def plus(self, k):
        return self.b + k if self.i is None else self.i * self.step + (self.b + k)

    def prior(self, k=0, times=1):
        n = ((self.b - self.slot) // 2 + k) * times
        return n if self.i is None else self.i * (self.step // 2 * times) + n

    def next(self, k=1):
        return Slab(self.b + k, self.i, self.step)


def at(base, i=None, step=0):
    return base if i is None else i * step + base


def loop(eng, n, body, chain=None, per=0):
    with eng.Fori(0, n) as i:
        if chain:
            chain.enter(i, per)
        body(i)
    if chain:
        chain.leave(n)


def build(nc, slabs, ada, vecs, consts, masks, rope, vbias, pos, xin, out):
    fp32, f32r, i32 = mybir.dt.float32, mybir.dt.float32r, mybir.dt.int32
    ALU, ACT, AX = mybir.AluOpType, mybir.ActivationFunctionType, mybir.AxisListType
    V_, S_, T_ = nc.vector, nc.scalar, nc.tensor
    ctx = ExitStack()
    with ctx:
        def sb(name, shape, dt=fp32, scope=ctx):
            return scope.enter_context(nc.sbuf_tensor(name, shape, dt))

        def sem(name):
            return ctx.enter_context(nc.semaphore(name))

        x = sb("x", [P, KC, T])
        raw = [sb(f"raw{s}", [P, SLAB]) for s in range(2)]
        hi = [sb(f"hi{s}", [P, SLAB], f32r) for s in range(2)]
        lo = [sb(f"lo{s}", [P, SLAB], f32r) for s in range(2)]
        vec = sb("vec", [P, NV])
        cst = sb("cst", [P, NC_])
        ident, ones, neg, caus = (cst[:, c:c + P] for c in (C_ID, C_ONE, C_NEG, C_CAUS))
        mod = sb("mod", [P, 96])
        eps = vec[:, V["eps"]:V["eps"] + 1]
        gsc = sb("gsc", [P, 4 * KC])
        hH = sb("hH", [P, KC, T], f32r)
        hL = sb("hL", [P, KC, T], f32r)
        small = sb("small", [P, 64])
        posi = sb("posi", [P, T], i32)
        swp = sb("swp", [P, 2 * P])
        D = [ctx.enter_context(nc.psum_tensor(f"D{i}", [P, 2, T], fp32)) for i in range(4)]

        first = ExitStack()
        ctx.enter_context(first)
        adar = [sb(f"adar{s}", [P, SLAB], scope=first) for s in range(2)]
        cact = sb("cact", [P, KC], scope=first)

        gdn = ExitStack()
        lvl = sb("lvl", [P, 7 * P], i32, gdn)
        rows = sb("rows", [GH, 4, T], scope=gdn)
        tsc = sb("tsc", [P, 4, NT, GH], scope=gdn)
        qs = sb("qs", [P, 2, T], scope=gdn)
        ks = sb("ks", [P, 2, T], scope=gdn)
        vs = sb("vs", [P, 2, T], scope=gdn)
        gs = sb("gs", [P, 2, T], scope=gdn)
        sq = sb("sq", [P, 4, T], scope=gdn)
        rtmp = sq[0:GH, 0:3]
        eg = sb("eg", [P, 2, T], scope=gdn)
        dt = sb("dt", [P, 2, T], scope=gdn)
        kb = sb("kb", [P, 2, T], scope=gdn)
        qd = sb("qd", [P, 2, T], scope=gdn)
        up = sb("up", [P, 2, T], scope=gdn)
        att = sb("att", [P, 2, T], scope=gdn)
        xi = sb("xi", [P, 2, T], scope=gdn)
        zi = sb("zi", [P, 2, T], scope=gdn)
        st = sb("st", [P, 4, P], scope=gdn)
        vn = sb("vn", [P, 2, P], scope=gdn)
        go = sb("go", [P, KC, T], scope=gdn)
        gdn.close()
        ffn = ExitStack()
        aH = sb("aH", [P, FA, T], f32r, ffn)
        aL = sb("aL", [P, FA, T], f32r, ffn)
        sg = sb("sg", [P, 2, T], scope=ffn)
        af = sb("af", [P, 2, T], scope=ffn)
        nrs = sb("nrs", [P, T], scope=ffn)
        ffn.close()
        mla = ExitStack()
        craw = sb("craw", [P, 6, T], scope=mla)
        cH = sb("cH", [P, 5, T], f32r, mla)
        cL = sb("cL", [P, 5, T], f32r, mla)
        mcos = sb("mcos", [P, T], scope=mla)
        msin = sb("msin", [P, T], scope=mla)
        qn = sb("qn", [P, 2, T], scope=mla)
        qr0 = sb("qr0", [P, T], scope=mla)
        qr = sb("qr", [P, T], scope=mla)
        kn = sb("kn", [P, 2, T], scope=mla)
        vt = sb("vt", [P, NT, 2 * P], scope=mla)
        pr = sb("pr", [P, 2, T], scope=mla)
        pT = sb("pT", [P, 2, T], scope=mla)
        krp = sb("krp", [P, T], scope=mla)
        nsq = sb("nsq", [P, 2, T], scope=mla)
        ntm = sb("ntm", [P, 2, T], scope=mla)
        mrs = sb("mrs", [P, T], scope=mla)
        mla.close()
        first.close()
        blk2 = ExitStack()
        TAB = 7 * T
        tab = sb("tab", [P, TAB], scope=blk2)
        rcos, rsin, acos, asin, intra, qdec, win = (tab[:, k * T:k * T + T] for k in range(7))
        vb = sb("vb", [P, 9 * P], scope=blk2)
        rH = sb("rH", [P, KC, T], f32r, blk2)
        rL = sb("rL", [P, KC, T], f32r, blk2)
        qk = sb("qk", [P, 2, T], scope=blk2)
        kq = sb("kq", [P, 2, T], scope=blk2)
        tm2 = sb("tm2", [P, 2, T], scope=blk2)
        rvt = sb("rvt", [P, NT, 2 * P], scope=blk2)
        rg = sb("rg", [P, 2, T], scope=blk2)
        ka = sb("ka", [P, 2, T], scope=blk2)
        qde = sb("qde", [P, T], scope=blk2)
        rst = sb("rst", [P, 2, 2 * P], scope=blk2)
        ry = sb("ry", [P, 2, T], scope=blk2)
        rsq = sb("rsq", [P, 2, T], scope=blk2)
        mg = sb("mg", [P, KC, T], scope=blk2)
        blk2.close()

        x_in, slab_in, ada_in = sem("x_in"), [sem("slab_in0"), sem("slab_in1")], [sem("ada_in0"), sem("ada_in1")]
        hi_ready, lo_ready, slab_done = sem("hi_ready"), sem("lo_ready"), sem("slab_done")
        bank_free = [sem("bank_free0"), sem("bank_free1")]
        ada_done, mod_ready, cact_ready = sem("ada_done"), sem("mod_ready"), sem("cact_ready")
        ada_sum, ada_sum_v, pool_chain, vec_in = sem("ada_sum"), sem("ada_sum_v"), sem("pool_chain"), sem("vec_in")
        dve_chain = sem("dve_chain")
        sq_ready, sq_used, xg_ready = sem("sq_ready"), sem("sq_used"), sem("xg_ready")
        hh_ready, h_ready = sem("hh_ready"), sem("h_ready")
        aH_ready, aL_ready = sem("aH_ready"), sem("aL_ready")
        out_done = sem("out_done")
        tab_in = sem("tab_in")
        rms_ready, x_added = sem("rms_ready"), sem("x_added")

        def product(pe, s, kc, nt, H, L, between=None):
            pe.wait_ge(lo_ready, s.plus(1))
            if s.b >= 2:
                pe.wait_ge(bank_free[s.slot], s.prior())
            for m in range(nt):
                for k in range(kc):
                    if between and m * kc + k in between:
                        between[m * kc + k]()
                    w = slice((k * nt + m) * P, (k * nt + m + 1) * P)
                    o = D[s.slot][:, m, :]
                    T_.matmul(o, lo[s.slot][:, w], H[:, k, :], start=(k == 0), stop=False)
                    T_.matmul(o, hi[s.slot][:, w], L[:, k, :], start=False, stop=False)
                    last = T_.matmul(o, hi[s.slot][:, w], H[:, k, :], start=False, stop=(k == kc - 1))
            last.then_inc(slab_done, 1)

        def product_first(pe, s, kc, nt, H, L, ready):
            pe.wait_ge(lo_ready, s.plus(1))
            if s.b >= 2:
                pe.wait_ge(bank_free[s.slot], s.prior())
            for k in range(kc):
                ready(k)
                for m in range(nt):
                    w = slice((k * nt + m) * P, (k * nt + m + 1) * P)
                    o = D[s.slot][:, m, :]
                    T_.matmul(o, lo[s.slot][:, w], H[:, k, :], start=(k == 0), stop=False)
                    T_.matmul(o, hi[s.slot][:, w], L[:, k, :], start=False, stop=False)
                    last = T_.matmul(o, hi[s.slot][:, w], H[:, k, :], start=False, stop=(k == kc - 1))
            last.then_inc(slab_done, 1)

        def h_batch(pe, hb):
            return lambda k: pe.wait_ge(h_ready, KC * hb + k + 1)

        def product_t(pe, s, kc, H, L, width=2 * P, between=None):
            pe.wait_ge(lo_ready, s.plus(1))
            pe.wait_ge(bank_free[s.slot], s.prior())
            for t in range(NT):
                o = D[s.slot].rearrange("p a (b n) -> p (a b) n", b=2)[:, t, 0:width]
                tok = slice(t * P, (t + 1) * P)
                if between and t in between:
                    between[t]()
                for k in range(kc):
                    w = slice(k * 2 * P, k * 2 * P + width)
                    T_.matmul(o, L[:, k, tok], hi[s.slot][:, w], start=(k == 0), stop=False)
                    T_.matmul(o, H[:, k, tok], lo[s.slot][:, w], start=False, stop=False)
                    last = T_.matmul(o, H[:, k, tok], hi[s.slot][:, w], start=False, stop=(k == kc - 1))
            last.then_inc(slab_done, 1)

        def split_hi(act, s, n=SLAB):
            act.wait_ge(slab_in[s.slot], s.prior(1, 16))
            if s.b >= 2:
                act.wait_ge(slab_done, s.plus(-1))
            S_.activation(hi[s.slot][:, 0:n], raw[s.slot][:, 0:n], ACT.Copy).then_inc(hi_ready, 1)

        def split_lo(dve, s, n=SLAB):
            dve.wait_ge(hi_ready, s.plus(1))
            V_.tensor_tensor(lo[s.slot][:, 0:n], raw[s.slot][:, 0:n], hi[s.slot][:, 0:n],
                             ALU.subtract).then_inc(lo_ready, 1)

        def ada_chunks(eng, E, chain, a, cols, done):
            r3 = adar[a.slot].rearrange("p (k n) -> p k n", k=KC)[:, :, cols]
            eng.wait_ge(ada_in[a.slot], a.prior(1, 16))
            chain.link(E.tensor_tensor(r3, r3, cact[:].unsqueeze(2).to_broadcast([P, KC, cols.stop - cols.start]),
                                       ALU.mult))
            for n in (4, 2, 1):
                last = E.tensor_tensor(r3[:, 0:n], r3[:, 0:n], r3[:, n:2 * n], ALU.add)
                if n > 1:
                    chain.link(last)
            last.then_inc(done, 1)

        def ada_pool(pool, chain):
            for a in range(ADA0):
                ada_chunks(pool, nc.gpsimd, chain, Slab(a), slice(ADA_V, 2 * P), ada_sum)

            def body(i):
                for j in range(2):
                    ada_chunks(pool, nc.gpsimd, chain, Slab(ADA0 + j, i, 2), slice(0, 2 * P), ada_sum)
            loop(pool, (2 * ADA_L - ADA0) // 2, body, chain, 6)

        def ada_pe(pe, a, wait_mod=0):
            if wait_mod:
                pe.wait_ge(mod_ready, wait_mod)
            pe.wait_ge(ada_sum, a.plus(1))
            for m in range(2):
                last = T_.matmul(D[3][:, 1, bass.ds(at(2 * a.b + m, a.i, 2 * a.step), 1)],
                                 adar[a.slot][:, m * P:(m + 1) * P], ones[:, 0:1], start=True, stop=True)
            last.then_inc(ada_done, 1)

        def load_slab(sp, s):
            if s.b >= 2:
                sp.wait_ge(lo_ready, s.plus(-1))
            sp.dma_start(raw[s.slot][:], slabs[bass.ds(s.plus(0), 1), :, :].rearrange("a p n -> p (a n)")
                         if s.i is not None else slabs[s.b, :, :]).then_inc(slab_in[s.slot], 16)

        def load_ada(sp, a):
            if a.b >= 2:
                sp.wait_ge(ada_done, a.plus(-1))
            sp.dma_start(adar[a.slot][:], ada[bass.ds(a.plus(0), 1), :, :].rearrange("a p n -> p (a n)")
                         if a.i is not None else ada[a.b, :, :]).then_inc(ada_in[a.slot], 16)

        def norm_pe(pe, n, nsq, chunks=range(KC)):
            for c in chunks:
                pe.wait_ge(sq_ready, KC * n + c + 1)
                last = T_.matmul(D[2][:, 0, :], ones, nsq[:, c % 2, :], start=(c == 0), stop=(c == KC - 1))
                last.then_inc(sq_used, 1)

        def x_written(eng, g):
            for s in (Slab(g - 1), Slab(g - 2)):
                eng.wait_ge(bank_free[s.slot], s.prior(1))

        def square(act, n, nsq, c):
            if c >= 2 or n:
                act.wait_ge(sq_used, KC * n + c - 1)
            S_.activation(nsq[:, c % 2, :], x[:, c, :], ACT.Square, scale=DM ** -0.5).then_inc(sq_ready, 1)

        def norm_act(act, n, nrs, ntm, shift, to_h=True, then=None):
            if then is not None:
                split_hi(act, Slab(then))
            act.wait_ge(sq_used, KC * n + KC)
            S_.activation(nrs, D[2][:, 0, :], ACT.Ln, bias=eps).then_inc(rms_ready, 1)
            act.wait_ge(rms_ready, 2 * n + 1)
            S_.activation(nrs, nrs, ACT.Exp, scale=-0.5).then_inc(rms_ready, 1)
            for c in range(KC if to_h else 0):
                act.wait_ge(xg_ready, KC * n + c + 1)
                S_.activation(hH[:, c, :], ntm[:, c % 2, :], ACT.Identity, bias=shift(c)).then_inc(hh_ready, 1)

        def norm_dve(dve, n, hb, nrs, ntm, gain, shift, then=None):
            if then is not None:
                split_lo(dve, Slab(then))
            dve.wait_ge(rms_ready, 2 * n + 2)
            for c in range(KC + 1):
                if c < KC:
                    if c >= 2:
                        dve.wait_ge(h_ready, KC * hb + c - 1)
                    V_.scalar_tensor_tensor(out=ntm[:, c % 2, :], in0=x[:, c, :], scalar=gain(c), in1=nrs,
                                            op0=ALU.mult, op1=ALU.mult).then_inc(xg_ready, 1)
                if c >= 1:
                    dve.wait_ge(hh_ready, KC * hb + c)
                    dve.wait_ge(xg_ready, KC * n + c)
                    V_.scalar_tensor_tensor(out=hL[:, c - 1, :], in0=ntm[:, (c - 1) % 2, :], scalar=shift(c - 1),
                                            in1=hH[:, c - 1, :], op0=ALU.add, op1=ALU.subtract).then_inc(h_ready, 1)

        def norm_x_dve(dve, n, nrs, gain):
            dve.wait_ge(rms_ready, 2 * n + 2)
            for c in range(KC):
                V_.scalar_tensor_tensor(out=x[:, c, :], in0=x[:, c, :], scalar=gain(c), in1=nrs,
                                        op0=ALU.mult, op1=ALU.mult).then_inc(xg_ready, 1)

        def to_h_act(act, src):
            for c in range(KC):
                S_.activation(hH[:, c, :], src[:, c, :], ACT.Copy).then_inc(hh_ready, 1)

        def to_h_dve(dve, hb, src):
            for c in range(KC):
                dve.wait_ge(hh_ready, KC * hb + c + 1)
                V_.tensor_tensor(hL[:, c, :], src[:, c, :], hH[:, c, :], ALU.subtract).then_inc(h_ready, 1)

        def add_chunk(s, m, c, gate):
            xc = x[:, bass.ds(c, 1), :].rearrange("p a n -> p (a n)")
            return V_.scalar_tensor_tensor(out=xc, in0=D[s.slot][:, m, :], scalar=gate(c) if gate else 1.0, in1=xc,
                                           op0=ALU.mult, op1=ALU.add)

        def add_act(act, base, n):
            def body(i):
                for j in range(2):
                    split_hi(act, Slab(base + j + 2, i, 2))
            loop(act, n // 2, body)

        def add_dve(dve, base, n, nt, gate):
            def body(i):
                for j in range(2):
                    s = Slab(base + j, i, 2)
                    dve.wait_ge(slab_done, s.plus(1))
                    for m in range(nt):
                        last = add_chunk(s, m, at(nt * j + m, i, 2 * nt), gate)
                    last.then_inc(bank_free[s.slot], 1)
                    split_lo(dve, s.next(2))
            loop(dve, n // 2, body)

        def final_pe(pe, base, kc, H, L, ready, n):
            for j in range(N_OUT):
                s, chunks = Slab(base + j), range(2 * j - 2, 2 * j)
                if j == 0:
                    product_first(pe, s, kc, 2, H, L, ready)
                else:
                    product(pe, s, kc, 2, H, L, {kc + 2: lambda: norm_pe(pe, n, sg, chunks)})
            norm_pe(pe, n, sg, range(KC - 2, KC))

        def final_act(act, base, n, f):
            for j in range(N_OUT):
                s = Slab(base + j)
                if j + 2 <= N_OUT:
                    split_hi(act, s.next(2))
                act.wait_ge(x_added, N_OUT * f + j + 1)
                square(act, n, sg, 2 * j)
                act.wait_ge(bank_free[s.slot], s.prior(1))
                square(act, n, sg, 2 * j + 1)

        def final_dve(dve, base, gate):
            for j in range(N_OUT):
                s = Slab(base + j)
                dve.wait_ge(slab_done, s.plus(1))
                add_chunk(s, 0, 2 * j, gate).then_inc(x_added, 1)
                add_chunk(s, 1, 2 * j + 1, gate).then_inc(bank_free[s.slot], 1)
                if j + 2 <= N_OUT:
                    split_lo(dve, s.next(2))

        MD = lambda layer, part: 48 * layer + KC * part

        def gain_cols(chain, norm, src, layer, part):
            chain.link(V_.scalar_tensor_tensor(
                out=gsc[:, KC * norm:KC * norm + KC], in0=mod[:, MD(layer, part):MD(layer, part) + KC], scalar=1.0,
                in1=vec[:, V[src] + KC * layer:V[src] + KC * layer + KC], op0=ALU.add, op1=ALU.mult))

        def mod_dve(dve, chain, lo_, hi_, ada_n):
            dve.wait_ge(ada_done, ada_n)
            V_.tensor_tensor(mod[:, lo_:hi_], D[3][:, 1, lo_:hi_], vec[:, V["ada_b"] + lo_:V["ada_b"] + hi_],
                             ALU.add).then_inc(mod_ready, 1)

        gg = {n: sem("g_" + n) for n in (
            "row", "rowd", "rowp", "qkv", "sq", "ssq", "sel", "br", "dif", "expd", "egr", "kbq", "gram", "up",
            "kt", "ktv", "bb", "pp", "pb", "qq1", "qq2", "qq3", "qq4",
            "qq5", "qq6", "xx", "xt", "zz", "wtp", "wt", "vp", "vn", "op", "stp", "st", "osq", "oss",
            "of", "rt", "ort")}

        def tiles(t_, m=None):
            v = t_[:].rearrange("p m (t n) -> p m t n", t=NT)
            return v if m is None else v[:, m]

        def over(ap, n=NT):
            return ap.unsqueeze(1).to_broadcast([P, n, P])

        def rows_dve(dve, chain):
            L = chain.link
            a_, u_, w_ = (rtmp[:, k, :] for k in range(3))
            gc, beta, dl, nbe = (rows[:, k, :] for k in range(4))
            dve.wait_ge(slab_done, 1)
            L(V_.tensor_scalar(a_, D[0][0:GH, 0, :], vec[0:GH, V["dt_b"]:V["dt_b"] + 1], None, ALU.add))
            L(V_.tensor_copy(beta, D[0][0:GH, 1, :]))
            V_.scalar_tensor_tensor(out=u_, in0=a_, scalar=-1.0, in1=a_, op0=ALU.mult,
                                    op1=ALU.max).then_inc(bank_free[0], 1)
            dve.wait_ge(gg["row"], 2)
            L(V_.tensor_scalar(w_, u_, 1.0, None, ALU.add))
            L(V_.tensor_copy(gc, w_))
            L(V_.tensor_scalar(dl, w_, 1.0, None, ALU.subtract))
            V_.tensor_scalar(w_, dl, 0.0, None, ALU.is_equal).then_inc(gg["rowd"], 1)
            dve.wait_ge(gg["row"], 3)
            dve.wait_ge(gg["rowd"], 1)
            L(V_.tensor_tensor(gc, gc, w_, ALU.add))
            L(V_.tensor_tensor(dl, dl, w_, ALU.add))
            L(V_.tensor_tensor(gc, gc, u_, ALU.mult))
            L(V_.reciprocal(dl, dl))
            L(V_.tensor_tensor(gc, gc, dl, ALU.mult))
            L(V_.scalar_tensor_tensor(out=gc, in0=a_, scalar=0.0, in1=gc, op0=ALU.max, op1=ALU.add))
            L(V_.tensor_scalar(a_, gc, small[0:GH, 0:1], -1.0, ALU.mult, ALU.mult))
            L(V_.memset(w_, 0.0))
            for t in range(NT):
                c = slice(t * P, t * P + P)
                L(V_.tensor_tensor_scan(gc[:, c], a_[:, c], w_[:, c], 0.0, ALU.add, ALU.add))
            g3 = gc.rearrange("p (t n) -> p t n", t=NT)
            V_.tensor_tensor(u_.rearrange("p (t n) -> p t n", t=NT), g3[:, :, P - 1:P].to_broadcast([GH, NT, P]), g3,
                             ALU.subtract).then_inc(gg["rowd"], 1)
            dve.wait_ge(gg["row"], 5)
            V_.scalar_tensor_tensor(out=nbe, in0=beta, scalar=-1.0, in1=w_, op0=ALU.mult,
                                    op1=ALU.mult).then_inc(gg["rowd"], 1)
            dve.wait_ge(gg["rowp"], 1)
            V_.tensor_copy(tsc[:].rearrange("p a t h -> p (a t h)"), D[3][:, 0, 0:4 * NT * GH]).then_inc(gg["of"], 1)
            dve.wait_ge(gg["of"], 1)

        def rows_act(act):
            u_, w_ = rtmp[:, 1, :], rtmp[:, 2, :]
            gc, beta, dl = (rows[:, k, :] for k in range(3))
            S_.activation(small[0:GH, 0:1], vec[0:GH, V["a_log"]:V["a_log"] + 1], ACT.Exp)
            act.wait_ge(bank_free[0], 1)
            S_.activation(beta, beta, ACT.Sigmoid).then_inc(gg["row"], 1)
            S_.activation(u_, u_, ACT.Exp, scale=-1.0).then_inc(gg["row"], 1)
            act.wait_ge(gg["rowd"], 1)
            S_.activation(gc, gc, ACT.Ln).then_inc(gg["row"], 1)
            act.wait_ge(gg["rowd"], 2)
            S_.activation(w_, gc, ACT.Exp).then_inc(gg["row"], 1)
            S_.activation(dl, u_, ACT.Exp).then_inc(gg["row"], 1)

        def rows_pe(pe):
            pe.wait_ge(gg["rowd"], 3)
            for a in range(4):
                for t in range(NT):
                    o = (a * NT + t) * GH
                    last = T_.transpose(D[3][:, 0, o:o + GH], rows[:, a, t * P:t * P + P], ident[0:GH, 0:GH])
            last.then_inc(gg["rowp"], 1)

        PAIR = 4
        qkv = (qs, ks, vs)
        half_t = lambda t_, m: t_[:, m, :].rearrange("p (t n) -> p t n", t=NT)

        def gdn_act(act):
            def body(p):
                w = lambda n, k, per: act.wait_ge(gg[n], at(k, p, per))

                def conv_done(j):
                    s = Slab(G_GDN + j, p, PAIR)
                    act.wait_ge(bank_free[s.slot], s.prior(1))
                    S_.activation(qkv[j][:], qkv[j][:], ACT.Silu).then_inc(gg["qkv"], 1)

                def log(a):
                    w("ssq", a + 1, 2)
                    S_.activation(sq[:, 2 * a:2 * a + 2], D[2][:], ACT.Ln, bias=eps).then_inc(gg["rt"], 1)
                split_hi(act, Slab(G_GDN + 1, p, PAIR))
                w("br", 1, 2)
                S_.activation(kb[:], D[2][:], ACT.Copy).then_inc(gg["bb"], 1)
                split_hi(act, Slab(G_GDN + 2, p, PAIR))
                w("br", 2, 2)
                S_.activation(eg[:], D[2][:], ACT.Exp).then_inc(gg["egr"], 1)
                conv_done(0)
                w("qkv", 1, 3)
                S_.activation(sq[:, 0:2], qs[:], ACT.Square).then_inc(gg["sq"], 1)
                split_hi(act, Slab(G_GDN + 3, p, PAIR))
                w("dif", 1, 1)
                S_.activation(dt[:], dt[:], ACT.Exp).then_inc(gg["expd"], 1)
                log(0)
                conv_done(1)
                w("qkv", 2, 3)
                S_.activation(sq[:, 2:4], ks[:], ACT.Square).then_inc(gg["sq"], 1)
                split_hi(act, Slab(G_GDN + 4, p, PAIR))
                log(1)
                w("rt", 2, 3)
                S_.activation(sq[:], sq[:], ACT.Exp, scale=-0.5).then_inc(gg["rt"], 1)
                conv_done(2)
                s = Slab(G_GDN + 3, p, PAIR)
                act.wait_ge(slab_done, s.plus(1))
                S_.activation(gs[:], D[s.slot][:], ACT.Silu).then_inc(bank_free[s.slot], 1)
                for lv in range(7):
                    for m in range(2 if lv else 0):
                        w("pp", 2 * lv - 1 + m, 12)
                        S_.activation(sq[:, m], D[0][:, m, :], ACT.Copy).then_inc(gg["pb"], 1)
                    for m in range(2):
                        w("xt", 2 * lv + m + 1, 14)
                        S_.activation((zi if lv else xi)[:, m], D[2][:, m, :], ACT.Copy).then_inc(gg["zz"], 1)
                w("wtp", 1, 1)
                S_.activation(sq[:, 2:4], D[0][:], ACT.Copy).then_inc(gg["wt"], 1)
                for t in range(NT):
                    w("vp", t + 1, NT)
                    S_.activation(vn[:], D[1][:, :, 0:P], ACT.Copy).then_inc(gg["vn"], 1)
                w("op", 1, 1)
                S_.activation(sq[:, 0:2], D[2][:], ACT.Square, scale=P ** -0.5).then_inc(gg["osq"], 1)
                w("oss", 1, 1)
                S_.activation(sq[:, 2:4], D[0][:], ACT.Ln, bias=eps).then_inc(gg["ort"], 1)
                w("ort", 1, 2)
                S_.activation(sq[:, 2:4], sq[:, 2:4], ACT.Exp, scale=-0.5).then_inc(gg["ort"], 1)
            loop(act, GH // 2, body)

        def gdn_dve(dve, chain):
            def body(p):
                L = chain.link
                w = lambda n, k, per: dve.wait_ge(gg[n], at(k, p, per))

                def conv(j):
                    s = Slab(G_GDN + j, p, PAIR)
                    dve.wait_ge(slab_done, s.plus(1))
                    for tap in range(4):
                        for m in range(2):
                            cw = vec[:, bass.ds(at(V["conv"] + (j * GH + m) * 4 + 3 - tap, p, 8), 1)]
                            o = qkv[j][:, m, tap:]
                            if tap == 0:
                                last = V_.tensor_scalar(o, D[s.slot][:, m, :], cw, None, ALU.mult)
                            else:
                                last = V_.scalar_tensor_tensor(out=o, in0=D[s.slot][:, m, 0:T - tap], scalar=cw, in1=o,
                                                               op0=ALU.mult, op1=ALU.add)
                        if tap < 3:
                            L(last)
                    last.then_inc(bank_free[s.slot], 1)
                for m in range(2):
                    one = cst[0:GH, bass.ds(at(C_ID + m, p, 2), 1)]
                    V_.tensor_scalar(up[0:GH, m, :], rows[:, 0, :], one, None, ALU.mult)
                    last = V_.tensor_scalar(att[0:GH, m, :], rows[:, 1, :], one, None, ALU.mult)
                last.then_inc(gg["sel"], 1)
                split_lo(dve, Slab(G_GDN + 1, p, PAIR))
                conv(0)
                split_lo(dve, Slab(G_GDN + 2, p, PAIR))
                w("br", 2, 2)
                w("egr", 1, 1)
                for m in range(2):
                    gcj = tsc[:, 0, :, bass.ds(at(m, p, 2), 1)].to_broadcast([P, NT, P])
                    last = V_.tensor_tensor(tiles(dt, m), tiles(D[2], m), gcj, ALU.subtract)
                L(last)
                V_.tensor_tensor(dt[:].rearrange("p m (t n) -> p (m t) n", t=NT),
                                 dt[:].rearrange("p m (t n) -> p (m t) n", t=NT), over(neg, 2 * NT),
                                 ALU.min).then_inc(gg["dif"], 1)
                conv(1)
                split_lo(dve, Slab(G_GDN + 3, p, PAIR))
                conv(2)
                split_lo(dve, Slab(G_GDN + 4, p, PAIR))
                w("rt", 3, 3)
                w("qkv", 2, 3)
                V_.scalar_tensor_tensor(out=qs[:], in0=qs[:], scalar=P ** -0.5, in1=sq[:, 0:2], op0=ALU.mult,
                                        op1=ALU.mult)
                L(V_.tensor_tensor(ks[:], ks[:], sq[:, 2:4], ALU.mult))
                w("bb", 1, 1)
                V_.tensor_tensor(kb[:], ks[:], kb[:], ALU.mult).then_inc(gg["kbq"], 1)
                V_.tensor_tensor(qd[:], qs[:], eg[:], ALU.mult).then_inc(gg["kbq"], 1)
                w("expd", 1, 1)
                for m in range(2):
                    w("gram", m + 1, 3)
                    V_.scalar_tensor_tensor(out=up[:, m], in0=D[1][:, m, :], scalar=-1.0, in1=dt[:, m], op0=ALU.mult,
                                            op1=ALU.mult).then_inc(gg["up"], 1)
                    if m == 0:
                        L(V_.tensor_copy(zi[:].rearrange("p m (t n) -> p (m t) n", t=NT), over(ident, 2 * NT)))
                for m in range(2):
                    dve.wait_ge(x_in, 48)
                    w("up", m + 1, 3)
                    V_.copy_predicated(half_t(zi, m), over(lvl[:, 0:P]), half_t(up, m)).then_inc(gg["xx"], 1)
                w("gram", 3, 3)
                V_.tensor_tensor(att[:], D[2][:], dt[:], ALU.mult).then_inc(gg["up"], 1)
                w("kt", 1, 2)
                for m in range(2):
                    h1 = bass.ds(at(m, p, 2), 1)
                    V_.tensor_tensor(tiles(kb, m), tiles(D[0], m), tsc[:, 3, :, h1].to_broadcast([P, NT, P]), ALU.mult)
                    last = V_.tensor_tensor(tiles(ks, m), tiles(D[0], m),
                                            tsc[:, 2, :, h1].to_broadcast([P, NT, P]), ALU.mult)
                last.then_inc(gg["ktv"], 1)
                w("kt", 2, 2)
                for m in range(2):
                    h1 = bass.ds(at(m, p, 2), 1)
                    last = V_.tensor_tensor(tiles(vs, m), tiles(D[1], m),
                                            tsc[:, 1, :, h1].to_broadcast([P, NT, P]), ALU.mult)
                last.then_inc(gg["ktv"], 1)
                for lv in range(1, 7):
                    for m in range(2):
                        dve.wait_ge(x_in, 48)
                        w(f"qq{lv}", m + 1, 2)
                        V_.copy_predicated(half_t(xi, m), over(lvl[:, lv * P:lv * P + P]),
                                           half_t(D[1], m)).then_inc(gg["xx"], 1)
                for t in range(NT - 1):
                    w("stp", t + 1, NT - 1)
                    for m in range(2):
                        if t == 0:
                            last = V_.tensor_copy(st[:, m], D[0][:, m, 0:P])
                        else:
                            last = V_.scalar_tensor_tensor(out=st[:, 2 * (t % 2) + m], in0=st[:, 2 * ((t - 1) % 2) + m],
                                                           scalar=eg[:, m, t * P + P - 1:t * P + P],
                                                           in1=D[0][:, m, 0:P], op0=ALU.mult, op1=ALU.add)
                    last.then_inc(gg["st"], 1)
                    w("st", t + 1, NT - 1)
                w("ort", 2, 2)
                L(V_.scalar_tensor_tensor(out=sq[:, 2:4], in0=D[2][:], scalar=vec[:, V["gdn_g"]:V["gdn_g"] + 1],
                                          in1=sq[:, 2:4], op0=ALU.mult, op1=ALU.mult))
                V_.tensor_tensor(go[:, bass.ds(at(0, p, 2), 2), :], sq[:, 2:4], gs[:], ALU.mult).then_inc(gg["of"], 1)
            loop(dve, GH // 2, body, chain, 3 * 3 + 4)

        def gdn_pe(pe):
            def body(p):
                w = lambda n, k, per: pe.wait_ge(gg[n], at(k, p, per))
                blk = lambda t_, b: t_[:, b // NT, (b % NT) * P:(b % NT) * P + P]
                heads = [range(m * NT, m * NT + NT) for m in range(2)]

                def along(src):
                    for m in range(2):
                        last = T_.matmul(D[2][:, m, :], ones[0:GH], src[0:GH, m, :], start=True, stop=True)
                    last.then_inc(gg["br"], 1)

                def gc_rows():
                    w("bb", 1, 1)
                    along(up)

                def squares(a):
                    w("sq", a + 1, 2)
                    if a:
                        w("rt", 1, 3)
                    else:
                        w("dif", 1, 1)
                    for m in range(2):
                        last = T_.matmul(D[2][:, m, :], ones, sq[:, 2 * a + m, :], start=True, stop=True)
                    last.then_inc(gg["ssq"], 1)
                slab = lambda j: Slab(G_GDN + j, p, PAIR)
                ada_at = lambda j: ada_pe(pe, Slab(ADA0 + j, p, ADA_P), 1)
                product(pe, slab(0), KC, 2, hH, hL)
                w("of", 1, 1)
                w("sel", 1, 1)
                along(att)
                product(pe, slab(1), KC, 2, hH, hL, {8: gc_rows})
                ada_at(0)
                product(pe, slab(2), KC, 2, hH, hL, {8: lambda: squares(0)})
                ada_at(1)
                product(pe, slab(3), KC, 2, hH, hL, {4: lambda: squares(1)})
                ada_at(2)
                pe.wait_ge(bank_free[slab(2).slot], slab(2).prior(1))
                w("kbq", 1, 2)
                for m in range(2):
                    for b in heads[m]:
                        last = T_.matmul(blk(D[1], b), blk(ks, b), blk(kb, b), start=True, stop=True)
                    last.then_inc(gg["gram"], 1)
                w("rt", 2, 3)
                for b in range(2 * NT):
                    last = T_.matmul(blk(D[2], b), blk(ks, b), blk(qs, b), start=True, stop=True)
                last.then_inc(gg["gram"], 1)
                pe.wait_ge(bank_free[slab(3).slot], slab(3).prior(1))
                for b in range(2 * NT):
                    last = T_.transpose(blk(D[0], b), blk(ks, b), ident)
                last.then_inc(gg["kt"], 1)
                ada_at(3)
                w("up", 2, 3)
                w("qkv", 3, 3)
                for b in range(2 * NT):
                    last = T_.transpose(blk(D[1], b), blk(vs, b), ident)
                last.then_inc(gg["kt"], 1)
                w("up", 3, 3)
                for m in range(2):
                    w("xx", m + 1, 14)
                    for b in heads[m]:
                        last = T_.transpose(blk(D[2], b), blk(zi, b), ident)
                    last.then_inc(gg["xt"], 1)
                for lv in range(1, 7):
                    if lv == 1:
                        w("ktv", 1, 2)
                    for m in range(2):
                        w("zz", 2 * lv - 1 + m, 14)
                        for b in heads[m]:
                            last = T_.matmul(blk(D[0], b), blk(up, b), blk(xi, b), start=True, stop=True)
                        last.then_inc(gg["pp"], 1)
                    if lv % 2 == 0:
                        ada_at(3 + lv // 2)
                    if lv == 1:
                        w("ktv", 2, 2)
                    for m in range(2):
                        w("pb", 2 * lv - 1 + m, 12)
                        for b in heads[m]:
                            last = T_.matmul(blk(D[1], b), blk(zi, b), blk(sq, b), start=True, stop=True)
                        last.then_inc(gg[f"qq{lv}"], 1)
                    for m in range(2):
                        w("xx", 2 * lv + m + 1, 14)
                        for b in heads[m]:
                            last = T_.transpose(blk(D[2], b), blk(xi, b), ident)
                        last.then_inc(gg["xt"], 1)
                w("zz", 14, 14)
                for b in range(2 * NT):
                    last = T_.matmul(blk(D[0], b), blk(kb, b), blk(zi, b), start=True, stop=True)
                last.then_inc(gg["wtp"], 1)
                w("kbq", 2, 2)
                for t in range(NT):
                    if t == 1:
                        w("wt", 1, 1)
                    if t:
                        w("st", t, NT - 1)
                    for m in range(2):
                        b = m * NT + t
                        last = T_.matmul(D[1][:, m, 0:P], blk(zi, b), blk(vs, b), start=True, stop=(t == 0))
                        if t:
                            last = T_.matmul(D[1][:, m, 0:P], sq[:, 2 + m, t * P:t * P + P],
                                             st[:, 2 * ((t - 1) % 2) + m], start=False, stop=True)
                    last.then_inc(gg["vp"], 1)
                    if t == 0:
                        w("wt", 1, 1)
                    w("vn", t + 1, NT)
                    if t < NT - 1:
                        for m in range(2):
                            last = T_.matmul(D[0][:, m, 0:P], blk(ks, m * NT + t), vn[:, m], start=True, stop=True)
                        last.then_inc(gg["stp"], 1)
                    for m in range(2):
                        b = m * NT + t
                        if t:
                            T_.matmul(blk(D[2], b), st[:, 2 * ((t - 1) % 2) + m], blk(qd, b), start=True, stop=False)
                        last = T_.matmul(blk(D[2], b), vn[:, m], blk(att, b), start=(t == 0), stop=True)
                last.then_inc(gg["op"], 1)
                ada_at(7)
                w("osq", 1, 1)
                for m in range(2):
                    last = T_.matmul(D[0][:, m, :], ones, sq[:, m, :], start=True, stop=True)
                last.then_inc(gg["oss"], 1)
            loop(pe, GH // 2, body)

        def linear_pe(pe, base, n, kc, nt, H, L, ready, ada_base=None):
            per = 2 if ada_base is None else 4
            def body(i):
                for j in range(per):
                    s = Slab(base + j + (per if i is not None else 0), i, per)
                    if i is None and j == 0:
                        product_first(pe, s, kc, nt, H, L, ready)
                    else:
                        product(pe, s, kc, nt, H, L)
                    if per == 4 and j % 2:
                        ada_pe(pe, Slab(ada_base + j // 2 + (2 if i is not None else 0), i, 2), 2)
            body(None)
            loop(pe, n // per - 1, body)

        def ffn_pe(pe, base, f, hb, n, ada_base=None):
            hidden = lambda off: lambda k: pe.wait_ge(aL_ready, 11 * f + off + k // 2 + 1) if k % 2 == 0 else None
            linear_pe(pe, base, N_GUA, KC, 2, hH, hL, h_batch(pe, hb), ada_base)
            linear_pe(pe, base + N_GUA, N_DNA, FA, 1, aH, aL, hidden(0))
            base += N_GUA + N_DNA
            linear_pe(pe, base, N_GUB, KC, 2, hH, hL, h_batch(pe, hb))
            final_pe(pe, base + N_GUB, FB, aH, aL, hidden(FA // 2), n)

        def ffn_act(act, base, f, n, nf):
            for ng, nd in ((N_GUA, N_DNA), (N_GUB, N_DNB)):
                def body(i):
                    s = Slab(base, i, 2)
                    act.wait_ge(slab_done, s.plus(1))
                    S_.activation(sg[:], D[s.slot][:], ACT.Silu).then_inc(bank_free[s.slot], 1)
                    split_hi(act, s.next(2))
                    u = s.next()
                    act.wait_ge(bank_free[u.slot], u.prior(1))
                    S_.activation(aH[:, bass.ds(at(0, i, 2), 2), :], af[:], ACT.Copy).then_inc(aH_ready, 1)
                    split_hi(act, u.next(2))
                loop(act, ng // 2, body)
                if nd == N_DNA:
                    add_act(act, base + ng, nd)
                else:
                    final_act(act, base + ng, n, nf)
                base += ng + nd

        def ffn_dve(dve, base, f, gate):
            for part, (ng, nd) in enumerate(((N_GUA, N_DNA), (N_GUB, N_DNB))):
                def body(i):
                    s = Slab(base, i, 2)
                    u = s.next()
                    split_lo(dve, s.next(2))
                    dve.wait_ge(slab_done, u.plus(1))
                    dve.wait_ge(bank_free[s.slot], s.prior(1))
                    V_.tensor_tensor(af[:], sg[:], D[u.slot][:], ALU.mult).then_inc(bank_free[u.slot], 1)
                    dve.wait_ge(aH_ready, at(11 * f + part * FA // 2 + 1, i, 1))
                    two = bass.ds(at(0, i, 2), 2)
                    V_.tensor_tensor(aL[:, two, :], af[:], aH[:, two, :], ALU.subtract).then_inc(aL_ready, 1)
                    split_lo(dve, u.next(2))
                loop(dve, ng // 2, body)
                if nd == N_DNA:
                    add_dve(dve, base + ng, nd, 1, gate)
                else:
                    final_dve(dve, base + ng, gate)
                base += ng + nd

        ms = {n: sem("m_" + n) for n in ("ang", "trig", "sq", "ss", "rs", "cn", "cH", "cL", "ksw", "kr", "sw", "qr", "sc",
                                         "mx", "ex", "pn", "tr", "pt", "pv")}
        MS = (128 + 64) ** -0.5
        MAGIC = 12582912.0
        PI = float(np.float32(np.pi)) - 2.4e-7
        C1, C2 = 6.28125, 0.0019350051879882812
        C3 = 2 * np.pi - C1 - C2
        csq = (qn[:, 0], qn[:, 1], kn[:, 0], kn[:, 1], pT[:, 0])

        def angles_dve(dve, chain):
            L = chain.link
            dve.wait_ge(tab_in, 32)
            L(V_.tensor_copy(qr0[:], posi[:]))
            L(V_.tensor_scalar(qr0[:], qr0[:], vec[:, V["freq"]:V["freq"] + 1], None, ALU.mult))
            for dst, turn in ((msin, 0.0), (mcos, 0.25)):
                L(V_.tensor_scalar(qr[:], qr0[:], float(0.5 / np.pi), turn, ALU.mult, ALU.add))
                L(V_.tensor_scalar(qr[:], qr[:], MAGIC, None, ALU.add))
                L(V_.tensor_scalar(qr[:], qr[:], -MAGIC, None, ALU.add))
                L(V_.scalar_tensor_tensor(out=dst[:], in0=qr[:], scalar=-C1, in1=qr0[:], op0=ALU.mult, op1=ALU.add))
                L(V_.scalar_tensor_tensor(out=dst[:], in0=qr[:], scalar=-C2, in1=dst[:], op0=ALU.mult, op1=ALU.add))
                L(V_.scalar_tensor_tensor(out=dst[:], in0=qr[:], scalar=-C3, in1=dst[:], op0=ALU.mult, op1=ALU.add))
                L(V_.tensor_scalar(dst[:], dst[:], 2 * np.pi * turn, PI, ALU.add, ALU.min))
                V_.tensor_scalar(dst[:], dst[:], -PI, None, ALU.max).then_inc(ms["ang"], 1)

        def mla_in_pe(pe):
            product_first(pe, Slab(G_MIN), KC, 2, hH, hL, h_batch(pe, 3))
            for j in range(1, N_MIN):
                product(pe, Slab(G_MIN + j), KC, 2, hH, hL)
            for c in range(5):
                pe.wait_ge(ms["sq"], c + 1)
                last = T_.matmul(D[2][:, c // 3, :], ones, csq[c], start=(c in (0, 3)), stop=(c in (2, 4)))
            last.then_inc(ms["ss"], 1)
            pe.wait_ge(tab_in, 32)
            T_.matmul(D[3][:, 0, :], swp[:, 0:P], craw[:, 5, :], start=True, stop=True).then_inc(ms["ksw"], 1)
            pe.wait_ge(ms["cL"], 5)

        def mla_in_act(act):
            for j in range(N_MIN):
                s = Slab(G_MIN + j)
                act.wait_ge(slab_done, s.plus(1))
                S_.activation(craw[:, 2 * j:2 * j + 2], D[s.slot][:], ACT.Copy).then_inc(bank_free[s.slot], 1)
                if j + 2 <= N_MIN:
                    split_hi(act, s.next(2))
            for j in range(N_MIN):
                s = Slab(G_MIN + j)
                act.wait_ge(bank_free[s.slot], s.prior(1))
            for c in range(5):
                S_.activation(csq[c], craw[:, c, :], ACT.Square,
                              scale=(3 if c < 3 else 2) ** -0.5 * P ** -0.5).then_inc(ms["sq"], 1)
            act.wait_ge(ms["ss"], 1)
            S_.activation(pr[:], D[2][:], ACT.Ln, bias=eps).then_inc(ms["rs"], 1)
            act.wait_ge(ms["rs"], 1)
            S_.activation(pr[:], pr[:], ACT.Exp, scale=-0.5).then_inc(ms["rs"], 1)
            for c in range(5):
                act.wait_ge(ms["cn"], c + 1)
                S_.activation(cH[:, c, :], craw[:, c, :], ACT.Copy).then_inc(ms["cH"], 1)
            act.wait_ge(ms["ang"], 2)
            S_.activation(mcos[:], mcos[:], ACT.Sin).then_inc(ms["trig"], 1)
            S_.activation(msin[:], msin[:], ACT.Sin, scale=vec[:, V["freq"] + 1:V["freq"] + 2]).then_inc(ms["trig"], 1)

        def mla_in_dve(dve, chain):
            for j in range(2, N_MIN + 1):
                split_lo(dve, Slab(G_MIN + j))
            angles_dve(dve, chain)
            dve.wait_ge(ms["rs"], 2)
            gain = [vec[:, V["q_g"] + c:V["q_g"] + c + 1] for c in range(3)]
            gain += [vec[:, V["kv_g"] + c:V["kv_g"] + c + 1] for c in range(2)]
            for c in range(5):
                V_.scalar_tensor_tensor(out=craw[:, c, :], in0=craw[:, c, :], scalar=gain[c], in1=pr[:, c // 3, :],
                                        op0=ALU.mult, op1=ALU.mult).then_inc(ms["cn"], 1)
            for c in range(5):
                dve.wait_ge(ms["cH"], c + 1)
                V_.tensor_tensor(cL[:, c, :], craw[:, c, :], cH[:, c, :], ALU.subtract).then_inc(ms["cL"], 1)
            dve.wait_ge(ms["trig"], 2)
            dve.wait_ge(ms["ksw"], 1)
            chain.link(V_.tensor_tensor(krp[:], craw[:, 5, :], mcos[:], ALU.mult))
            chain.link(V_.tensor_tensor(qr0[:], D[3][:, 0, :], msin[:], ALU.mult))
            V_.tensor_tensor(krp[:], krp[:], qr0[:], ALU.add).then_inc(ms["kr"], 1)

        U = 2 * NT
        KV_W = 4 * P
        mxs, sums = small[:, 8:8 + U], small[:, 16:16 + U]

        def mla_pe(pe, hb):
            def q_product(s, between=None):
                product(pe, s, 3, 2, cH[:, 0:3], cL[:, 0:3], between)

            def body(p, last_pair=False):
                w = lambda n, k, per: pe.wait_ge(ms[n], at(k, p, per))
                s = Slab(G_MLA, p, PAIR)
                product(pe, s.next(1), 3, 1, cH[:, 0:3], cL[:, 0:3])
                product(pe, s.next(2), 2, 2, cH[:, 3:5], cL[:, 3:5])
                pe.wait_ge(bank_free[s.next(1).slot], s.next(1).prior(1))
                T_.matmul(D[2][:, 0, :], swp[:, 0:P], qr0[:], start=True, stop=True).then_inc(ms["sw"], 1)
                product_t(pe, s.next(3), 2, cH[:, 3:5], cL[:, 3:5])
                for k in (2, 3):
                    pe.wait_ge(bank_free[s.next(k).slot], s.next(k).prior(1))
                pe.wait_ge(ms["kr"], 1)
                w("qr", 1, 1)

                def steps(*us):
                    for u in us:
                        if u < U:
                            m, b = divmod(u, NT)
                            n = (b + 1) * P
                            if u >= 2:
                                w("ex", u - 1, U)
                            o = D[2][:, u % 2, 0:n]
                            T_.matmul(o, qn[:, m, b * P:b * P + P], kn[:, m, 0:n], start=True, stop=False)
                            T_.matmul(o, qr[64 * m:64 * m + 64, b * P:b * P + P], krp[64 * m:64 * m + 64, 0:n],
                                      start=False, stop=True).then_inc(ms["sc"], 1)
                        if 2 <= u < U + 2:
                            v = u - 2
                            w("pn", v + 1, U)
                            if v >= 2:
                                w("pt", v - 1, U)
                            for j in range(v % NT + 1):
                                last = T_.transpose(D[3][:, v % 2, j * P:j * P + P], pr[:, v % 2, j * P:j * P + P],
                                                    ident)
                            last.then_inc(ms["tr"], 1)
                        if u >= 3:
                            v = u - 3
                            m, b = divmod(v, NT)
                            w("pt", v + 1, U)
                            for j in range(b + 1):
                                last = T_.matmul(D[1][:, m, b * P:b * P + P], vt[:, j, m * P:m * P + P],
                                                 pT[:, v % 2, j * P:j * P + P], start=(j == 0), stop=(j == b))
                            last.then_inc(ms["pv"], 1)
                if last_pair:
                    steps(*range(U))
                else:
                    steps(0, 1, 2)
                    q_product(s.next(PAIR), {k: lambda u=k + 3: steps(u) for k in range(5)})
                steps(U, U + 1, U + 2)
                pe.wait_ge(h_ready, at(KC * hb + 2, p, 2))
            q_product(Slab(G_MLA))
            loop(pe, GH // 2 - 1, body)
            body(GH // 2 - 1, True)

        def mla_act(act):
            def body(p):
                w = lambda n, k, per: act.wait_ge(ms[n], at(k, p, per))
                for k in range(PAIR):
                    s = Slab(G_MLA + k, p, PAIR)
                    if k == 2:
                        split_hi(act, s.next(2))
                        continue
                    act.wait_ge(slab_done, s.plus(1))
                    if k == 0:
                        last = S_.activation(qn[:], D[s.slot][:], ACT.Copy)
                    elif k == 1:
                        last = S_.activation(qr0[:], D[s.slot][:, 0, :], ACT.Copy)
                    else:
                        last = S_.activation(vt[:].rearrange("p t n -> p (t n)"),
                                             D[s.slot].rearrange("p a n -> p (a n)"), ACT.Copy)
                    last.then_inc(bank_free[s.slot], 1)
                    split_hi(act, s.next(2), KV_W if k < 2 else SLAB)
                for u in range(U + 1):
                    if u < U:
                        n = (u % NT + 1) * P
                        w("mx", u + 1, U)
                        if u >= 2:
                            w("tr", u - 1, U)
                        S_.activation(pr[:, u % 2, 0:n], D[2][:, u % 2, 0:n], ACT.Exp, bias=mxs[:, u:u + 1], scale=MS,
                                      accum_out=sums[:, u:u + 1]).then_inc(ms["ex"], 1)
                    if u >= 1:
                        v = u - 1
                        n = (v % NT + 1) * P
                        w("tr", v + 1, U)
                        if v >= 2:
                            w("pv", v - 1, U)
                        S_.activation(pT[:, v % 2, 0:n], D[3][:, v % 2, 0:n], ACT.Copy).then_inc(ms["pt"], 1)
                w("pv", U, U)
                S_.activation(hH[:, bass.ds(at(0, p, 2), 2), :], D[1][:], ACT.Copy).then_inc(hh_ready, 2)
            loop(act, GH // 2, body)

        def mla_dve(dve, chain, hb):
            def body(p):
                L = chain.link
                w = lambda n, k, per: dve.wait_ge(ms[n], at(k, p, per))
                for k in range(PAIR):
                    s = Slab(G_MLA + k, p, PAIR)
                    if k == 2:
                        dve.wait_ge(slab_done, s.plus(1))
                        V_.tensor_copy(kn[:], D[s.slot][:]).then_inc(bank_free[s.slot], 1)
                    if k < 2:
                        split_lo(dve, s.next(2), KV_W)
                w("sw", 1, 1)
                V_.tensor_tensor(qr[:], qr0[:], mcos[:], ALU.mult)
                L(V_.tensor_tensor(craw[:, 5, :], D[2][:, 0, :], msin[:], ALU.mult))
                V_.tensor_tensor(qr[:], qr[:], craw[:, 5, :], ALU.add).then_inc(ms["qr"], 1)
                for u in range(U + 1):
                    if u < U:
                        b = u % NT
                        w("sc", u + 1, U)
                        dg = D[2][:, u % 2, b * P:b * P + P]
                        L(V_.tensor_tensor(dg, dg, caus, ALU.add))
                        L(V_.reduce_max(mxs[:, u:u + 1], D[2][:, u % 2, 0:(b + 1) * P], AX.X))
                        V_.tensor_scalar(mxs[:, u:u + 1], mxs[:, u:u + 1], -MS, None, ALU.mult).then_inc(ms["mx"], 1)
                    if u in (1, 5):
                        split_lo(dve, Slab(G_MLA + PAIR + u // 5, p, PAIR))
                    if u >= 1:
                        v = u - 1
                        n = (v % NT + 1) * P
                        w("ex", v + 1, U)
                        L(V_.reciprocal(sums[:, v:v + 1], sums[:, v:v + 1]))
                        V_.tensor_scalar(pr[:, v % 2, 0:n], pr[:, v % 2, 0:n], sums[:, v:v + 1], None,
                                         ALU.mult).then_inc(ms["pn"], 1)
                dve.wait_ge(hh_ready, at(KC * hb + 2, p, 2))
                two = bass.ds(at(0, p, 2), 2)
                V_.tensor_tensor(hL[:, two, :], D[1][:], hH[:, two, :], ALU.subtract).then_inc(h_ready, 2)
            loop(dve, GH // 2, body, chain, 1 + 3 * U)

        rs_ = {n: sem("r_" + n) for n in ("sw", "rot", "kt", "sc", "a", "ds", "st", "y", "yc", "mu", "c", "sq", "var",
                                          "rs", "o", "H", "L")}
        HS = 3
        b_col = lambda o, i=None, step=0: vec[:, bass.ds(at(V["b_in"] + o, i, step), 1)]
        pairs = lambda ap: ap.unsqueeze(1).to_broadcast([P, 2, T])

        def rope_dve(chain, dst, raw_, cos_, sin_):
            V_.tensor_tensor(dst[:], raw_[:], pairs(cos_), ALU.mult)
            chain.link(V_.tensor_tensor(tm2[:], D[2][:], pairs(sin_), ALU.mult))
            return V_.tensor_tensor(dst[:], dst[:], tm2[:], ALU.add)

        def ret_pe(pe):
            def body(i):
                for m in range(2):
                    w = lambda n, k=1, per=1: pe.wait_ge(rs_[n], at(m * per + k, i, 2 * per))
                    s = Slab(G_RET + HS * m, i, 2 * HS)

                    def swap():
                        pe.wait_ge(bank_free[s.slot], s.prior(1))
                        for e in range(2):
                            last = T_.matmul(D[2][:, e, :], swp[:, P:2 * P], qk[:, e, :], start=True, stop=True)
                        last.then_inc(rs_["sw"], 1)

                    def over_features(a, src, b):
                        w(a)
                        for e in range(2):
                            last = T_.matmul(D[3][:, 1, :], ones, src[:, e, :], start=(e == 0), stop=(e == 1))
                        last.then_inc(rs_[b], 1)
                    product_t(pe, s.next(1), KC, hH, hL, between={1: swap})
                    w("rot")
                    for t in range(NT):
                        c = slice(t * P, t * P + P)
                        last = T_.transpose(D[3][:, 0, c], kq[:, 1, c], ident)
                    last.then_inc(rs_["kt"], 1)
                    for t in range(NT):
                        c = slice(t * P, t * P + P)
                        last = T_.matmul(D[3][:, 1, c], kq[:, 1, c], kq[:, 0, c], start=True, stop=True)
                    last.then_inc(rs_["sc"], 1)
                    product(pe, s.next(2), KC, 2, hH, hL)
                    pe.wait_ge(bank_free[s.next(1).slot], s.next(1).prior(1))
                    w("a")
                    for t in range(NT):
                        c = slice(t * P, t * P + P)
                        if t < NT - 1:
                            if t:
                                w("st", t, NT - 1)
                            T_.matmul(D[3][:, 0, 0:2 * P], ka[:, 0, c], rvt[:, t, :], start=True,
                                      stop=True).then_inc(rs_["ds"], 1)
                        elif t:
                            w("st", t, NT - 1)
                        for e in range(2):
                            o = D[2][:, e, c]
                            if t:
                                T_.matmul(o, rst[:, (t - 1) % 2, e * P:e * P + P], qde[:, c], start=True, stop=False)
                            last = T_.matmul(o, rvt[:, t, e * P:e * P + P], ka[:, 1, c], start=(t == 0), stop=True)
                    last.then_inc(rs_["y"], 1)
                    product(pe, s.next(3), KC, 2, hH, hL, {3: lambda: over_features("yc", ry, "mu"),
                                                           11: lambda: over_features("sq", rsq, "var")})
            product_first(pe, Slab(G_RET), KC, 2, hH, hL, h_batch(pe, 6))
            loop(pe, 2, body)
            pe.wait_ge(rs_["L"], 4)

        def ret_act(act):
            def body(i):
                for m in range(2):
                    w = lambda n, k=1, per=1: act.wait_ge(rs_[n], at(m * per + k, i, 2 * per))
                    s = Slab(G_RET + HS * m, i, 2 * HS)
                    act.wait_ge(slab_done, s.plus(1))
                    for e in range(2):
                        last = S_.activation(qk[:, e, :], D[s.slot][:, e, :], ACT.Identity, bias=b_col(4 * m + e, i, 8))
                    last.then_inc(bank_free[s.slot], 1)
                    split_hi(act, s.next(2))
                    split_hi(act, s.next(3))
                    g = s.next(2)
                    act.wait_ge(slab_done, g.plus(1))
                    for e in range(2):
                        last = S_.activation(rg[:, e, :], D[g.slot][:, e, :], ACT.Silu, bias=b_col(4 * m + 2 + e, i, 8))
                    last.then_inc(bank_free[g.slot], 1)
                    w("y")
                    S_.activation(ry[:], D[2][:], ACT.Copy).then_inc(rs_["yc"], 1)
                    split_hi(act, s.next(4))
                    w("c")
                    S_.activation(rsq[:], ry[:], ACT.Square, scale=1 / 16).then_inc(rs_["sq"], 1)
                    w("var")
                    S_.activation(tm2[:, 0, :], D[3][:, 1, :], ACT.Ln, bias=eps).then_inc(rs_["rs"], 1)
                    w("rs", 1, 2)
                    S_.activation(tm2[:, 0, :], tm2[:, 0, :], ACT.Exp, scale=-0.5).then_inc(rs_["rs"], 1)
                    w("o")
                    S_.activation(rH[:, bass.ds(at(2 * m, i, 4), 2), :], ry[:], ACT.Copy).then_inc(rs_["H"], 1)
            loop(act, 2, body)

        def ret_dve(dve, chain):
            def body(i):
                L = chain.link
                for m in range(2):
                    w = lambda n, k=1, per=1: dve.wait_ge(rs_[n], at(m * per + k, i, 2 * per))
                    s = Slab(G_RET + HS * m, i, 2 * HS)
                    head = lambda ap: ap.rearrange("p (h n) -> p h n", n=P)[:, bass.ds(at(m, i, 2), 1), :]
                    split_lo(dve, s.next(2))
                    w("sw")
                    dve.wait_ge(bank_free[s.slot], s.prior(1))
                    rope_dve(chain, kq, qk, rcos, rsin).then_inc(rs_["rot"], 1)
                    w("rot")
                    V_.tensor_tensor(qde[:].rearrange("p (t n) -> p t n", t=NT),
                                     kq[:, 0, :].rearrange("p (t n) -> p t n", t=NT),
                                     head(qdec).to_broadcast([P, NT, P]), ALU.mult)
                    v = s.next(1)
                    dve.wait_ge(slab_done, v.plus(1))
                    vbh = vb[:, bass.ds(at(2 * P * m, i, 4 * P), 2 * P)].unsqueeze(1).to_broadcast([P, NT, 2 * P])
                    V_.tensor_tensor(rvt[:], D[v.slot].rearrange("p a (b n) -> p (a b) n", b=2), vbh,
                                     ALU.add).then_inc(bank_free[v.slot], 1)
                    split_lo(dve, s.next(3))
                    w("kt")
                    w("sc")
                    V_.tensor_scalar(ka[:, 0, :], D[3][:, 0, :], vec[:, bass.ds(at(V["kdec"] + m, i, 2), 1)], None,
                                     ALU.mult)
                    V_.tensor_tensor(ka[:, 1, :].rearrange("p (t n) -> p t n", t=NT),
                                     D[3][:, 1, :].rearrange("p (t n) -> p t n", t=NT),
                                     head(intra).to_broadcast([P, NT, P]), ALU.mult).then_inc(rs_["a"], 1)
                    for t in range(NT - 1):
                        w("ds", t + 1, NT - 1)
                        if t == 0:
                            V_.tensor_copy(rst[:, 0, :], D[3][:, 0, 0:2 * P]).then_inc(rs_["st"], 1)
                        else:
                            V_.scalar_tensor_tensor(out=rst[:, t % 2, :], in0=rst[:, (t - 1) % 2, :],
                                                    scalar=vec[:, bass.ds(at(V["cdec"] + m, i, 2), 1)],
                                                    in1=D[3][:, 0, 0:2 * P], op0=ALU.mult,
                                                    op1=ALU.add).then_inc(rs_["st"], 1)
                        w("st", t + 1, NT - 1)
                    w("mu")
                    V_.scalar_tensor_tensor(out=ry[:], in0=D[3][:, 1:2, :].to_broadcast([P, 2, T]), scalar=-1 / 256,
                                            in1=ry[:], op0=ALU.mult, op1=ALU.add).then_inc(rs_["c"], 1)
                    split_lo(dve, s.next(4))
                    w("rs", 2, 2)
                    for e in range(2):
                        last = V_.scalar_tensor_tensor(out=rsq[:, e, :], in0=ry[:, e, :],
                                                       scalar=vec[:, bass.ds(at(V["ret_g"] + 2 * m + e, i, 4), 1)],
                                                       in1=tm2[:, 0, :], op0=ALU.mult, op1=ALU.mult)
                    L(last)
                    V_.tensor_tensor(ry[:], rsq[:], rg[:], ALU.mult).then_inc(rs_["o"], 1)
                    w("H")
                    two = bass.ds(at(2 * m, i, 4), 2)
                    V_.tensor_tensor(rL[:, two, :], ry[:], rH[:, two, :], ALU.subtract).then_inc(rs_["L"], 1)
            loop(dve, 2, body, chain, 4)

        def merge_pe(pe, base, H, L):
            def body(i):
                product(pe, Slab(base + 1, i, 2), KC, 2, H, L)
                product(pe, Slab(base + 2, i, 2), KC, 2, hH, hL)
            loop(pe, N_OUT - 1, body)
            product(pe, Slab(base + 2 * N_OUT - 1), KC, 2, H, L)

        def merge_act(act, base, bias0):
            def body(i):
                s = Slab(base, i, 2)
                u = s.next()
                act.wait_ge(slab_done, s.plus(1))
                for m in range(2):
                    last = S_.activation(qk[:, m, :], D[s.slot][:, m, :], ACT.Sigmoid, bias=b_col(bias0 + m, i, 2))
                last.then_inc(bank_free[s.slot], 1)
                split_hi(act, u.next())
                act.wait_ge(bank_free[u.slot], u.prior(1))
                split_hi(act, u.next(2))
            loop(act, N_OUT, body)

        def merge_dve(dve, chain, base, add):
            def body(i):
                s = Slab(base, i, 2)
                u = s.next()
                split_lo(dve, u.next())
                dve.wait_ge(slab_done, u.plus(1))
                dve.wait_ge(bank_free[s.slot], s.prior(1))
                two = mg[:, bass.ds(at(0, i, 2), 2), :]
                if add:
                    chain.link(V_.tensor_tensor(tm2[:], qk[:], D[u.slot][:], ALU.mult))
                    V_.tensor_tensor(two, two, tm2[:], ALU.add).then_inc(bank_free[u.slot], 1)
                else:
                    V_.tensor_tensor(two, qk[:], D[u.slot][:], ALU.mult).then_inc(bank_free[u.slot], 1)
                split_lo(dve, u.next(2))
            loop(dve, N_OUT, body, chain, int(add))

        as_ = {n: sem("a_" + n) for n in ("sw", "kk", "stage", "qr", "sc", "mx", "ex", "pn", "tr", "pt", "pv", "H", "L")}
        kks, kst, av, vst, ptb = rg, qde, rvt, rst[:, 0, :].rearrange("p (t n) -> p t n", t=NT), ka
        four = lambda t_: t_[:].rearrange("p a (b n) -> p (a b) n", b=2)
        AS = 64 ** -0.5
        AU = 4

        def kv_pe(pe):
            s = Slab(G_KV)
            product(pe, s, KC, 2, hH, hL)
            pe.wait_ge(bank_free[s.slot], s.prior(1))
            for e in range(2):
                last = T_.matmul(D[2][:, e, :], swp[:, 0:P], qk[:, e, :], start=True, stop=True)
            last.then_inc(as_["sw"], 1)
            product_t(pe, s.next(), KC, hH, hL, P)

        def kv_act(act):
            s = Slab(G_KV)
            act.wait_ge(slab_done, s.plus(1))
            for e in range(2):
                last = S_.activation(qk[:, e, :], D[s.slot][:, e, :], ACT.Identity, bias=b_col(24 + e))
            last.then_inc(bank_free[s.slot], 1)
            split_hi(act, s.next(2))

        def kv_dve(dve, chain):
            s = Slab(G_KV)
            dve.wait_ge(as_["sw"], 1)
            rope_dve(chain, kks, qk, acos, asin).then_inc(as_["kk"], 1)
            split_lo(dve, s.next(2))
            dve.wait_ge(slab_done, s.plus(2))
            V_.tensor_tensor(av[:, :, 0:P], D[s.next().slot].rearrange("p a (b n) -> p (a b) n", b=2)[:, :, 0:P],
                             vb[:, 8 * P:9 * P].unsqueeze(1).to_broadcast([P, NT, P]),
                             ALU.add).then_inc(bank_free[s.next().slot], 1)
            dve.wait_ge(as_["kk"], 1)
            dve.wait_ge(bank_free[s.next().slot], s.next().prior(1))

        sco, prb = (ry, tm2), (rsq, qk)
        amx, asum, aes = ([small[:, c + 4 * k:c + 4 * k + 4] for k in range(2)] for c in (24, 32, 40))

        def swa_pe(pe):
            def body(i):
                pe.wait_ge(as_["stage"], at(1, i, 1))
                for j in range(2):
                    w = lambda n, k=1, per=1: pe.wait_ge(as_[n], at(j * per + k, i, 2 * per))
                    s = Slab(G_AQ + j, i, 2)
                    pe.wait_ge(bank_free[s.slot], s.prior(1))
                    for e in range(2):
                        last = T_.matmul(D[2][:, e, :], swp[:, 0:P], qk[:, e, :], start=True, stop=True)
                    last.then_inc(as_["sw"], 1)

                    def scores(v):
                        if v:
                            w("mx", v, AU)
                        else:
                            w("qr")
                        m, hh = divmod(v, 2)
                        half = slice(64 * hh, 64 * hh + 64)
                        for b in range(NT):
                            k0 = max(b - 1, 0) * P
                            last = T_.matmul(four(D[3])[:, b, :], kq[half, m, b * P:b * P + P],
                                             kst[half, k0:k0 + 2 * P], start=True, stop=True)
                        last.then_inc(as_["sc"], 1)

                    def turn(v):
                        w("pn", v + 1, AU)
                        if v:
                            w("pt", v, AU)
                        for b in range(NT):
                            for k in range(2):
                                last = T_.transpose(four(D[2])[:, b, k * P:k * P + P],
                                                    four(prb[v % 2])[:, b, k * P:k * P + P], ident)
                        last.then_inc(as_["tr"], 1)

                    def values(v):
                        w("pt", v + 1, AU)
                        m, hh = divmod(v, 2)
                        for b in range(NT):
                            k0 = max(b - 1, 0)
                            for k in range(2 if b else 1):
                                last = T_.matmul(D[s.slot][64 * hh:64 * hh + 64, m, b * P:b * P + P],
                                                 vst[:, k0 + k, 0:64], four(ptb)[:, b, k * P:k * P + P],
                                                 start=(k == 0), stop=(k == (1 if b else 0)))
                        last.then_inc(as_["pv"], 1)
                    product(pe, s.next(), KC, 2, hH, hL, {5: lambda: scores(0), 10: lambda: scores(1),
                                                          15: lambda: scores(2)})
                    turn(0)
                    values(0)
                    scores(3)
                    turn(1)
                    values(1)
                    turn(2)
                    values(2)
                    turn(3)
                    values(3)
                    if j == 0:
                        w("L")
            product(pe, Slab(G_AQ), KC, 2, hH, hL)
            loop(pe, 2, body)
            pe.wait_ge(as_["L"], 4)

        def swa_act(act):
            def body(i):
                for j in range(2):
                    w = lambda n, k=1, per=1: act.wait_ge(as_[n], at(j * per + k, i, 2 * per))
                    s = Slab(G_AQ + j, i, 2)
                    act.wait_ge(slab_done, s.plus(1))
                    for e in range(2):
                        last = S_.activation(qk[:, e, :], D[s.slot][:, e, :], ACT.Identity,
                                             bias=b_col(26 + 2 * j + e, i, 4))
                    last.then_inc(bank_free[s.slot], 1)
                    split_hi(act, s.next(2))

                    def exps(v):
                        sink = vec[:, bass.ds(at(V["sink"] + 4 * j + v, i, 8), 1)]
                        k = v % 2
                        w("mx", v + 1, AU)
                        if v >= 2:
                            w("tr", v - 1, AU)
                        for b in range(NT):
                            S_.activation(four(prb[k])[:, b, :], four(sco[k])[:, b, :], ACT.Exp,
                                          bias=amx[k][:, b:b + 1], accum_out=asum[k][:, b:b + 1])
                        S_.activation(aes[k], amx[k], ACT.Exp, bias=sink).then_inc(as_["ex"], 1)
                    exps(0)
                    for v in range(AU):
                        if v < AU - 1:
                            exps(v + 1)
                        w("tr", v + 1, AU)
                        if v:
                            w("pv", v, AU)
                        S_.activation(ptb[:], D[2][:], ACT.Copy).then_inc(as_["pt"], 1)
                    w("pv", AU, AU)
                    S_.activation(rH[:, bass.ds(at(2 * j, i, 4), 2), :], D[s.slot][:], ACT.Copy).then_inc(as_["H"], 1)
            split_hi(act, Slab(G_AQ + 1))
            loop(act, 2, body)

        def swa_dve(dve, chain):
            def body(i):
                L = chain.link
                V_.tensor_copy(kst[:], kks[:, bass.ds(i, 1), :].rearrange("p a n -> p (a n)"))
                V_.tensor_scalar(vst, av[:, :, bass.ds(at(0, i, 64), 64)], 1.0, None,
                                 ALU.mult).then_inc(as_["stage"], 1)
                for j in range(2):
                    w = lambda n, k=1, per=1: dve.wait_ge(as_[n], at(j * per + k, i, 2 * per))
                    s = Slab(G_AQ + j, i, 2)
                    dve.wait_ge(bank_free[s.slot], s.prior(1))
                    dve.wait_ge(as_["sw"], at(j + 2, i, 2))
                    rope_dve(chain, kq, qk, acos, asin).then_inc(as_["qr"], 1)
                    w("qr")
                    w1 = win[:, 2 * P:4 * P]

                    def maxima(v):
                        sink = vec[:, bass.ds(at(V["sink"] + 4 * j + v, i, 8), 1)]
                        k = v % 2
                        w("sc", v + 1, AU)
                        if v >= 2:
                            w("ex", v - 1, AU)
                        sc4 = four(sco[k])
                        V_.scalar_tensor_tensor(out=sc4[:, 0, :], in0=four(D[3])[:, 0, :], scalar=AS,
                                                in1=win[:, 0:2 * P], op0=ALU.mult, op1=ALU.add)
                        L(V_.scalar_tensor_tensor(out=sc4[:, 1:4, :], in0=four(D[3])[:, 1:4, :], scalar=AS,
                                                  in1=w1.unsqueeze(1).to_broadcast([P, 3, 2 * P]), op0=ALU.mult,
                                                  op1=ALU.add))
                        L(V_.reduce_max(amx[k], sc4, AX.X))
                        V_.tensor_scalar(amx[k], amx[k], sink, -1.0, ALU.max, ALU.mult).then_inc(as_["mx"], 1)
                    maxima(0)
                    for v in range(AU):
                        if v < AU - 1:
                            maxima(v + 1)
                        k = v % 2
                        w("ex", v + 1, AU)
                        L(V_.tensor_tensor(asum[k], asum[k], aes[k], ALU.add))
                        L(V_.reciprocal(asum[k], asum[k]))
                        V_.tensor_tensor(four(prb[k]), four(prb[k]), asum[k].unsqueeze(2).to_broadcast([P, NT, 2 * P]),
                                         ALU.mult).then_inc(as_["pn"], 1)
                        if v == 0:
                            split_lo(dve, s.next(2))
                    w("H")
                    two = bass.ds(at(2 * j, i, 4), 2)
                    V_.tensor_tensor(rL[:, two, :], D[s.slot][:], rH[:, two, :], ALU.subtract).then_inc(as_["L"], 1)
            split_lo(dve, Slab(G_AQ + 1))
            loop(dve, 2, body, chain, 2 * (1 + 4 * AU))

        block = ctx.enter_context(nc.Block())
        gate_col = lambda layer, part: lambda c: mod[:, bass.ds(c + MD(layer, part), 1)]
        col = lambda t_, o: lambda c: t_[:, o + c:o + c + 1]
        zero = lambda c: vec[:, V["zero"]:V["zero"] + 1]

        @block.sync
        def _(sp):
            sp.dma_start(vec[:], vecs[:, :]).then_inc(vec_in, 16)
            load_ada(sp, Slab(0))
            load_ada(sp, Slab(1))
            sp.dma_start(cst[:], consts[:, :]).then_inc(x_in, 16)
            sp.dma_start(x[:], xin[:, :, :]).then_inc(x_in, 16)
            sp.dma_start(lvl[:], masks[:, :]).then_inc(x_in, 16)
            load_slab(sp, Slab(0))
            sp.dma_start(posi[:], pos[0:1, :].to_broadcast([P, T])).then_inc(tab_in, 16)
            sp.dma_start(swp[:], rope[:, 0:2 * P]).then_inc(tab_in, 16)
            for a in range(2, ADA0):
                load_ada(sp, Slab(a))
            load_slab(sp, Slab(1))

            def both(g, a, n, per, ada_per):
                def body(i):
                    k = 0
                    for j in range(per):
                        load_slab(sp, Slab(g + j, i, per))
                        for _ in range(ada_per[j]):
                            load_ada(sp, Slab(a + k, i, sum(ada_per)))
                            k += 1
                loop(sp, n, body)

            def alone(g, n):
                def body(i):
                    for j in range(2):
                        load_slab(sp, Slab(g + j, i, 2))
                loop(sp, n // 2, body)
                if n % 2:
                    load_slab(sp, Slab(g + n - 1))
            both(2, ADA0, GH // 2, PAIR, (0, 1, 2, 5))
            alone(2 + N_GDN, N_OUT)
            ada1 = ADA0 + GH // 2 * ADA_P
            both(G_FFN0 + 1, ada1, (2 * ADA_L - ada1) // 2, 4, (0, 1, 0, 1))
            g = G_FFN0 + 1 + 2 * (2 * ADA_L - ada1)
            alone(g, G_RET + 1 - g)
            x_written(sp, G_RET)
            sp.dma_start(tab[:], rope[:, 2 * P:2 * P + TAB]).then_inc(tab_in, 16)
            sp.dma_start(vb[:], vbias[0:1, :].to_broadcast([P, 9 * P])).then_inc(tab_in, 16)
            alone(G_RET + 1, N_SLABS + 1 - (G_RET + 1))
            sp.wait_ge(xg_ready, 8 * KC)
            sp.dma_start(out[:, :, :], x[:]).then_inc(out_done, 16)
            sp.wait_ge(out_done, 16)

        @block.tensor
        def _(pe):
            pe.wait_ge(x_in, 48)
            norm_pe(pe, 0, sq)
            for a in range(ADA0):
                pe.wait_ge(ada_sum_v, a + 1)
                ada_pe(pe, Slab(a))
            product_first(pe, Slab(G_AB), KC, 2, hH, hL, h_batch(pe, 0))
            rows_pe(pe)
            gdn_pe(pe)
            final_pe(pe, G_GOUT, KC, hH, hL, h_batch(pe, 1), 1)
            ffn_pe(pe, G_FFN0, 0, 2, 2, ADA0 + GH // 2 * ADA_P)
            mla_in_pe(pe)
            mla_pe(pe, 4)
            final_pe(pe, G_MOUT, KC, hH, hL, h_batch(pe, 4), 3)
            ffn_pe(pe, G_FFN1, 1, 5, 4)
            norm_pe(pe, 5, ry)
            ret_pe(pe)
            merge_pe(pe, G_GR, rH, rL)
            kv_pe(pe)
            swa_pe(pe)
            merge_pe(pe, G_GA, rH, rL)
            final_pe(pe, G_ROUT, KC, hH, hL, h_batch(pe, 7), 6)
            ffn_pe(pe, G_FFN2, 2, 8, 7)

        @block.gpsimd
        def _(pool):
            chain = Chain(pool, pool_chain)
            pool.wait_ge(cact_ready, 1)
            ada_pool(pool, chain)

        @block.scalar
        def _(act):
            act.wait_ge(vec_in, 16)
            S_.activation(cact[:], vec[:, V["c"]:V["c"] + KC], ACT.Silu).then_inc(cact_ready, 1)
            act.wait_ge(x_in, 48)
            for c in range(KC):
                square(act, 0, sq, c)
            split_hi(act, Slab(0))
            norm_act(act, 0, kb[:, 0, :], sq[:, 2:4], col(mod, MD(0, 0)), then=1)
            rows_act(act)
            gdn_act(act)
            act.wait_ge(gg["of"], GH // 2 + 1)
            to_h_act(act, go)
            split_hi(act, Slab(G_GOUT + 1))
            final_act(act, G_GOUT, 1, 0)
            norm_act(act, 1, nrs[:], af, col(mod, MD(0, 3)), then=G_FFN0 + 1)
            ffn_act(act, G_FFN0, 0, 2, 1)
            norm_act(act, 2, mrs[:], ntm, col(mod, MD(1, 0)), then=G_MIN + 1)
            mla_in_act(act)
            split_hi(act, Slab(G_MLA + 1))
            mla_act(act)
            final_act(act, G_MOUT, 3, 2)
            norm_act(act, 3, nrs[:], af, col(mod, MD(1, 3)), then=G_FFN1 + 1)
            ffn_act(act, G_FFN1, 1, 4, 3)
            norm_act(act, 4, nrs[:], None, None, to_h=False)
            for c in range(KC):
                act.wait_ge(xg_ready, KC * 4 + c + 1)
                square(act, 5, ry, c)
            norm_act(act, 5, rst[:].rearrange("p a n -> p (a n)"), rsq, zero, then=G_RET + 1)
            act.wait_ge(tab_in, 64)
            ret_act(act)
            merge_act(act, G_GR, 16)
            kv_act(act)
            swa_act(act)
            merge_act(act, G_GA, 34)
            to_h_act(act, mg)
            final_act(act, G_ROUT, 6, 4)
            norm_act(act, 6, nrs[:], af, zero, then=G_FFN2 + 1)
            ffn_act(act, G_FFN2, 2, 7, 5)
            norm_act(act, 7, nrs[:], None, None, to_h=False)

        @block.vector
        def _(dve):
            chain = Chain(dve, dve_chain)
            dve.wait_ge(vec_in, 16)
            dve.wait_ge(cact_ready, 1)
            for a in range(ADA0):
                ada_chunks(dve, V_, chain, Slab(a), slice(0, ADA_V), ada_sum_v)
            dve.wait_ge(x_in, 48)
            split_lo(dve, Slab(0))
            mod_dve(dve, chain, 0, 2 * KC, ADA0)
            dve.wait_ge(mod_ready, 1)
            gain_cols(chain, 0, "mix_g", 0, 1)
            norm_dve(dve, 0, 0, kb[:, 0, :], sq[:, 2:4], col(gsc, 0), col(mod, MD(0, 0)), 1)
            rows_dve(dve, chain)
            gdn_dve(dve, chain)
            mod_dve(dve, chain, 2 * KC, 6 * KC, ADA0 + GH // 2 * ADA_P)
            dve.wait_ge(mod_ready, 2)
            gain_cols(chain, 1, "ffn_g", 0, 4)
            to_h_dve(dve, 1, go)
            split_lo(dve, Slab(G_GOUT + 1))
            final_dve(dve, G_GOUT, gate_col(0, 2))
            norm_dve(dve, 1, 2, nrs[:], af, col(gsc, KC), col(mod, MD(0, 3)), G_FFN0 + 1)
            ffn_dve(dve, G_FFN0, 0, gate_col(0, 5))
            mod_dve(dve, chain, 6 * KC, 12 * KC, 2 * ADA_L)
            dve.wait_ge(mod_ready, 3)
            gain_cols(chain, 2, "mix_g", 1, 1)
            gain_cols(chain, 3, "ffn_g", 1, 4)
            norm_dve(dve, 2, 3, mrs[:], ntm, col(gsc, 2 * KC), col(mod, MD(1, 0)), G_MIN + 1)
            mla_in_dve(dve, chain)
            split_lo(dve, Slab(G_MLA + 1))
            mla_dve(dve, chain, 4)
            final_dve(dve, G_MOUT, gate_col(1, 2))
            norm_dve(dve, 3, 5, nrs[:], af, col(gsc, 3 * KC), col(mod, MD(1, 3)), G_FFN1 + 1)
            ffn_dve(dve, G_FFN1, 1, gate_col(1, 5))
            norm_x_dve(dve, 4, nrs[:], col(vec, V["fin_g"]))
            norm_dve(dve, 5, 6, rst[:].rearrange("p a n -> p (a n)"), rsq, col(vec, V["ln1"]), zero, G_RET + 1)
            dve.wait_ge(tab_in, 64)
            ret_dve(dve, chain)
            merge_dve(dve, chain, G_GR, False)
            kv_dve(dve, chain)
            swa_dve(dve, chain)
            merge_dve(dve, chain, G_GA, True)
            to_h_dve(dve, 7, mg)
            final_dve(dve, G_ROUT, None)
            norm_dve(dve, 6, 8, nrs[:], af, col(vec, V["ln2"]), zero, G_FFN2 + 1)
            ffn_dve(dve, G_FFN2, 2, None)
            norm_x_dve(dve, 7, nrs[:], col(vec, V["lnf"]))


def _slab(cols):
    k, n = cols.shape
    a = cols.reshape(k // P, P, n).transpose(1, 0, 2).reshape(P, -1)
    return np.pad(a, ((0, 0), (0, SLAB - a.shape[1])))


def _cols(w, n=2 * P):
    return [_slab(w[:, c:c + n]) for c in range(0, w.shape[1], n)]


def _ffn(wg, wu, wd):
    out = []
    for lo_, hi_ in ((0, FA), (FA, FA + FB)):
        g, u = (_cols(w[:, lo_ * P:hi_ * P]) for w in (wg, wu))
        for a, b in zip(g, u):
            out += [a, b]
        out += _cols(wd[lo_ * P:hi_ * P], P if lo_ == 0 else 2 * P)
    return out


def _slabs(i):
    w = i["gdn_w_in"][0]
    ab = np.zeros((DM, 2 * P), np.float32)
    ab[:, 0:GH] = w[:, 4096:4096 + GH]
    ab[:, P:P + GH] = w[:, 4096 + GH:4096 + 2 * GH]
    out = [_slab(ab)]
    for p in range(GH // 2):
        out += [_slab(w[:, j * DM + p * 256:j * DM + p * 256 + 256]) for j in range(4)]
    out += _cols(i["gdn_w_out"][0])
    out += _ffn(i["ffn_w_gate"][0], i["ffn_w_up"][0], i["ffn_w_down"][0])
    w = i["mla_w_in"][0]
    out += _cols(np.concatenate([w, w[:, 640:704]], 1))
    uq = i["mla_w_uq"][0].reshape(384, GH, 192)
    ukv = i["mla_w_ukv"][0].reshape(256, GH, 256)
    for p in range(0, GH, 2):
        out += [_slab(uq[:, p:p + 2, 0:128].reshape(384, 256)), _slab(uq[:, p:p + 2, 128:192].reshape(384, 128)),
                _slab(ukv[:, p:p + 2, 0:128].reshape(256, 256)), _slab(ukv[:, p:p + 2, 128:256].reshape(256, 256))]
    out += _cols(i["mla_w_out"][0])
    out += _ffn(i["ffn_w_gate"][1], i["ffn_w_up"][1], i["ffn_w_down"][1])
    w = i["w_in_2"][0]
    for h in range(4):
        qk = np.concatenate([w[:, h * P:h * P + P], w[:, 512 + h * P:512 + h * P + P]], 1)
        out += [_slab(qk), _slab(w[:, 1024 + 256 * h:1280 + 256 * h]), _slab(w[:, 2048 + 256 * h:2304 + 256 * h])]
    ga, ro = _cols(w[:, 4352:5376]), _cols(i["w_ret_out_2"][0])
    for a, b in zip(ga, ro):
        out += [a, b]
    k0, k1 = w[:, 4096:4160], w[:, 4160:4224]
    out += [_slab(np.concatenate([k0, k0, k1, k1], 1)), _slab(np.pad(w[:, 4224:4352], ((0, 0), (0, P))))]
    out += _cols(w[:, 3072:4096])
    gb, ao = _cols(w[:, 5376:6400]), _cols(i["w_attn_out_2"][0])
    for a, b in zip(gb, ao):
        out += [a, b]
    out += _cols(i["w_out_2"][0])
    out += _ffn(i["w_ffn_gate_2"][0], i["w_ffn_up_2"][0], i["w_ffn_down_2"][0])
    out += [np.zeros((P, SLAB), np.float32)]
    assert len(out) == N_SLABS + 1, (len(out), N_SLABS)
    return np.stack(out)


def _vectors(i):
    col = lambda a: np.ascontiguousarray(a).reshape(-1, P).T
    rep = lambda a: np.broadcast_to(a, (P, a.size))
    b = i["b_in_2"][0]
    bt = []
    for h in range(4):
        bt += [b[h * P:h * P + P], b[512 + h * P:512 + h * P + P], b[2048 + 256 * h:2304 + 256 * h]]
    bt += [b[4352:5376], b[4096:4160], b[4096:4160], b[4160:4224], b[4160:4224], b[3072:4096], b[5376:6400]]
    eight = lambda a: np.pad(a.reshape(-1, 1), ((0, P - GH), (0, 0)))
    j = np.arange(P)
    lg = np.log1p(-np.exp2(-5.0 - np.arange(4)))
    inv64 = 10000.0 ** (-np.arange(0, 64, 2, dtype=np.float32) / np.float32(64))
    parts = {
        "c": col(i["c"]), "ada_b": col(i["ada_b"]), "mix_g": col(i["norm_mix_g"]), "ffn_g": col(i["norm_ffn_g"]),
        "conv": i["gdn_conv_w"][0].reshape(24, P, 4).transpose(1, 0, 2).reshape(P, 96), "gdn_g": col(i["gdn_norm_g"]),
        "a_log": eight(i["gdn_a_log"][0]), "dt_b": eight(i["gdn_dt_bias"][0]), "q_g": col(i["mla_q_norm_g"]),
        "kv_g": col(i["mla_kv_norm_g"]), "fin_g": col(i["final_norm_g"]), "ln1": col(i["ln1_g_2"]),
        "b_in": col(np.concatenate(bt)), "ret_g": col(i["ret_norm_g_2"]), "ln2": col(i["ln2_g_2"]),
        "lnf": col(i["lnf_g_2"]), "sink": rep(i["attn_sinks_2"][0]), "zero": np.zeros((P, 1)),
        "kdec": np.exp(lg[None] * (P - 1.0 - j)[:, None]),
        "freq": np.stack([inv64[j % 32], np.where(j % 64 < 32, -1.0, 1.0)], 1), "eps": np.full((P, 1), EPS),
        "cdec": rep(np.exp(lg * P)),
    }
    out = []
    for n, c in V.items():
        a = parts[n]
        assert c == sum(o.shape[1] for o in out), n
        out.append(np.asarray(a, np.float32))
    return np.ascontiguousarray(np.concatenate(out, 1))


def _constants():
    j, i = np.arange(P)[:, None], np.arange(P)[None]
    return np.concatenate([np.eye(P), np.ones((P, P)), np.where(j <= i, 0, -1e30), np.where(i <= j, 0, -1e30)],
                          1).astype(np.float32)


def _levels():
    i, j = np.arange(P)[:, None], np.arange(P)[None]
    m = [(i // (2 * b) == j // (2 * b)) & (i % (2 * b) >= b) & (j % (2 * b) < b) for b in (1, 2, 4, 8, 16, 32, 64)]
    m[0] = m[0].T
    return np.concatenate(m, 1).astype(np.int32)


def _rope_tables():
    j = np.arange(P)
    perm = [np.eye(P)[(j // 64) * 64 + (j + 32) % 64], np.eye(P)[(j + 64) % P]]
    t = np.arange(T, dtype=np.float32)
    tabs = []
    for half in (64, 32):
        inv = (np.float32(10000.0) ** (-np.arange(half, dtype=np.float32) / np.float32(half))).astype(np.float32)
        ang = (t[None] * inv[j % half][:, None]).astype(np.float64)
        tabs += [np.cos(ang), np.sin(ang) * np.where(j % (2 * half) < half, -1.0, 1.0)[:, None]]
    lg = np.log1p(-np.exp2(-5.0 - np.arange(4)))
    rel = j[None] - j[:, None]
    intra = [np.where(rel >= 0, np.exp(g * np.maximum(rel, 0)), 0) * P ** -0.5 for g in lg]
    qdec = [np.broadcast_to(np.exp(g * (j + 1.0)) * P ** -0.5, (P, P)) for g in lg]
    cur = np.where(j[None] <= j[:, None], 0, -1e30)
    prev = np.where(j[None] > j[:, None], 0, -1e30)
    none = np.full((P, P), -1e30)
    win = [cur, none, prev, cur]
    return np.concatenate(perm + tabs + intra + qdec + win, 1).astype(np.float32)


def kernel(**inputs):
    import concourse.bacc as bacc
    from concourse.bass_utils import run_bass_kernel_spmd

    i = {k: np.asarray(v) for k, v in inputs.items()}
    b = i["b_in_2"][0]
    arrays = {
        "slabs": _slabs(i),
        "ada": np.stack([s for layer in range(2) for s in _cols(i["ada_w"][layer])]),
        "vecs": _vectors(i),
        "consts": _constants(),
        "masks": _levels(),
        "rope": _rope_tables(),
        "vbias": np.concatenate([b[1024:2048], b[4224:4352]]).reshape(1, -1),
        "pos": i["positions"].astype(np.int32).reshape(1, T),
        "xin": np.ascontiguousarray(i["x"][0].T.reshape(KC, P, T).transpose(1, 0, 2)),
    }
    nc = bacc.Bacc("TRN2", target_bir_lowering=False, num_devices=1)
    args = [nc.dram_tensor(f"in_{n}", a.shape, mybir.dt.from_np(a.dtype), kind="ExternalInput").ap()
            for n, a in arrays.items()]
    out = nc.dram_tensor("out", (P, KC, T), mybir.dt.float32, kind="ExternalOutput").ap()
    build(nc, *args, out)
    r = run_bass_kernel_spmd(nc, [{f"in_{n}": a for n, a in arrays.items()}], core_ids=[0])
    return r.results[0]["out"].transpose(1, 0, 2).reshape(DM, T).T.reshape(1, T, DM)
```
